# Optimizing a Trainium2 kernel written in Bass

```python
import math
import jax, jax.numpy as jnp
from jax import lax
import numpy as np

D_MODEL = 2048
BATCH = 1
SEQ = 256
DEPTH = 1

CHUNK = 64
N_META = 16
SSD_D_INNER = 2048
SSD_HEADDIM = 64
SSD_HEADS = SSD_D_INNER // SSD_HEADDIM
SSD_GROUPS = 8
SSD_STATE = 128
SSD_CONV = 4
SSD_XBC = SSD_D_INNER + 2 * SSD_GROUPS * SSD_STATE
CF_WIDTH = 2048
CF_CONV = 31
PEER_HEADS = 8
PEER_NKEYS = 128
PEER_EXPERTS = PEER_NKEYS * PEER_NKEYS
PEER_DKEY = 256
PEER_TOPK = 16
PEER_BLOCK = 128
OFF_Z = SSD_D_INNER
OFF_XBC = OFF_Z + SSD_XBC
OFF_DT = OFF_XBC + SSD_HEADS
OFF_CF = OFF_DT + 2 * CF_WIDTH
IN_COLS = OFF_CF + 2 * D_MODEL
LN_EPS = 1e-5
DN_ALPHA = (2.0 * DEPTH) ** 0.25
DN_BETA = (8.0 * DEPTH) ** -0.25

kernel_name = "hybrid_ssd_conformer_peer_block"

def layer_norm(x, g, b):
    xf = x.astype(jnp.float32)
    mu = jnp.mean(xf, -1, keepdims=True)
    var = jnp.mean(jnp.square(xf - mu), -1, keepdims=True)
    return ((xf - mu) * lax.rsqrt(var + LN_EPS) * g.astype(jnp.float32) + b.astype(jnp.float32)).astype(x.dtype)

def causal_dwconv(x, w, b):
    k = w.shape[0]
    xp = jnp.pad(x, ((0, 0), (k - 1, 0), (0, 0)))
    y = lax.conv_general_dilated(xp, w.astype(x.dtype)[:, None, :], window_strides=(1,), padding='VALID',
                                 dimension_numbers=('NWC', 'WIO', 'NWC'), feature_group_count=x.shape[-1])
    return y + b.astype(x.dtype)

def gated_rmsnorm(y, z, w):
    yf = (y.astype(jnp.float32) * jax.nn.silu(z.astype(jnp.float32)))
    shp = yf.shape
    yg = yf.reshape(shp[:-1] + (SSD_GROUPS, shp[-1] // SSD_GROUPS))
    yg = yg * lax.rsqrt(jnp.mean(yg * yg, -1, keepdims=True) + LN_EPS)
    return (yg.reshape(shp) * w.astype(jnp.float32)).astype(z.dtype)

def ssd_chunked(xh, dt, a, bm, cm):
    bsz, L, H, P = xh.shape
    G, N = bm.shape[-2], bm.shape[-1]
    R = H // G
    nc = L // CHUNK
    x = (xh * dt[..., None]).reshape(bsz, nc, CHUNK, G, R, P)
    da = (dt * a).reshape(bsz, nc, CHUNK, G, R)
    bm = bm.reshape(bsz, nc, CHUNK, G, N)
    cm = cm.reshape(bsz, nc, CHUNK, G, N)
    cs = jnp.cumsum(da, axis=2)
    mask = jnp.tril(jnp.ones((CHUNK, CHUNK), dtype=bool))[:, :, None, None]
    seg = cs[:, :, :, None] - cs[:, :, None, :]
    decay = jnp.exp(jnp.where(mask, seg, -jnp.inf))
    scores = jnp.einsum('bcign,bcjgn->bcijg', cm, bm)
    y_diag = jnp.einsum('bcijgr,bcjgrp->bcigrp', scores[..., None] * decay, x)
    xd = x * jnp.exp(cs[:, :, -1:] - cs)[..., None]
    states = jnp.einsum('bcjgn,bcjgrp->bcgrpn', bm, xd)
    chunk_decay = jnp.exp(cs[:, :, -1])

    def step(h, inp):
        s, d = inp
        return h * d[..., None, None] + s, h

    h0 = jnp.zeros((bsz, G, R, P, N), dtype=states.dtype)
    _, prev = lax.scan(step, h0, (jnp.swapaxes(states, 0, 1), jnp.swapaxes(chunk_decay, 0, 1)))
    prev = jnp.swapaxes(prev, 0, 1)
    y_off = jnp.einsum('bcign,bcgrpn->bcigrp', cm, prev) * jnp.exp(cs)[..., None]
    return (y_diag + y_off).reshape(bsz, L, H, P)

def mixer(u, w_in, ssd_conv_w, ssd_conv_b, ssd_dt_bias, ssd_a_log, ssd_d, ssd_norm_w, ssd_out,
          cf_dw_w, cf_dw_b, cf_ln_g, cf_ln_b, cf_out, w_o):
    bsz, L, _ = u.shape
    proj = u @ w_in
    z, xbc, dt_raw, cf_in, gate_raw = jnp.split(proj, [OFF_Z, OFF_XBC, OFF_DT, OFF_CF], axis=-1)
    xbc = jax.nn.silu(causal_dwconv(xbc, ssd_conv_w, ssd_conv_b)).astype(jnp.float32)
    xs, bm, cm = jnp.split(xbc, [SSD_D_INNER, SSD_D_INNER + SSD_GROUPS * SSD_STATE], axis=-1)
    xs = xs.reshape(bsz, L, SSD_HEADS, SSD_HEADDIM)
    bm = bm.reshape(bsz, L, SSD_GROUPS, SSD_STATE)
    cm = cm.reshape(bsz, L, SSD_GROUPS, SSD_STATE)
    dt = jax.nn.softplus(dt_raw.astype(jnp.float32) + ssd_dt_bias.astype(jnp.float32))
    a = -jnp.exp(ssd_a_log.astype(jnp.float32))
    pad = (-L) % CHUNK
    padl = lambda t: jnp.pad(t, ((0, 0), (pad, 0)) + ((0, 0),) * (t.ndim - 2))
    y = ssd_chunked(padl(xs), padl(dt), a, padl(bm), padl(cm))[:, pad:]
    y = y + ssd_d.astype(jnp.float32)[:, None] * xs
    y = gated_rmsnorm(y.reshape(bsz, L, SSD_D_INNER), z, ssd_norm_w)
    y_ssd = y @ ssd_out
    c_val, c_gate = jnp.split(cf_in, 2, axis=-1)
    c = c_val * jax.nn.sigmoid(c_gate)
    c = causal_dwconv(c, cf_dw_w, cf_dw_b)
    c = jax.nn.silu(layer_norm(c, cf_ln_g, cf_ln_b))
    y_cf = c @ cf_out
    g_ssd, g_cf = jnp.split(jax.nn.sigmoid(gate_raw), 2, axis=-1)
    return (g_ssd * y_ssd + g_cf * y_cf) @ w_o

def peer(xf, peer_wq, peer_keys, peer_u, peer_v):
    T = xf.shape[0]
    q = (xf @ peer_wq).reshape(T, PEER_HEADS, 2, PEER_DKEY // 2)
    s = jnp.einsum('thsk,shnk->thsn', q, peer_keys).astype(jnp.float32)
    top_s, top_i = lax.top_k(s, PEER_TOPK)
    cand_s = top_s[:, :, 0, :, None] + top_s[:, :, 1, None, :]
    cand_i = top_i[:, :, 0, :, None] * PEER_NKEYS + top_i[:, :, 1, None, :]
    best_s, best_j = lax.top_k(cand_s.reshape(T, PEER_HEADS, PEER_TOPK * PEER_TOPK), PEER_TOPK)
    idx = jnp.take_along_axis(cand_i.reshape(T, PEER_HEADS, PEER_TOPK * PEER_TOPK), best_j, axis=-1)
    gate = jax.nn.softmax(best_s, axis=-1)
    tp = (-T) % PEER_BLOCK
    nb = (T + tp) // PEER_BLOCK
    xb = jnp.pad(xf, ((0, tp), (0, 0))).reshape(nb, PEER_BLOCK, D_MODEL)
    ib = jnp.pad(idx, ((0, tp), (0, 0), (0, 0))).reshape(nb, PEER_BLOCK, PEER_HEADS, PEER_TOPK)
    gb = jnp.pad(gate, ((0, tp), (0, 0), (0, 0))).reshape(nb, PEER_BLOCK, PEER_HEADS, PEER_TOPK)

    def block(args):
        xt, it, gt = args
        ue = peer_u[it]
        act = jax.nn.gelu(jnp.einsum('td,thkd->thk', xt, ue).astype(jnp.float32), approximate=False) * gt
        ve = peer_v[it]
        return jnp.einsum('thk,thkd->td', act.astype(ve.dtype), ve)

    out = lax.map(block, (xb, ib, gb)).reshape(nb * PEER_BLOCK, D_MODEL)
    return out[:T].astype(xf.dtype)

def setup_inputs(seed: int = 0) -> dict:
    key = jax.random.key(seed)
    ks = jax.random.split(key, 26)
    f32 = jnp.float32
    nrm = lambda k, shp, sc: jax.random.normal(k, shp, f32) * sc
    dt0 = jnp.exp(jax.random.uniform(ks[6], (DEPTH, SSD_HEADS), f32) * (math.log(0.1) - math.log(0.001)) + math.log(0.001))
    return {
        "x": nrm(ks[0], (BATCH, SEQ, D_MODEL), 1.0),
        "meta": nrm(ks[1], (N_META, D_MODEL), 1.0),
        "ln0_g": 1.0 + nrm(ks[2], (D_MODEL,), 0.02),
        "ln0_b": nrm(ks[3], (D_MODEL,), 0.02),
        "w_in": nrm(ks[4], (DEPTH, D_MODEL, IN_COLS), D_MODEL ** -0.5),
        "ssd_conv_w": nrm(ks[5], (DEPTH, SSD_CONV, SSD_XBC), SSD_CONV ** -0.5),
        "ssd_conv_b": nrm(ks[7], (DEPTH, SSD_XBC), 0.01),
        "ssd_dt_bias": dt0 + jnp.log(-jnp.expm1(-dt0)),
        "ssd_a_log": jnp.log(jax.random.uniform(ks[8], (DEPTH, SSD_HEADS), f32, 1.0, 16.0)),
        "ssd_d": 1.0 + nrm(ks[9], (DEPTH, SSD_HEADS), 0.1),
        "ssd_norm_w": 1.0 + nrm(ks[10], (DEPTH, SSD_D_INNER), 0.02),
        "ssd_out": nrm(ks[11], (DEPTH, SSD_D_INNER, D_MODEL), SSD_D_INNER ** -0.5),
        "cf_dw_w": nrm(ks[12], (DEPTH, CF_CONV, CF_WIDTH), CF_CONV ** -0.5),
        "cf_dw_b": nrm(ks[13], (DEPTH, CF_WIDTH), 0.01),
        "cf_ln_g": 1.0 + nrm(ks[14], (DEPTH, CF_WIDTH), 0.02),
        "cf_ln_b": nrm(ks[15], (DEPTH, CF_WIDTH), 0.02),
        "cf_out": nrm(ks[16], (DEPTH, CF_WIDTH, D_MODEL), CF_WIDTH ** -0.5),
        "w_o": nrm(ks[17], (DEPTH, D_MODEL, D_MODEL), DN_BETA * D_MODEL ** -0.5),
        "ln1_g": 1.0 + nrm(ks[18], (DEPTH, D_MODEL), 0.02),
        "ln1_b": nrm(ks[19], (DEPTH, D_MODEL), 0.02),
        "peer_wq": nrm(ks[20], (DEPTH, D_MODEL, PEER_HEADS * PEER_DKEY), D_MODEL ** -0.5),
        "peer_keys": nrm(ks[21], (DEPTH, 2, PEER_HEADS, PEER_NKEYS, PEER_DKEY // 2), (PEER_DKEY // 2) ** -0.5),
        "peer_u": nrm(ks[22], (DEPTH, PEER_EXPERTS, D_MODEL), D_MODEL ** -0.5),
        "peer_v": nrm(ks[23], (DEPTH, PEER_EXPERTS, D_MODEL), DN_BETA),
        "ln2_g": 1.0 + nrm(ks[24], (DEPTH, D_MODEL), 0.02),
        "ln2_b": nrm(ks[25], (DEPTH, D_MODEL), 0.02),
    }

def reference(x, meta, ln0_g, ln0_b, w_in, ssd_conv_w, ssd_conv_b, ssd_dt_bias, ssd_a_log, ssd_d,
              ssd_norm_w, ssd_out, cf_dw_w, cf_dw_b, cf_ln_g, cf_ln_b, cf_out, w_o, ln1_g, ln1_b,
              peer_wq, peer_keys, peer_u, peer_v, ln2_g, ln2_b):
    bsz = x.shape[0]
    h = jnp.concatenate([jnp.broadcast_to(meta[None].astype(x.dtype), (bsz, N_META, D_MODEL)), x], axis=1)
    h = layer_norm(h, ln0_g, ln0_b)
    for l in range(DEPTH):
        m = mixer(h, w_in[l], ssd_conv_w[l], ssd_conv_b[l], ssd_dt_bias[l], ssd_a_log[l], ssd_d[l],
                  ssd_norm_w[l], ssd_out[l], cf_dw_w[l], cf_dw_b[l], cf_ln_g[l], cf_ln_b[l], cf_out[l], w_o[l])
        h = layer_norm(DN_ALPHA * h + m, ln1_g[l], ln1_b[l])
        f = peer(h.reshape(-1, D_MODEL), peer_wq[l], peer_keys[l], peer_u[l], peer_v[l]).reshape(h.shape)
        h = layer_norm(DN_ALPHA * h + f, ln2_g[l], ln2_b[l])
    return h[:, N_META:]


_drawn_inputs = setup_inputs


def setup_inputs(seed=0):
    import zlib

    import numpy as np

    out = dict(_drawn_inputs(seed))
    spreads = {}
    factors = {'ssd_conv_b': 3.233,
     'ssd_norm_w': 2.884,
     'cf_dw_b': 3.59,
     'cf_ln_g': 3.374,
     'cf_ln_b': 3.373,
     'ln2_g': 2.84,
     'ln2_b': 2.73}
    for name, (base, spread) in spreads.items():
        noise = np.random.default_rng([zlib.crc32(name.encode()), seed]).standard_normal(out[name].shape)
        drawn = base * np.exp(spread * noise) if base else spread * noise
        out[name] = __import__('jax').numpy.asarray(drawn.astype(out[name].dtype))
    for name, factor in factors.items():
        out[name] = (out[name] * factor).astype(out[name].dtype)
    return out
```

```python
from contextlib import ExitStack

import concourse.bass as bass
from concourse import mybir
from concourse.alu_op_type import AluOpType as ALU

ACT = mybir.ActivationFunctionType
AX = mybir.AxisListType
F32 = mybir.dt.float32
U32 = mybir.dt.uint32

P = 128
D = 2048
SEQ, META = 256, 16
L = META + SEQ
KT = D // P
SW = 256
NS = D // SW
GROUPS, HEADS, HPG, HD = 8, 32, 4, 64
KC, KF = 4, 31
XBC = D + 2 * GROUPS * P
OFF_XBC = D
OFF_DT = OFF_XBC + XBC
OFF_VAL = OFF_DT + HEADS
OFF_CGATE = OFF_VAL + D
OFF_GSSD = OFF_CGATE + D
OFF_GCF = OFF_GSSD + D
CHUNKS = [(0, META), (META, META + P), (META + P, L)]
PH, NK, TOPK = 8, 128, 16
NT = SEQ // P
EPS = 1e-5
ALPHA = 2.0 ** 0.25
LOW = -3.0e38
SLOTS = 5
UB = 4
LN_X, LN_META, LN_H1, LN_OUT = 0, 2, 3, 5


def build(nc, A, out):
    ds = bass.ds
    x, meta = A["x"][0], A["meta"]
    w_in, ssd_out, cf_out, w_o, wq = (A[n][0] for n in ("w_in", "ssd_out", "cf_out", "w_o", "peer_wq"))
    peer_u, peer_v = A["peer_u"][0], A["peer_v"][0]

    with ExitStack() as ctx:
        def sb(name, shape, dt=F32):
            return ctx.enter_context(nc.sbuf_tensor(name, shape, dt))

        def sem(name):
            return ctx.enter_context(nc.semaphore(name))

        slab = [sb(f"slab{i}", [P, KT, SW]) for i in range(SLOTS)]
        hT = sb("hT", [P, KT, L])
        rows = sb("rows", [P, NT, D])
        gain = sb("gain", [P, 2, D])
        yT = sb("yT", [P, KT, SEQ])
        cT = sb("cT", [P, KT, SEQ])
        mT = slab[4]
        scr = sb("scr", [P, 12, L])
        xin, acc, xg = scr[:, 0:4, :], scr[:, 4:8, :], scr[:, 8:12, :]
        vraw = sb("vraw", [P, 2, L])
        gsig = sb("gsig", [P, 2, L])
        zs = sb("zs", [P, 2, SEQ])
        v = sb("v", [P, 2, SEQ])
        v2 = sb("v2", [P, 2, SEQ])
        rinv = sb("rinv", [P, 2, SEQ])
        gflat = gain[:, :, :].rearrange("p a b -> p (a b)")
        seg = gflat[:, 0:1024].rearrange("p (c h i) -> p c h i", c=2, h=HPG)
        ecs = gflat[:, 1024:2048].rearrange("p (c h i) -> p c h i", c=2, h=HPG)
        rmask = gflat[0:HEADS, 2048:3072].rearrange("p (c h i) -> p c h i", c=2, h=HPG)
        xdt = gflat[:, 3072:3584].rearrange("p (c n) -> p c n", c=2)
        xw = gflat[:, 3584:4096].rearrange("p (c n) -> p c n", c=2)
        btm = sb("btm", [P, 2, P])
        scm = sb("scm", [P, 2, P])
        state = sb("state", [P, 2, HPG * HD])
        keysT = sb("keysT", [P, 2 * PH, NK])
        ident = sb("ident", [P, P])
        ones = sb("ones", [P, P])
        avg = sb("avg", [P, P])
        zero = sb("zero", [P, P])
        causal = sb("causal", [P, P])
        iota16 = sb("iota16", [P, TOPK])
        eps = sb("eps", [P, 1])
        pcol = sb("pcol", [P, 96])
        convw = sb("convw", [P, KC, 32])
        cfw = sb("cfw", [P, 4 * 124])
        dcol = sb("dcol", [P, KT])
        head = sb("head", [HEADS, 4])
        wdt = sb("wdt", [P, KT, HEADS])
        cs = sb("cs", [HEADS, L])
        tm = sb("tm", [P, 6, HEADS])
        edec = sb("edec", [P, HEADS])
        stats = sb("stats", [P, 4, 6])
        mv = sb("mv", [P, 2])
        sd = sb("sd", [P, 2])
        gsum = sb("gsum", [P, NT * PH, 1])

        yflat = yT[:, :, :].rearrange("p a b -> p (a b)")
        prow = yflat[0:96, 0:128]
        convrow = yflat[:, 128:256]
        cfrow = yflat[0:124, 256:768].rearrange("p (a b) -> p a b", a=4)
        keyrow = yflat[:, 1024:3072].rearrange("p (a b) -> p a b", a=2 * PH)
        meta_t = cT[:, :, :].rearrange("p a b -> p (a b)")[0:META, 0:D]
        csq = gflat.rearrange("p (a b) -> p a b", a=KT)
        hsm = [scr[0:HEADS, i, :] for i in range(12)]
        qts = [yflat[:, 512 + 512 * i:1024 + 512 * i].rearrange("p (s t) -> p s t", s=2) for i in range(2)]
        scs = [yflat[:, 1536 + 512 * i:2048 + 512 * i].rearrange("p (a b) -> p a b", a=4) for i in range(2)]
        cflat = cT[:, :, :].rearrange("p a b -> p (a b)")
        left = cflat[:, 0:512].rearrange("p (a b) -> p a b", a=4)
        cand = cflat[:, 512:1024].rearrange("p (t a) -> p t a", t=2)
        cand2 = cflat[:, 1024:1536].rearrange("p (t a) -> p t a", t=2)
        hot = cflat[:, 1536:2048].rearrange("p (t k i) -> p t k i", t=2, k=TOPK)
        topv = cflat[:, 2048:2112].rearrange("p (a b) -> p a b", a=4)
        topif = cflat[:, 2112:2176].rearrange("p (a b) -> p a b", a=4)
        topi = cflat[:, 2176:2240].rearrange("p (a b) -> p a b", a=4).bitcast(U32)
        bestv = cflat[:, 2240:2272].rearrange("p (a b) -> p a b", a=2)
        bestj = cflat[:, 2272:2304].rearrange("p (a b) -> p a b", a=2).bitcast(U32)
        part = cflat[:, 2304:2368].rearrange("p (s a b) -> p s a b", s=2, a=2).bitcast(U32)
        partf = cflat[:, 2368:2432].rearrange("p (s a b) -> p s a b", s=2, a=2)
        pick = cflat[:, 2432:2496].rearrange("p (s a b) -> p s a b", s=2, a=2)
        gates = cflat[:, 2560:2816].rearrange("p (a b) -> p a b", b=TOPK)
        best = cflat[:, 2816:3072].rearrange("p (a b) -> p a b", b=TOPK)
        idx = cflat[:, 3072:3360].rearrange("p (a b) -> p a b", b=TOPK).bitcast(U32)
        ubuf = [slab[i][:, 0:KT // 2, :].rearrange("p a b -> p (a b)") for i in range(UB)]
        vbuf = [slab[i][:, KT // 2:KT, :].rearrange("p a b -> p (a b)") for i in range(UB)]
        dots, gel, wgt, ixu, ixv = (cflat[:, 3360 + 32 * i:3392 + 32 * i].rearrange("p (a b) -> p a b", a=2)
                                    for i in range(5))
        ixu, ixv = ixu.bitcast(U32), ixv.bitcast(U32)
        diag = [yflat[:, i * P:(i + 1) * P] for i in range(4)]

        ps = ctx.enter_context(nc.psum_tensor("ps", [P, 8, 512], F32))
        T0, T1, T2, T3 = (ps[:, 4 + i, :] for i in range(4))

        x_loaded = [sem(f"x_loaded{i}") for i in range(NT)]
        meta_loaded, gain_loaded, param_loaded = sem("meta_loaded"), sem("gain_loaded"), sem("param_loaded")
        wdt_loaded = sem("wdt_loaded")
        slab_loaded = [sem(f"slab_loaded{i}") for i in range(SLOTS)]
        u_loaded = [sem(f"u_loaded{i}") for i in range(UB)]
        v_loaded = [sem(f"v_loaded{i}") for i in range(UB)]
        const_step, const_ready = sem("const_step"), sem("const_ready")
        vec_step, gated = sem("vec_step"), sem("gated")
        var_ready, sd_done, ln_done = sem("var_ready"), sem("sd_done"), sem("ln_done")
        turned, turned_copied = sem("turned"), sem("turned_copied")
        dt_done, u_ready, rel_ready, w_ready, tabs_ready = (sem(n) for n in (
            "dt_done", "u_ready", "rel_ready", "w_ready", "tabs_ready"))
        x1_ready, ex_ready, alog_ready, ecl_ready = (sem(n) for n in ("x1_ready", "ex_ready", "alog_ready", "ecl_ready"))
        tabs_done, tabs_copied = sem("tabs_done"), sem("tabs_copied")
        proj_done, proj_copied = sem("proj_done"), sem("proj_copied")
        r_ready, csb_done, seg_ready, ecs_ready, exp_ready = (sem(n) for n in (
            "r_ready", "csb_done", "seg_ready", "ecs_ready", "exp_ready"))
        conv_ready, xg_ready, xpose_done, score_done = (sem(n) for n in (
            "conv_ready", "xg_ready", "xpose_done", "score_done"))
        xtm_ready, btm_ready, mt_ready, state_done, s_ready = (sem(n) for n in (
            "xtm_ready", "btm_ready", "mt_ready", "state_done", "s_ready"))
        y_done, v_ready, sq_ready, nsum_done, nsd_ready, ynorm_ready = (sem(n) for n in (
            "y_done", "v_ready", "sq_ready", "nsum_done", "nsd_ready", "ynorm_ready"))
        mm2_done, sg_ready, mix_ready = sem("mm2_done"), sem("sg_ready"), sem("mix_ready")
        cf_ready, mean_done, cen_ready, csq_ready, cvar_done, csd_ready, cn_ready, c_ready = (sem(n) for n in (
            "cf_ready", "mean_done", "cen_ready", "csq_ready", "cvar_done", "csd_ready", "cn_ready", "c_ready"))
        wo_done, res_ready = sem("wo_done"), sem("res_ready")
        q_done, q_copied, sc_done, sc_copied, topk_done = (sem(n) for n in (
            "q_done", "q_copied", "sc_done", "sc_copied", "topk_done"))
        gexp_in, gexp_done = sem("gexp_in"), sem("gexp_done")
        ix_staged, u_used, v_used, gelu_ready, wgt_ready, diag_ready = (sem(n) for n in (
            "ix_staged", "u_used", "v_used", "gelu_ready", "wgt_ready", "diag_ready"))
        stored, waited = sem("stored"), sem("waited")

        block = ctx.enter_context(nc.Block())

        N_PARAM, N_X, N_KEY = 3, 4 * NT + 1, 4
        TURN_X = N_PARAM
        TURN_META = TURN_X + 4 * NT
        TURN_KEYS = TURN_META + 1
        TURN_H1 = TURN_KEYS + N_KEY

        def run_steps(eng, step, middle=lambda: None):
            step(0, 0, True, False)
            step(1, 1, True, True)
            with eng.Fori(2, PH, 2) as s:
                step(s, 0, True, True)
                step(s + 1, 1, True, True)
            step(PH, 0, True, True)
            middle()
            step(PH + 1, 1, True, True)
            with eng.Fori(PH + 2, 2 * PH, 2) as s:
                step(s, 0, True, True)
                step(s + 1, 1, True, True)
            step(2 * PH, 0, False, True)

        def settle(eng):
            eng.sem_inc(waited, 1)

        @block.sync
        def _(sp):
            for t in range(NT):
                sp.dma_start(rows[:, t, :], x[t * P:(t + 1) * P, :]).then_inc(x_loaded[t], 16)
            sp.dma_start(meta_t, meta).then_inc(meta_loaded, 16)

            def load_gain(g, b):
                for i, r in enumerate((g, b)):
                    sp.dma_start(gain[:, i, :], r.partition_broadcast(P)).then_inc(gain_loaded, 16)

            load_gain(A["ln0_g"], A["ln0_b"])
            at = 0
            for r, n in (("ssd_conv_b", 32), ("ssd_norm_w", 16), ("cf_dw_b", 16), ("cf_ln_g", 16), ("cf_ln_b", 16)):
                sp.dma_start(prow[at:at + n, :], A[r][0].rearrange("(t p) -> t p", p=P)).then_inc(param_loaded, 16)
                at += n
            for k in range(KC):
                sp.dma_start(convrow[32 * k:32 * k + 32, :],
                             A["ssd_conv_w"][0, k].rearrange("(t p) -> t p", p=P)).then_inc(param_loaded, 16)
            sp.dma_start(cfrow, A["cf_dw_w"][0].rearrange("k (t p) -> (k t) p", p=P).rearrange(
                "(a r) p -> r a p", r=124)).then_inc(param_loaded, 16)
            sp.dma_start(keyrow, A["peer_keys"][0].rearrange("s h n k -> n (s h) k")).then_inc(param_loaded, 16)
            sp.dma_start(head[:, 0:1], A["ssd_dt_bias"][0].rearrange("(h o) -> h o", o=1)).then_inc(param_loaded, 16)
            sp.dma_start(head[:, 1:2], A["ssd_a_log"][0].rearrange("(h o) -> h o", o=1)).then_inc(param_loaded, 16)
            d2 = A["ssd_d"][0].rearrange("(t u) -> u t", u=2)
            with nc.allow_non_contiguous_dma(reason="32 values"):
                for u in range(2):
                    sp.dma_start(dcol[HD * u:HD * u + HD, :],
                                 d2[u:u + 1, :].to_broadcast([HD, KT])).then_inc(param_loaded, 16)
            sp.dma_start(wdt[:, :, :], w_in[:, OFF_DT:OFF_DT + HEADS].rearrange(
                "(k p) n -> p k n", p=P)).then_inc(wdt_loaded, 16)

            def cols(w, at, n=SW):
                return w[:, ds(at, n)].rearrange("(k p) n -> p k n", p=P)

            def load(slot, w, at):
                sp.dma_start(slab[slot][:, :, :], cols(w, at)).then_inc(slab_loaded[slot], 16)

            def group_slabs(g, free):
                free(0)
                load(0, w_in, g * SW + OFF_XBC)
                free(1)
                sp.dma_start(slab[1][:, :, 0:P], cols(w_in, g * P + OFF_XBC + D, P)).then_inc(slab_loaded[1], 16)
                sp.dma_start(slab[1][:, :, P:SW], cols(w_in, g * P + OFF_XBC + D + GROUPS * P, P)).then_inc(
                    slab_loaded[1], 16)
                for slot, off in ((2, OFF_VAL), (3, 0), (4, OFF_CGATE)):
                    free(slot)
                    load(slot, w_in, g * SW + off)

            group_slabs(0, lambda slot: None)
            with sp.Fori(1, GROUPS) as g:
                group_slabs(g, lambda slot: (sp.wait_ge(proj_done, g * 5 + (slot - 4)), settle(sp)))

            def mix_slabs(i, gate_off, w, free):
                for j in range(2):
                    free(2 * j)
                    load(2 * j, w_in, i * (2 * SW) + (gate_off + j * SW))
                    free(2 * j + 1)
                    load(2 * j + 1, w, i * (2 * SW) + j * SW)

            mix_slabs(0, OFF_GSSD, ssd_out, lambda slot: sp.wait_ge(proj_done, 5 * (GROUPS - 1) + slot + 1))
            with sp.Fori(1, 4) as i:
                mix_slabs(i, OFF_GSSD, ssd_out, lambda slot: (sp.wait_ge(mm2_done, i * 4 + (slot - 3)), settle(sp)))
            with sp.Fori(0, 4) as i:
                mix_slabs(i, OFF_GCF, cf_out, lambda slot: (sp.wait_ge(mm2_done, i * 4 + (slot + 13)), settle(sp)))
            for j in range(4):
                sp.wait_ge(mm2_done, 28 + j + 1)
                load(j, w_o, j * SW)
            for j in range(4):
                if j == 0:
                    sp.wait_ge(csq_ready, 1)
                    sp.wait_ge(cvar_done, 1)
                    load_gain(A["ln1_g"][0], A["ln1_b"][0])
                sp.wait_ge(wo_done, j + 1)
                load(j, w_o, (4 + j) * SW)
            for j in range(4):
                sp.wait_ge(wo_done, 4 + j + 1)
                load(j, wq, j * SW)
            for j in range(4):
                sp.wait_ge(q_done, j + 1)
                load(j, wq, (4 + j) * SW)
            sp.wait_ge(ln_done, LN_OUT)
            load_gain(A["ln2_g"][0], A["ln2_b"][0])
            for t in range(NT):
                sp.wait_ge(ln_done, LN_OUT + t + 1)
                sp.dma_start(out[0, t * P:(t + 1) * P, :], rows[:, t, :]).then_inc(stored, 16)
            sp.wait_ge(stored, 16 * NT)

        @block.gpsimd
        def _(pool):
            pool.memset(ident[:, :], 0.0).then_inc(const_step, 1)
            pool.memset(causal[:, :], 1.0).then_inc(const_step, 1)
            pool.memset(ones[:, :], 1.0).then_inc(const_ready, 1)
            pool.memset(avg[:, :], 1.0 / D).then_inc(const_ready, 1)
            pool.memset(zero[:, :], 0.0).then_inc(const_ready, 1)
            pool.memset(eps[:, :], EPS).then_inc(const_ready, 1)
            pool.iota(iota16[:, :], [[1, TOPK]], base=0, channel_multiplier=0,
                      allow_small_or_imprecise_dtypes=True).then_inc(const_ready, 1)
            pool.wait_ge(const_step, 2)
            pool.affine_select(out=ident[:, :], in_=ident[:, :], compare_op=ALU.not_equal, fill=1.0, base=0,
                               pattern=[[-1, P]], channel_multiplier=1).then_inc(const_ready, 1)
            pool.affine_select(out=causal[:, :], in_=causal[:, :], compare_op=ALU.is_ge, fill=0.0, base=0,
                               pattern=[[1, P]], channel_multiplier=-1).then_inc(const_ready, 1)

            def gather(dst, table, index, landed):
                pool.indirect_dma_start(dst, None, table, bass.IndirectOffsetOnAxis(ap=index, axis=0)).then_inc(landed, 16)

            def step(s, par, u, v_):
                pool.wait_ge(ix_staged, s + 1)
                for k in range(TOPK):
                    b = k % UB
                    if u:
                        if not (isinstance(s, int) and s * TOPK + k < UB):
                            pool.wait_ge(u_used, s * TOPK + (k - UB + 1))
                            settle(pool)
                        gather(ubuf[b], peer_u, ixu[:, par, k:k + 1], u_loaded[b])
                    if v_:
                        if not (isinstance(s, int) and (s - 1) * TOPK + k < UB):
                            pool.wait_ge(v_used, s * TOPK + (k - UB + 1 - TOPK))
                            settle(pool)
                        gather(vbuf[b], peer_v, ixv[:, 1 - par, k:k + 1], v_loaded[b])

            run_steps(pool, step)

        @block.tensor
        def _(pe):
            def turn(i, sources, waits=()):
                for s, n in waits:
                    pe.wait_ge(s, n)
                if i >= 4:
                    pe.wait_ge(turned_copied, i - 3)
                at = 0
                for src in sources:
                    n = src.shape[0]
                    last = pe.transpose(ps[0:src.shape[1], 4 + i % 4, at:at + n], src, ident[0:n, 0:n])
                    at += n
                last.then_inc(turned, 1)

            turn(0, [prow], [(const_ready, 7), (param_loaded, 16 * 15)])
            turn(1, [convrow])
            turn(2, [cfrow[:, a, :] for a in range(4)])
            for t in range(NT):
                for q in range(4):
                    turn(TURN_X + 4 * t + q, [rows[:, t, (4 * q + r) * P:(4 * q + r + 1) * P] for r in range(4)],
                         [(ln_done, LN_X + t + 1)])
            turn(TURN_META, [meta_t[:, k * P:(k + 1) * P] for k in range(KT)], [(ln_done, LN_META + 1)])
            for q in range(4):
                turn(TURN_KEYS + q, [keyrow[:, 4 * q + r, :] for r in range(4)])

            pe.wait_ge(turned_copied, TURN_H1)
            pe.wait_ge(wdt_loaded, 16)
            for k in range(KT):
                last = pe.matmul(T0[0:HEADS, 0:L], wdt[:, k, :], hT[:, k, :], start=(k == 0), stop=(k == KT - 1))
            last.then_inc(dt_done, 1)
            pe.wait_ge(tabs_ready, 1)
            dtv, ncs, wst = hsm[4], hsm[5], hsm[6]
            for n, (tab, c) in enumerate(((dtv, 1), (dtv, 2), (ncs, 1), (ncs, 2), (wst, 1), (wst, 0))):
                a, b = CHUNKS[c]
                pe.transpose(T1[0:b - a, n * HEADS:(n + 1) * HEADS], tab[:, a:b], ident[0:HEADS, 0:HEADS])
            pe.matmul(T1[:, 6 * HEADS:7 * HEADS], hsm[7][:, 0:P], ident[0:HEADS, 0:HEADS],
                      start=True, stop=True).then_inc(tabs_done, 1)
            pe.wait_ge(tabs_copied, 2)

            def project(slot, bank, a, b, width=1):
                for u in range(2):
                    o = ps[:, bank + u, 0:b - a] if width else ps[:, bank, u * (b - a):(u + 1) * (b - a)]
                    for k in range(KT):
                        last = pe.matmul(o, slab[slot][:, k, u * P:(u + 1) * P], hT[:, k, a:b],
                                         start=(k == 0), stop=(k == KT - 1))
                return last

            with pe.Fori(0, GROUPS) as g:
                pe.wait_ge(slab_loaded[0], g * 16 + 16)
                pe.wait_ge(proj_copied, g * 5 + 3)
                project(0, 0, 0, L).then_inc(proj_done, 1)
                pe.wait_ge(slab_loaded[1], g * 32 + 32)
                pe.wait_ge(proj_copied, g * 5 + 5)
                project(1, 2, 0, L).then_inc(proj_done, 1)
                pe.wait_ge(r_ready, g + 1)
                pe.matmul(T0, ones[0:HEADS, :], rmask[:, 0, :, :].rearrange("p a b -> p (a b)"),
                          start=True, stop=True)
                pe.matmul(T1, ones[0:HEADS, :], rmask[:, 1, :, :].rearrange("p a b -> p (a b)"),
                          start=True, stop=True).then_inc(csb_done, 1)
                pe.wait_ge(slab_loaded[2], g * 16 + 16)
                pe.wait_ge(proj_copied, g * 5 + 6)
                project(2, 0, 0, L).then_inc(proj_done, 1)
                pe.wait_ge(xg_ready, g * 4 + 4)
                for c in range(2):
                    for u in range(2):
                        a, b = CHUNKS[1 + c]
                        pe.transpose(T2[:, (2 * c + u) * P:(2 * c + u + 1) * P], xg[:, u, a:b], ident[:, :])
                pe.transpose(T3[:, 0:P], xg[:, 2, META:META + P], ident[:, :])
                pe.transpose(T3[0:META, P:2 * P], xg[:, 2, 0:META], ident[:, :])
                for u in range(2):
                    last = pe.transpose(T3[0:META, (2 + u) * P:(3 + u) * P], xg[:, u, 0:META], ident[:, :])
                last.then_inc(xpose_done, 1)
                pe.wait_ge(seg_ready, g + 1)
                pe.wait_ge(ecs_ready, g + 1)
                for c in range(2):
                    a, b = CHUNKS[1 + c]
                    last = pe.matmul(T0[:, c * P:(c + 1) * P], xg[:, 2, a:b], xg[:, 3, a:b], start=True, stop=True)
                last.then_inc(score_done, 1)
                pe.wait_ge(slab_loaded[3], g * 16 + 16)
                pe.wait_ge(proj_copied, g * 5 + 7)
                project(3, 2, META, L).then_inc(proj_done, 1)
                pe.wait_ge(xtm_ready, g + 1)
                pe.wait_ge(btm_ready, g * 2 + 2)
                pe.matmul(T3[:, 0:HPG * HD], btm[0:META, 1, :], xw[0:META, 1, :], start=True, stop=True)
                pe.matmul(T3[:, HPG * HD:2 * HPG * HD], btm[:, 0, :], xw[:, 0, :],
                          start=True, stop=True).then_inc(state_done, 1)
                pe.wait_ge(mt_ready, g + 1)
                pe.wait_ge(s_ready, g + 1)
                for u in range(2):
                    for c in range(2):
                        for r in range(2):
                            hh = 2 * u + r
                            o = ps[HD * r:HD * r + HD, 5, (2 * u + c) * P:(2 * u + c + 1) * P]
                            pe.matmul(o, xdt[:, c, hh * HD:(hh + 1) * HD], seg[:, c, hh, :], start=True, stop=False)
                            last = pe.matmul(o, state[:, c, hh * HD:(hh + 1) * HD], ecs[:, c, hh, :],
                                             start=False, stop=True)
                last.then_inc(y_done, 1)
                pe.wait_ge(slab_loaded[4], g * 16 + 16)
                pe.wait_ge(proj_copied, g * 5 + 9)
                project(4, 2, 0, L).then_inc(proj_done, 1)
                pe.wait_ge(sq_ready, g + 1)
                for u in range(2):
                    last = pe.matmul(T2[:, 0:SEQ], ones[:, :], v2[:, u, :], start=(u == 0), stop=(u == 1))
                last.then_inc(nsum_done, 1)

            def mix_body(i, base, src):
                for j in range(2):
                    pe.wait_ge(slab_loaded[2 * j], (i + (GROUPS + base + 1)) * 16)
                    pe.wait_ge(sg_ready, (i + base) * 2 + (j + 1))
                    project(2 * j, 2 * j, META, L, width=0).then_inc(mm2_done, 1)
                    pe.wait_ge(slab_loaded[2 * j + 1], (i + (GROUPS * (2 - j) + base + 1)) * 16)
                    pe.wait_ge(mix_ready, (i + base) * 2 + (j + 1))
                    for u in range(2):
                        for k in range(KT):
                            last = pe.matmul(ps[:, 2 * j + 1, u * SEQ:(u + 1) * SEQ],
                                             slab[2 * j + 1][:, k, u * P:(u + 1) * P], src[:, k, :],
                                             start=(k == 0), stop=(k == KT - 1))
                    last.then_inc(mm2_done, 1)

            pe.wait_ge(proj_copied, 5 * GROUPS + 5)
            pe.wait_ge(ynorm_ready, GROUPS)
            with pe.Fori(0, 2) as i:
                mix_body(i, 0, yT)
            pe.wait_ge(cf_ready, GROUPS + 1)
            for k in range(KT):
                last = pe.matmul(T0[:, 0:SEQ], avg[:, :], cT[:, k, :], start=(k == 0), stop=(k == KT - 1))
            last.then_inc(mean_done, 1)
            mix_body(2, 0, yT)
            pe.wait_ge(csq_ready, 1)
            for k in range(KT):
                last = pe.matmul(T1[:, 0:SEQ], avg[:, :], csq[:, k, :], start=(k == 0), stop=(k == KT - 1))
            last.then_inc(cvar_done, 1)
            mix_body(3, 0, yT)
            pe.wait_ge(c_ready, KT)
            with pe.Fori(0, 4) as i:
                mix_body(i, 4, cT)

            pe.wait_ge(mix_ready, 2 + 16)
            with pe.Fori(0, 2) as i:
                for j in range(4):
                    pe.wait_ge(slab_loaded[j], (i + (16 + 1 + (GROUPS if j == 1 else 0))) * 16)
                    pe.wait_ge(res_ready, i * 4 + (j + 1))
                    for t in range(NT):
                        for k in range(KT):
                            last = pe.matmul(ps[:, j, t * SW:(t + 1) * SW], mT[:, k, t * P:(t + 1) * P],
                                             slab[j][:, k, :], start=(k == 0), stop=(k == KT - 1))
                    last.then_inc(wo_done, 1)
            for t in range(NT):
                for q in range(4):
                    turn(TURN_H1 + 4 * t + q, [rows[:, t, (4 * q + r) * P:(4 * q + r + 1) * P] for r in range(4)],
                         [(ln_done, LN_H1 + t + 1)])
            pe.wait_ge(turned_copied, TURN_H1 + 4 * NT)

            def scores(i, j):
                pe.wait_ge(q_copied, i * 4 + (j + 3))
                pe.wait_ge(sc_copied, i * 4 + (j + 1))
                for t in range(NT):
                    for s in range(2):
                        last = pe.matmul(ps[:, 2 + j % 2, (2 * t + s) * NK:(2 * t + s + 1) * NK],
                                         qts[j % 2][:, s, t * P:(t + 1) * P],
                                         keysT[:, ds(i * 4 + (s * PH + j), 1), :].rearrange("p a b -> p (a b)"),
                                         start=True, stop=True)
                last.then_inc(sc_done, 1)

            pe.wait_ge(c_ready, KT)
            pe.nop().then_inc(sc_done, 2)
            with pe.Fori(0, 2) as i:
                for j in range(4):
                    pe.wait_ge(slab_loaded[j], (i + (18 + 1 + (GROUPS if j == 1 else 0))) * 16)
                    pe.wait_ge(q_copied, i * 4 + (j + 1))
                    for s in range(2):
                        for k in range(KT):
                            last = pe.matmul(ps[:, j % 2, s * SEQ:(s + 1) * SEQ], slab[j][:, k, s * P:(s + 1) * P],
                                             hT[:, k, 0:SEQ], start=(k == 0), stop=(k == KT - 1))
                    last.then_inc(q_done, 1)
                    if j:
                        scores(i, j - 1)
                scores(i, 3)

            def clear(t):
                for b in range(4):
                    pe.matmul(ps[:, 4 * t + b, :], zero[:, :], ones[:, 0:1].to_broadcast([P, 512]),
                              start=True, stop=False, skip_group_check=True)

            pe.wait_ge(sc_copied, 2 + PH)
            clear(0)
            clear(1)

            def step(s, par, u, v_):
                if not v_:
                    return
                t = tile_of_v[0]
                for k in range(TOPK):
                    b = k % UB
                    pe.wait_ge(v_loaded[b], (s - 1) * (TOPK // UB * 16) + (k // UB + 1) * 16)
                    pe.wait_ge(diag_ready, (s - 1) * TOPK + (k + 1))
                    for c in range(4):
                        last = pe.matmul(ps[:, 4 * t + c, :], diag[b], vbuf[b][:, c * 512:(c + 1) * 512],
                                         start=False, stop=False, skip_group_check=True)
                    last.then_inc(v_used, 1)

            tile_of_v = [0]
            run_steps(pe, step, lambda: tile_of_v.__setitem__(0, 1))

        @block.scalar
        def _(act):
            act.nop().then_inc(proj_copied, 5)
            act.nop().then_inc(sg_ready, 2)
            act.nop().then_inc(q_copied, 2)
            act.nop().then_inc(sc_copied, 2)

            def ln_sd(n, p=P):
                act.wait_ge(var_ready, n + 1)
                act.activation(sd[0:p, 0:1], mv[0:p, 1:2], ACT.Sqrt, bias=eps[0:p, :]).then_inc(sd_done, 1)

            def turned_copy(i, dst, src):
                act.wait_ge(turned, i + 1)
                act.activation(dst, src, ACT.Copy).then_inc(turned_copied, 1)

            def bank(i):
                return ps[:, 4 + i % 4, :]

            act.wait_ge(const_ready, 7)
            ln_sd(LN_X)
            turned_copy(0, pcol[:, :], bank(0)[:, 0:96])
            turned_copy(1, convw[:, :, :].rearrange("p a b -> p (a b)"), bank(1)[:, 0:128])
            turned_copy(2, cfw[:, :], bank(2)[:, 0:496])
            ln_sd(LN_X + 1)
            ln_sd(LN_META, META)
            for t in range(NT):
                for q in range(4):
                    i = TURN_X + 4 * t + q
                    turned_copy(i, hT[:, 4 * q:4 * q + 4, META + t * P:META + (t + 1) * P],
                                bank(i).rearrange("p (a b) -> p a b", a=4))
            turned_copy(TURN_META, hT[:, :, 0:META], bank(TURN_META)[:, 0:KT * META].rearrange("p (a b) -> p a b", a=KT))
            for q in range(4):
                i = TURN_KEYS + q
                turned_copy(i, keysT[:, 4 * q:4 * q + 4, :], bank(i).rearrange("p (a b) -> p a b", a=4))

            act.wait_ge(param_loaded, 16 * 15)
            act.activation(head[:, 1:2], head[:, 1:2], ACT.Exp).then_inc(alog_ready, 1)
            act.wait_ge(x1_ready, 1)
            act.activation(hsm[2], hsm[1], ACT.Exp, scale=-1.0).then_inc(ex_ready, 1)
            act.wait_ge(rel_ready, 1)
            act.activation(hsm[6], hsm[8], ACT.Exp, scale=-1.0).then_inc(w_ready, 1)
            a, b = CHUNKS[1]
            act.activation(head[:, 2:3], cs[:, b - 1:b], ACT.Exp).then_inc(ecl_ready, 1)
            act.wait_ge(tabs_done, 1)
            act.activation(tm[:, 0:5, :], T1[:, 0:5 * HEADS].rearrange("p (a b) -> p a b", a=5), ACT.Copy)
            act.activation(tm[0:META, 5, :], T1[0:META, 5 * HEADS:6 * HEADS], ACT.Copy).then_inc(tabs_copied, 1)
            act.activation(edec[:, :], T1[:, 6 * HEADS:7 * HEADS], ACT.Copy).then_inc(tabs_copied, 1)

            with act.Fori(0, GROUPS) as g:
                act.wait_ge(proj_done, g * 5 + 1)
                act.wait_ge(conv_ready, g * 4 + 4)
                act.activation(xin[:, 0:2, :], ps[:, 0:2, 0:L], ACT.Copy).then_inc(proj_copied, 1)
                act.wait_ge(proj_done, g * 5 + 2)
                act.activation(xin[:, 2:4, :], ps[:, 2:4, 0:L], ACT.Copy).then_inc(proj_copied, 1)
                for i, tile in enumerate((g * 2, g * 2 + 1, g + 16, g + 24)):
                    act.wait_ge(conv_ready, g * 4 + (i + 5))
                    act.activation(xg[:, i, :], acc[:, i, :], ACT.Silu, bias=pcol[:, ds(tile, 1)]).then_inc(xg_ready, 1)
                act.wait_ge(seg_ready, g + 1)
                act.activation(ecs[:, :, :, :].rearrange("p c h i -> p c (h i)"), ps[:, 4:6, :], ACT.Exp).then_inc(
                    ecs_ready, 1)
                act.activation(seg[:, :, :, :], seg[:, :, :, :], ACT.Exp).then_inc(exp_ready, 1)
                act.wait_ge(proj_done, g * 5 + 3)
                act.wait_ge(cf_ready, g + 1)
                act.activation(vraw[:, :, :], ps[:, 0:2, 0:L], ACT.Copy).then_inc(proj_copied, 1)
                act.wait_ge(xtm_ready, g + 1)
                act.activation(btm[:, 0, :], T3[:, 0:P], ACT.Copy).then_inc(btm_ready, 1)
                act.activation(btm[0:META, 1, :], T3[0:META, P:2 * P], ACT.Copy).then_inc(btm_ready, 1)
                act.wait_ge(proj_done, g * 5 + 4)
                act.activation(zs[:, :, :], ps[:, 2:4, 0:SEQ], ACT.Silu).then_inc(proj_copied, 1)
                act.wait_ge(v_ready, g + 1)
                act.activation(v2[:, :, :], v[:, :, :], ACT.Square).then_inc(sq_ready, 1)
                act.wait_ge(proj_done, g * 5 + 5)
                act.activation(gsig[:, :, :], ps[:, 2:4, 0:L], ACT.Sigmoid).then_inc(proj_copied, 1)
                act.wait_ge(nsum_done, g + 1)
                act.activation(rinv[:, 0, :], T2[:, 0:SEQ], ACT.Sqrt, bias=eps[:, :], scale=1.0 / SW).then_inc(nsd_ready, 1)

            def sig_body(i, base):
                for j in range(2):
                    act.wait_ge(mm2_done, (i + base) * 4 + (2 * j + 1))
                    act.wait_ge(mix_ready, (i + base) * 2 + (j + 1))
                    act.activation((v, v2)[j][:, :, :], ps[:, 2 * j, :].rearrange("p (u t) -> p u t", u=2),
                                   ACT.Sigmoid).then_inc(sg_ready, 1)

            with act.Fori(0, 2) as i:
                sig_body(i, 0)
            act.wait_ge(cen_ready, 1)
            act.activation(csq[:, :, :], cT[:, :, :], ACT.Square).then_inc(csq_ready, 1)
            sig_body(2, 0)
            act.wait_ge(cvar_done, 1)
            act.activation(rinv[:, 0, :], T1[:, 0:SEQ], ACT.Sqrt, bias=eps[:, :]).then_inc(csd_ready, 1)
            sig_body(3, 0)
            act.wait_ge(cn_ready, 1)
            for k in range(KT):
                act.activation(cT[:, k, :], cT[:, k, :], ACT.Silu, bias=pcol[:, 80 + k:81 + k],
                               scale=pcol[:, 64 + k:65 + k]).then_inc(c_ready, 1)
            with act.Fori(0, 4) as i:
                sig_body(i, 4)

            for t in range(NT):
                ln_sd(LN_H1 + t)
            for t in range(NT):
                for q in range(4):
                    i = TURN_H1 + 4 * t + q
                    turned_copy(i, hT[:, 4 * q:4 * q + 4, t * P:(t + 1) * P], bank(i).rearrange("p (a b) -> p a b", a=4))

            def sc_copy(i, j):
                act.wait_ge(sc_done, i * 4 + (j + 3))
                act.wait_ge(topk_done, i * 4 + (j + 1))
                act.activation(scs[j % 2], ps[:, 2 + j % 2, :].rearrange("p (a b) -> p a b", a=4), ACT.Copy).then_inc(
                    sc_copied, 1)

            with act.Fori(0, 2) as i:
                for j in range(4):
                    act.wait_ge(q_done, i * 4 + (j + 1))
                    act.wait_ge(sc_done, i * 4 + (j + 1))
                    act.activation(qts[j % 2], ps[:, j % 2, :].rearrange("p (a b) -> p a b", a=2), ACT.Copy).then_inc(
                        q_copied, 1)
                    if j:
                        sc_copy(i, j - 1)
                sc_copy(i, 3)
            act.wait_ge(gexp_in, 1)
            act.activation(gates[:, :, :], gates[:, :, :], ACT.Exp).then_inc(gexp_done, 1)

            def step(s, par, u, v_):
                if not v_:
                    return
                act.wait_ge(u_used, s * TOPK)
                act.activation(gel[:, 1 - par, :], dots[:, 1 - par, :], ACT.Gelu).then_inc(gelu_ready, 1)
                act.wait_ge(wgt_ready, s)
                for k in range(TOPK):
                    if not (isinstance(s, int) and (s - 1) * TOPK + k < 4):
                        act.wait_ge(v_used, s * TOPK + (k - 3 - TOPK))
                    act.activation(diag[k % 4], ident[:, :], ACT.Copy, scale=wgt[:, 1 - par, k:k + 1]).then_inc(
                        diag_ready, 1)

            def tail(t):
                ln_sd(LN_OUT + t)

            run_steps(act, step, lambda: tail(0))
            tail(1)

        @block.vector
        def _(dve):
            dve.nop().then_inc(conv_ready, 4)
            dve.nop().then_inc(cf_ready, 1)
            dve.nop().then_inc(mix_ready, 2)
            dve.nop().then_inc(res_ready, 4)
            dve.nop().then_inc(topk_done, 2)
            count = [0]

            def done(ins):
                ins.then_inc(vec_step, 1)
                count[0] += 1

            def then():
                dve.wait_ge(vec_step, count[0])

            def layer_norm(n, rows_, p=P):
                for q in range(4):
                    last = dve.bn_stats(stats[0:p, q, :], rows_[:, q * 512:(q + 1) * 512])
                done(last)
                then()
                dve.bn_aggr(mv[0:p, :], stats[0:p, :, :].rearrange("p a b -> p (a b)")).then_inc(var_ready, 1)
                dve.wait_ge(var_ready, n + 1)
                dve.wait_ge(sd_done, n + 1)
                done(dve.reciprocal(sd[0:p, 1:2], sd[0:p, 0:1]))
                then()
                done(dve.tensor_scalar(rows_, rows_, mv[0:p, 0:1], sd[0:p, 1:2], ALU.subtract, ALU.mult))
                then()
                done(dve.tensor_tensor(rows_, rows_, gain[0:p, 0, :], ALU.mult))
                then()
                dve.tensor_tensor(rows_, rows_, gain[0:p, 1, :], ALU.add).then_inc(ln_done, 1)

            for t in range(NT):
                dve.wait_ge(x_loaded[t], 16)
                dve.wait_ge(gain_loaded, 32)
                layer_norm(LN_X + t, rows[:, t, :])
            dve.wait_ge(meta_loaded, 16)
            layer_norm(LN_META, meta_t, META)

            xb, xa, u_, s_, dtv, ncs, wst, ecl, rel, q_, p_ = hsm[0:11]
            dve.wait_ge(param_loaded, 16 * 15)
            dve.wait_ge(const_ready, 7)
            dve.wait_ge(dt_done, 1)
            done(dve.tensor_scalar(xb, T0[0:HEADS, 0:L], head[:, 0:1], None, ALU.add))
            then()
            dve.scalar_tensor_tensor(xa, xb, -1.0, xb, ALU.mult, ALU.max).then_inc(x1_ready, 1)
            dve.wait_ge(ex_ready, 1)
            done(dve.tensor_scalar(s_, u_, 2.0, None, ALU.add))
            then()
            done(dve.reciprocal(q_, s_))
            then()
            done(dve.tensor_tensor(s_, u_, q_, ALU.mult))
            then()
            done(dve.tensor_tensor(q_, s_, s_, ALU.mult))
            then()
            done(dve.tensor_scalar(p_, q_, 1.0 / 15, None, ALU.mult))
            then()
            for n in (13, 11, 9, 7, 5, 3):
                done(dve.scalar_tensor_tensor(p_, p_, 1.0 / n, q_, ALU.add, ALU.mult))
                then()
            done(dve.scalar_tensor_tensor(p_, p_, 1.0, s_, ALU.add, ALU.mult))
            done(dve.tensor_scalar(xb, xb, 0.0, None, ALU.max))
            then()
            done(dve.scalar_tensor_tensor(dtv, p_, 2.0, xb, ALU.mult, ALU.add))
            then()
            dve.wait_ge(alog_ready, 1)
            done(dve.tensor_scalar(q_, dtv, head[:, 1:2], -1.0, ALU.mult, ALU.mult))
            then()
            for a, b in CHUNKS:
                done(dve.tensor_tensor_scan(cs[:, a:b], ones[0:HEADS, 0:b - a], q_[:, a:b], 0.0, ALU.mult, ALU.add))
            then()
            done(dve.tensor_scalar(ncs, cs[:, :], -1.0, None, ALU.mult))
            for a, b in CHUNKS[0:1]:
                done(dve.tensor_scalar(rel[:, a:b], cs[:, a:b], cs[:, b - 1:b], None, ALU.subtract))
            a, b = CHUNKS[2]
            done(dve.tensor_scalar(rel[:, a:b], cs[:, a:b], cs[:, b - 1:b], None, ALU.subtract))
            a, b = CHUNKS[1]
            dve.tensor_scalar(rel[:, a:b], cs[:, a:b], cs[:, b - 1:b], None, ALU.subtract).then_inc(rel_ready, 1)
            dve.wait_ge(w_ready, 1)
            done(dve.tensor_tensor(wst, wst, dtv, ALU.mult))
            dve.wait_ge(ecl_ready, 1)
            dve.tensor_scalar(ecl[:, 0:P], ones[0:HEADS, :], head[:, 2:3], None, ALU.mult).then_inc(tabs_ready, 1)

            PER = 4 * (KC - 1) + 1 + 2 + 2 + 1 + 1 + 2 * (KF - 1) + 1
            start = count[0]
            with dve.Fori(0, GROUPS) as g:
                count[0] = start
                turn_ = g * PER

                def hold(back=0):
                    dve.wait_ge(vec_step, turn_ + (count[0] - back))

                for c in range(2):
                    a, b = CHUNKS[1 + c]
                    last = dve.tensor_tensor(rmask[:, c, :, :],
                                             ident[0:HEADS, ds(g * HPG, HPG)].unsqueeze(2).to_broadcast([HEADS, HPG, P]),
                                             cs[:, a:b].unsqueeze(1).to_broadcast([HEADS, HPG, P]), ALU.mult)
                last.then_inc(r_ready, 1)
                tiles = (g * 2, g * 2 + 1, g + 16, g + 24)
                for k in range(KC - 1, -1, -1):
                    for i, tile in enumerate(tiles):
                        w = convw[:, k, ds(tile, 1)]
                        m = KC - 1 - k
                        if k == KC - 1:
                            if i % 2 == 0:
                                dve.wait_ge(proj_copied, g * 5 + (6 + i // 2))
                            done(dve.tensor_scalar(acc[:, i, :], xin[:, i, :], w, None, ALU.mult))
                        else:
                            hold(3 if k else 3 - i)
                            ins = dve.scalar_tensor_tensor(acc[:, i, m:L], xin[:, i, 0:L - m], w, acc[:, i, m:L],
                                                           ALU.mult, ALU.add)
                            if k:
                                done(ins)
                            else:
                                ins.then_inc(conv_ready, 1)
                dve.wait_ge(csb_done, g + 1)
                for c in range(2):
                    for hh in range(HPG):
                        last = dve.tensor_scalar(seg[:, c, hh, :], ps[:, 4 + c, hh * P:(hh + 1) * P],
                                                 tm[:, 2 + c, ds(g * HPG + hh, 1)], 0.0, ALU.add, ALU.min)
                last.then_inc(seg_ready, 1)
                dve.wait_ge(xpose_done, g + 1)

                def per_head(table, p=P):
                    return tm[0:p, table, ds(g * HPG, HPG)].unsqueeze(2).to_broadcast([p, HPG, HD])

                def heads(ap):
                    return ap.rearrange("p (h d) -> p h d", d=HD)

                for c in range(2):
                    dve.tensor_tensor(heads(xdt[:, c, :]), heads(T2[:, c * 2 * P:(c + 1) * 2 * P]), per_head(c), ALU.mult)
                dve.tensor_tensor(heads(xw[:, 0, :]), heads(T2[:, 0:2 * P]), per_head(4), ALU.mult)
                dve.tensor_tensor(heads(xw[0:META, 1, :]), heads(T3[0:META, 2 * P:4 * P]), per_head(5, META),
                                  ALU.mult).then_inc(xtm_ready, 1)
                dve.wait_ge(score_done, g + 1)
                done(dve.tensor_tensor(scm[:, :, :], T0[:, 0:2 * P].rearrange("p (c i) -> p c i", c=2),
                                       causal[:, :].unsqueeze(1).to_broadcast([P, 2, P]), ALU.mult))
                hold()
                dve.wait_ge(exp_ready, g + 1)
                for c in range(2):
                    dve.tensor_tensor(seg[:, c, :, :], seg[:, c, :, :],
                                      scm[:, c, :].unsqueeze(1).to_broadcast([P, HPG, P]), ALU.mult)
                dve.wait_ge(ecs_ready, g + 1)
                for c in range(2):
                    a, b = CHUNKS[1 + c]
                    last = dve.tensor_tensor(ecs[:, c, :, :], ecs[:, c, :, :],
                                             xg[:, 3, a:b].unsqueeze(1).to_broadcast([P, HPG, P]), ALU.mult)
                last.then_inc(mt_ready, 1)
                dve.wait_ge(state_done, g + 1)
                done(dve.tensor_copy(state[:, 0, :], T3[:, 0:HPG * HD]))
                hold()
                done(dve.tensor_tensor(heads(state[:, 1, :]), heads(state[:, 0, :]),
                                       edec[:, ds(g * HPG, HPG)].unsqueeze(2).to_broadcast([P, HPG, HD]), ALU.mult))
                hold()
                dve.tensor_tensor(state[:, 1, :], state[:, 1, :], T3[:, HPG * HD:2 * HPG * HD], ALU.add).then_inc(
                    s_ready, 1)
                dve.wait_ge(y_done, g + 1)
                for u in range(2):
                    done(dve.scalar_tensor_tensor(v[:, u, :], xg[:, u, META:L], dcol[:, ds(g * 2 + u, 1)],
                                                  T1[:, u * SEQ:(u + 1) * SEQ], ALU.mult, ALU.add))
                hold()
                dve.wait_ge(proj_copied, g * 5 + 9)
                dve.tensor_tensor(v[:, :, :], v[:, :, :], zs[:, :, :], ALU.mult).then_inc(v_ready, 1)
                dve.wait_ge(nsd_ready, g + 1)
                done(dve.reciprocal(rinv[:, 1, :], rinv[:, 0, :]))
                hold()
                for u in range(2):
                    last = dve.scalar_tensor_tensor(yT[:, ds(g * 2 + u, 1), :].rearrange("p a b -> p (a b)"), v[:, u, :],
                                                    pcol[:, ds(g * 2 + (32 + u), 1)], rinv[:, 1, :], ALU.mult, ALU.mult)
                last.then_inc(ynorm_ready, 1)
                dve.wait_ge(proj_copied, g * 5 + 10)
                done(dve.tensor_tensor(gsig[:, :, :], gsig[:, :, :], vraw[:, :, :], ALU.mult))
                hold()
                for k in range(KF - 1, -1, -1):
                    back = KF - 1 - k
                    t0 = max(META, back)
                    for u in range(2):
                        ct = cT[:, ds(g * 2 + u, 1), :].rearrange("p a b -> p (a b)")
                        w = cfw[:, ds(g * 2 + (k * KT + u), 1)]
                        if back == 0:
                            ins = dve.tensor_scalar(ct, gsig[:, u, META:L], w, pcol[:, ds(g * 2 + (48 + u), 1)],
                                                    ALU.mult, ALU.add)
                        else:
                            hold(1)
                            o = cT[:, ds(g * 2 + u, 1), t0 - META:SEQ].rearrange("p a b -> p (a b)")
                            ins = dve.scalar_tensor_tensor(o, gsig[:, u, t0 - back:L - back], w, o, ALU.mult, ALU.add)
                        if k or u == 0:
                            done(ins)
                        else:
                            ins.then_inc(cf_ready, 1)
                body_steps = count[0] - start
            assert PER == body_steps, (PER, body_steps)
            count[0] = start + GROUPS * PER

            def mix_body(i, base, add):
                for j in range(2):
                    dve.wait_ge(sg_ready, (i + base) * 2 + (j + 3))
                    dve.wait_ge(mm2_done, (i + base) * 4 + (2 * j + 2))
                    g_ = (v, v2)[j]
                    src = ps[:, 2 * j + 1, :].rearrange("p (u t) -> p u t", u=2)
                    dst = mT[:, ds(i * 4 + 2 * j, 2), :]
                    if add:
                        dve.tensor_tensor(g_[:, :, :], g_[:, :, :], src, ALU.mult).then_inc(gated, 1)
                        dve.wait_ge(gated, i * 2 + (j + 1))
                        dve.tensor_tensor(dst, dst, g_[:, :, :], ALU.add).then_inc(mix_ready, 1)
                    else:
                        dve.tensor_tensor(dst, g_[:, :, :], src, ALU.mult).then_inc(mix_ready, 1)

            with dve.Fori(0, 2) as i:
                mix_body(i, 0, False)
            dve.wait_ge(mean_done, 1)
            dve.tensor_tensor(cT[:, :, :], cT[:, :, :], T0[:, 0:SEQ].unsqueeze(1).to_broadcast([P, KT, SEQ]),
                              ALU.subtract).then_inc(cen_ready, 1)
            mix_body(2, 0, False)
            dve.wait_ge(csd_ready, 1)
            dve.wait_ge(csq_ready, 1)
            done(dve.reciprocal(rinv[:, 1, :], rinv[:, 0, :]))
            then()
            dve.tensor_tensor(cT[:, :, :], cT[:, :, :], rinv[:, 1, :].unsqueeze(1).to_broadcast([P, KT, SEQ]),
                              ALU.mult).then_inc(cn_ready, 1)
            mix_body(3, 0, False)
            with dve.Fori(0, 4) as i:
                mix_body(i, 4, True)

            with dve.Fori(0, 2) as i:
                for j in range(4):
                    dve.wait_ge(wo_done, i * 4 + (j + 1))
                    o = rows[:, :, ds(i * (4 * SW) + j * SW, SW)]
                    dve.scalar_tensor_tensor(o, o, ALPHA, ps[:, j, :].rearrange("p (t n) -> p t n", t=NT),
                                             ALU.mult, ALU.add).then_inc(res_ready, 1)
            dve.wait_ge(res_ready, 12)
            dve.wait_ge(gain_loaded, 64)
            for t in range(NT):
                layer_norm(LN_H1 + t, rows[:, t, :])

            start4 = count[0]
            with dve.Fori(0, 2) as i:
                count[0] = start4

                def hold():
                    dve.wait_ge(vec_step, i * T4 + count[0])
                    settle(dve)

                for j in range(4):
                    sc = scs[j % 2]
                    dve.wait_ge(sc_copied, i * 4 + (j + 3))
                    settle(dve)
                    for q in range(4):
                        last = dve.max(topv[:, q, 0:8], sc[:, q, :])
                    done(last)
                    hold()
                    for q in range(4):
                        dve.max_index(topi[:, q, 0:8], topv[:, q, 0:8], sc[:, q, :])
                        last = dve.match_replace(left[:, q, :], topv[:, q, 0:8], sc[:, q, :], LOW)
                    done(last)
                    hold()
                    for q in range(4):
                        last = dve.max(topv[:, q, 8:16], left[:, q, :])
                    done(last)
                    hold()
                    for q in range(4):
                        last = dve.max_index(topi[:, q, 8:16], topv[:, q, 8:16], left[:, q, :])
                    done(last)
                    for t in range(NT):
                        last = dve.tensor_tensor(cand[:, t, :].rearrange("p (a b) -> p a b", a=TOPK),
                                                 topv[:, 2 * t, :].unsqueeze(2).to_broadcast([P, TOPK, TOPK]),
                                                 topv[:, 2 * t + 1, :].unsqueeze(1).to_broadcast([P, TOPK, TOPK]),
                                                 ALU.add)
                    done(last)
                    hold()
                    dve.tensor_copy(topif, topi)
                    for t in range(NT):
                        last = dve.max(bestv[:, t, 0:8], cand[:, t, :])
                    done(last)
                    hold()
                    for t in range(NT):
                        dve.max_index(bestj[:, t, 0:8], bestv[:, t, 0:8], cand[:, t, :])
                        last = dve.match_replace(cand2[:, t, :], bestv[:, t, 0:8], cand[:, t, :], LOW)
                    done(last)
                    hold()
                    for t in range(NT):
                        last = dve.max(bestv[:, t, 8:16], cand2[:, t, :])
                    done(last)
                    hold()
                    for t in range(NT):
                        last = dve.max_index(bestj[:, t, 8:16], bestv[:, t, 8:16], cand2[:, t, :])
                        dve.tensor_copy(best[:, ds(i * 4 + (t * PH + j), 1), :].rearrange("p a b -> p (a b)"),
                                        bestv[:, t, :])
                    done(last)
                    hold()
                    dve.tensor_scalar(part[:, 0, :, :], bestj, 4, None, ALU.logical_shift_right)
                    done(dve.tensor_scalar(part[:, 1, :, :], bestj, 15, None, ALU.bitwise_and))
                    hold()
                    done(dve.tensor_copy(partf, part))
                    hold()
                    for s in range(2):
                        keyno = topif.rearrange("p (t s) i -> p s t i", s=2)[:, s, :, :]
                        done(dve.tensor_tensor(hot, partf[:, s, :, :].unsqueeze(3).to_broadcast([P, NT, TOPK, TOPK]),
                                               iota16[:, :].unsqueeze(1).unsqueeze(1).to_broadcast([P, NT, TOPK, TOPK]),
                                               ALU.is_equal))
                        hold()
                        for t in range(NT):
                            last = dve.tensor_tensor(hot[:, t, :, :], hot[:, t, :, :],
                                                     keyno[:, t, :].unsqueeze(1).to_broadcast([P, TOPK, TOPK]), ALU.mult)
                        done(last)
                        hold()
                        done(dve.tensor_reduce(pick[:, s, :, :], hot, AX.X, ALU.add))
                        hold()
                    for t in range(NT):
                        last = dve.scalar_tensor_tensor(
                            idx[:, ds(i * 4 + (t * PH + j), 1), :].rearrange("p a b -> p (a b)"),
                            pick[:, 0, t, :], float(NK), pick[:, 1, t, :], ALU.mult, ALU.add)
                    last.then_inc(topk_done, 1)
                body4 = count[0] - start4
            assert T4 == body4, body4
            count[0] = start4 + 2 * T4
            dve.memset(idx[:, NT * PH:, :], 0)
            dve.wait_ge(topk_done, 2 + PH)
            dve.tensor_copy(ixv[:, 0, :], idx[:, 0, :])
            dve.tensor_copy(ixu[:, 0, :], idx[:, 0, :]).then_inc(ix_staged, 1)
            dve.tensor_tensor(gates[:, :, :], best[:, :, :], best[:, :, 0:1].to_broadcast([P, NT * PH, TOPK]),
                              ALU.subtract).then_inc(gexp_in, 1)
            dve.wait_ge(gexp_done, 1)
            done(dve.tensor_reduce(gsum[:, :, 0], gates[:, :, :], AX.X, ALU.add))
            then()
            done(dve.reciprocal(gsum[:, :, :], gsum[:, :, :]))
            then()
            done(dve.tensor_tensor(gates[:, :, :], gates[:, :, :], gsum[:, :, 0:1].to_broadcast([P, NT * PH, TOPK]),
                                   ALU.mult))
            then()

            tile_of_u = [0]

            def weights(s, par):
                dve.wait_ge(gelu_ready, s)
                if not (isinstance(s, int) and s < 3):
                    dve.wait_ge(diag_ready, s * TOPK - 2 * TOPK)
                g_ = gates[:, ds(s - 1, 1), :].rearrange("p a b -> p (a b)")
                dve.tensor_tensor(wgt[:, 1 - par, :], gel[:, 1 - par, :], g_, ALU.mult).then_inc(wgt_ready, 1)

            def step(s, par, u, v_):
                if isinstance(s, int) and s == PH:
                    tile_of_u[0] = 1
                for k in range(TOPK):
                    if k == 1 and v_:
                        weights(s, par)
                    if k == 8 and not (isinstance(s, int) and s == 2 * PH):
                        if not (isinstance(s, int) and s < 2):
                            dve.wait_ge(v_used, s * TOPK - TOPK)
                        if not (isinstance(s, int) and s == 2 * PH - 1):
                            dve.tensor_copy(ixu[:, 1 - par, :], idx[:, ds(s + 1, 1), :].rearrange("p a b -> p (a b)"))
                        dve.tensor_copy(ixv[:, par, :], idx[:, ds(s, 1), :].rearrange("p a b -> p (a b)")).then_inc(
                            ix_staged, 1)
                    if u:
                        b = k % UB
                        dve.wait_ge(u_loaded[b], s * (TOPK // UB * 16) + (k // UB + 1) * 16)
                        dve.tensor_tensor_reduce(ubuf[b], ubuf[b], rows[:, tile_of_u[0], :], 1.0, 0.0,
                                                 ALU.mult, ALU.add, dots[:, par, k:k + 1]).then_inc(u_used, 1)

            def finish(t):
                dve.wait_ge(v_used, (t + 1) * PH * TOPK)
                dve.wait_ge(gain_loaded, 96)
                done(dve.scalar_tensor_tensor(rows[:, t, :], rows[:, t, :], ALPHA,
                                              ps[:, 4 * t:4 * t + 4, :].rearrange("p a b -> p (a b)"),
                                              ALU.mult, ALU.add))
                then()
                layer_norm(LN_OUT + t, rows[:, t, :])

            run_steps(dve, step, lambda: finish(0))
            finish(1)


T4 = 4 * 17


_INS = ["x", "meta", "ln0_g", "ln0_b", "w_in", "ssd_conv_w", "ssd_conv_b", "ssd_dt_bias", "ssd_a_log", "ssd_d",
        "ssd_norm_w", "ssd_out", "cf_dw_w", "cf_dw_b", "cf_ln_g", "cf_ln_b", "cf_out", "w_o", "ln1_g", "ln1_b",
        "peer_wq", "peer_keys", "peer_u", "peer_v", "ln2_g", "ln2_b"]


def kernel(**inputs):
    import numpy as _np
    import concourse.bacc as _bacc
    from concourse import mybir as _mybir
    from concourse.bass_utils import run_bass_kernel_spmd as _run

    nc = _bacc.Bacc("TRN2", target_bir_lowering=False, num_devices=1)
    arrays, A = {}, {}
    for name in _INS:
        a = _np.ascontiguousarray(inputs[name])
        arrays[f"in_{name}"] = a
        A[name] = nc.dram_tensor(f"in_{name}", a.shape, _mybir.dt.from_np(a.dtype), kind="ExternalInput").ap()
    out = nc.dram_tensor("out", (1, SEQ, D), _mybir.dt.float32, kind="ExternalOutput").ap()
    build(nc, A, out)
    return _run(nc, [arrays], core_ids=[0]).results[0]["out"]
```

```python
from contextlib import ExitStack

import concourse.bass as bass
from concourse import mybir
from concourse.alu_op_type import AluOpType as ALU

ACT = mybir.ActivationFunctionType
AX = mybir.AxisListType
F32 = mybir.dt.float32
U32 = mybir.dt.uint32
F32R = mybir.dt.float32r

P = 128
D = 2048
SEQ, META = 256, 16
L = META + SEQ
KT = D // P
SW = 256
NS = D // SW
GROUPS, HEADS, HPG, HD = 8, 32, 4, 64
KC, KF = 4, 31
XBC = D + 2 * GROUPS * P
OFF_XBC = D
OFF_DT = OFF_XBC + XBC
OFF_VAL = OFF_DT + HEADS
OFF_CGATE = OFF_VAL + D
OFF_GSSD = OFF_CGATE + D
OFF_GCF = OFF_GSSD + D
CHUNKS = [(0, META), (META, META + P), (META + P, L)]
PH, NK, TOPK = 8, 128, 16
NT = SEQ // P
EPS = 1e-5
ALPHA = 2.0 ** 0.25
LOW = -3.0e38
UNITS = 4
KU = KT // UNITS
S_GROUP = 1
S_SSD = S_GROUP + 5 * GROUPS
S_CF = S_SSD + 2 * NS
S_WO = S_CF + 2 * NS
S_WQ = S_WO + NS
S_END = S_WQ + NS
UB = 4
LN_X, LN_META, LN_H1, LN_OUT = 0, 2, 3, 5


def build(nc, A, out):
    ds = bass.ds
    x, meta = A["x"][0], A["meta"]
    w_in, ssd_out, cf_out, w_o, wq = (A[n][0] for n in ("w_in", "ssd_out", "cf_out", "w_o", "peer_wq"))
    peer_u, peer_v = A["peer_u"][0], A["peer_v"][0]

    with ExitStack() as ctx:
        def sb(name, shape, dt=F32):
            return ctx.enter_context(nc.sbuf_tensor(name, shape, dt))

        def arena(name, split):
            at = (nc.sbuf_base + 31) // 32 * 32
            flat = sb(name, [P, 2 * KT * SEQ])
            return flat, nc.alloc_sbuf_tensor_at(split, [P, 2, KT, SEQ], F32R, offset=at)

        def sem(name):
            return ctx.enter_context(nc.semaphore(name))

        mem_a, c_split = arena("mem_a", "c_split")
        mem_b, ym_split = arena("mem_b", "ym_split")
        h_split = sb("h_split", [P, 2, KT, L], F32R)
        rows = sb("rows", [P, NT, D])
        gain = sb("gain", [P, 2, D])
        raw = [sb(f"raw{i}", [P, KU, SW]) for i in range(UNITS)]
        whi = [sb(f"whi{i}", [P, KU, SW], F32R) for i in range(UNITS)]
        wlo = [sb(f"wlo{i}", [P, KU, SW], F32R) for i in range(UNITS)]
        v = sb("v", [P, 2, SEQ])
        v2 = sb("v2", [P, 2, SEQ])
        rinv = sb("rinv", [P, 2, SEQ])
        ident = sb("ident", [P, P])
        ones = sb("ones", [P, P])
        avg = sb("avg", [P, P])
        zero = sb("zero", [P, P])
        causal = sb("causal", [P, P])
        iota16 = sb("iota16", [P, TOPK])
        eps = sb("eps", [P, 1])
        pcol = sb("pcol", [P, 96])
        convw = sb("convw", [P, KC, 32])
        cfw = sb("cfw", [P, 4 * 124])
        dcol = sb("dcol", [P, KT])
        head = sb("head", [HEADS, 4])
        cs = sb("cs", [HEADS, L])
        tm = sb("tm", [P, 6, HEADS])
        edec = sb("edec", [P, HEADS])
        stats = sb("stats", [P, 4, 6])
        mv = sb("mv", [P, 2])
        sd = sb("sd", [P, 2])
        route = sb("route", [P, 992])

        def f32(ap):
            return ap.bitcast(F32)

        scr = mem_a[:, 0:12 * L].rearrange("p (a b) -> p a b", b=L)
        xin, acc, xg = scr[:, 0:4, :], scr[:, 4:8, :], scr[:, 8:12, :]
        hsm = [scr[0:HEADS, i, :] for i in range(12)]

        vraw = mem_a[:, 3264:3808].rearrange("p (a b) -> p a b", a=2)
        gsig = mem_a[:, 3808:4352].rearrange("p (a b) -> p a b", a=2)
        zs = mem_a[:, 4352:4864].rearrange("p (a b) -> p a b", a=2)
        btm = mem_a[:, 4864:5120].rearrange("p (a b) -> p a b", a=2)
        scm = mem_a[:, 5120:5376].rearrange("p (a b) -> p a b", a=2)
        state = mem_a[:, 5376:5888].rearrange("p (a b) -> p a b", a=2)
        meta_t = mem_a[0:META, 5888:5888 + D]
        prow = mem_b[0:96, 0:128]
        convrow = mem_b[:, 128:256]
        cfrow = mem_b[0:124, 256:768].rearrange("p (a b) -> p a b", a=4)
        rflat = rows[:, :, :].rearrange("p a b -> p (a b)")
        seg = rflat[:, 0:1024].rearrange("p (c h i) -> p c h i", c=2, h=HPG)
        ecs = rflat[:, 1024:2048].rearrange("p (c h i) -> p c h i", c=2, h=HPG)
        rmask = rflat[0:HEADS, 2048:3072].rearrange("p (c h i) -> p c h i", c=2, h=HPG)
        xdt = rflat[:, 3072:3584].rearrange("p (c n) -> p c n", c=2)
        xw = rflat[:, 3584:4096].rearrange("p (c n) -> p c n", c=2)
        mix1 = rflat.rearrange("p (a b) -> p a b", a=KT)
        gflat = gain[:, :, :].rearrange("p a b -> p (a b)")
        cT = gflat.rearrange("p (a b) -> p a b", a=KT)
        csq = mem_a[:, 0:KT * SEQ].rearrange("p (a b) -> p a b", a=KT)
        res = [v, v2]
        qts = [v, v2]
        left = mem_a[:, 0:512].rearrange("p (a b) -> p a b", a=4)
        cand = mem_a[:, 512:1024].rearrange("p (t a) -> p t a", t=2)
        cand2 = mem_a[:, 1024:1536].rearrange("p (t a) -> p t a", t=2)
        hot = mem_a[:, 1536:2048].rearrange("p (t k i) -> p t k i", t=2, k=TOPK)
        topv = mem_a[:, 2048:2112].rearrange("p (a b) -> p a b", a=4)
        topif = mem_a[:, 2112:2176].rearrange("p (a b) -> p a b", a=4)
        topi = mem_a[:, 2176:2240].rearrange("p (a b) -> p a b", a=4).bitcast(U32)
        bestv = mem_a[:, 2240:2272].rearrange("p (a b) -> p a b", a=2)
        bestj = mem_a[:, 2272:2304].rearrange("p (a b) -> p a b", a=2).bitcast(U32)
        part = mem_a[:, 2304:2368].rearrange("p (s a b) -> p s a b", s=2, a=2).bitcast(U32)
        partf = mem_a[:, 2368:2432].rearrange("p (s a b) -> p s a b", s=2, a=2)
        pick = mem_a[:, 2432:2496].rearrange("p (s a b) -> p s a b", s=2, a=2)
        scs = [mem_a[:, 2560 + 512 * i:3072 + 512 * i].rearrange("p (a b) -> p a b", a=4) for i in range(2)]
        keysT = mem_a[:, 3584:5632].rearrange("p (a b) -> p a b", a=2 * PH)
        keyrow = mem_a[:, 5632:7680].rearrange("p (a b) -> p a b", a=2 * PH)
        gates = route[:, 0:256].rearrange("p (a b) -> p a b", b=TOPK)
        best = route[:, 256:512].rearrange("p (a b) -> p a b", b=TOPK)
        idx = route[:, 512:800].rearrange("p (a b) -> p a b", b=TOPK).bitcast(U32)
        dots, gel, wgt, ixu, ixv = (route[:, 800 + 32 * i:832 + 32 * i].rearrange("p (a b) -> p a b", a=2)
                                    for i in range(5))
        ixu, ixv = ixu.bitcast(U32), ixv.bitcast(U32)
        gsum = route[:, 960:976].rearrange("p (a b) -> p a b", b=1)
        ubuf = [mem_a[:, D * i:D * (i + 1)] for i in range(UB)]
        vbuf = [mem_b[:, D * i:D * (i + 1)] for i in range(UB)]
        diag = [raw[0][:, 0, i * P:(i + 1) * P] for i in range(2)] + [raw[0][:, 1, i * P:(i + 1) * P] for i in range(2)]

        ps = ctx.enter_context(nc.psum_tensor("ps", [P, 8, 512], F32))
        T0, T1, T2, T3 = (ps[:, 4 + i, :] for i in range(4))

        x_loaded = [sem(f"x_loaded{i}") for i in range(NT)]
        meta_loaded, gain_loaded, param_loaded, keys_loaded = (sem(n) for n in (
            "meta_loaded", "gain_loaded", "param_loaded", "keys_loaded"))
        raw_loaded = [sem(f"raw_loaded{i}") for i in range(UNITS)]
        c_cols_loaded = [sem(f"c_cols_loaded{i}") for i in range(UNITS)]
        hi_ready, lo_ready, unit_done = sem("hi_ready"), sem("lo_ready"), sem("unit_done")
        u_loaded = [sem(f"u_loaded{i}") for i in range(UB)]
        v_loaded = [sem(f"v_loaded{i}") for i in range(UB)]
        const_step, const_ready = sem("const_step"), sem("const_ready")
        vec_step, gated = sem("vec_step"), sem("gated")
        var_ready, sd_done, ln_done = sem("var_ready"), sem("sd_done"), sem("ln_done")
        turned, turned_hi, turned_lo = sem("turned"), sem("turned_hi"), sem("turned_lo")
        rel_ready, w_ready, tabs_ready = sem("rel_ready"), sem("w_ready"), sem("tabs_ready")
        x1_ready, ex_ready, alog_ready, ecl_ready = (sem(n) for n in ("x1_ready", "ex_ready", "alog_ready", "ecl_ready"))
        tabs_done, tabs_copied, proj_copied = sem("tabs_done"), sem("tabs_copied"), sem("proj_copied")
        r_ready, csb_done, seg_ready, ecs_ready, exp_ready = (sem(n) for n in (
            "r_ready", "csb_done", "seg_ready", "ecs_ready", "exp_ready"))
        conv_ready, xg_ready, xpose_done, score_done = (sem(n) for n in (
            "conv_ready", "xg_ready", "xpose_done", "score_done"))
        xtm_ready, btm_ready, mt_ready, state_done, s_ready = (sem(n) for n in (
            "xtm_ready", "btm_ready", "mt_ready", "state_done", "s_ready"))
        y_done, v_ready, sq_ready, nsum_done, nsd_ready, ynorm_ready = (sem(n) for n in (
            "y_done", "v_ready", "sq_ready", "nsum_done", "nsd_ready", "ynorm_ready"))
        sg_ready, mix_ready = sem("sg_ready"), sem("mix_ready")
        cf_ready, mean_done, cen_ready, csq_ready, cvar_done, csd_ready, cn_ready, silu_ready, c_ready = (sem(n) for n in (
            "cf_ready", "mean_done", "cen_ready", "csq_ready", "cvar_done", "csd_ready", "cn_ready", "silu_ready",
            "c_ready"))
        m_ready = sem("m_ready")
        res_ready, res_turned, res_copied = sem("res_ready"), sem("res_turned"), sem("res_copied")
        q_copied, sc_done, sc_copied, topk_done = (sem(n) for n in ("q_copied", "sc_done", "sc_copied", "topk_done"))
        gexp_in, gexp_done = sem("gexp_in"), sem("gexp_done")
        ix_staged, u_used, v_used, gelu_ready, wgt_ready, diag_ready = (sem(n) for n in (
            "ix_staged", "u_used", "v_used", "gelu_ready", "wgt_ready", "diag_ready"))
        stored, waited = sem("stored"), sem("waited")

        block = ctx.enter_context(nc.Block())

        TURN_X = 3
        TURN_META = TURN_X + 4 * NT
        TURN_KEYS = TURN_META + 1
        TURN_H1 = TURN_KEYS + 4
        TURN_END = TURN_H1 + 4 * NT
        WITH_LO = [*range(TURN_X, TURN_META + 1), *range(TURN_H1, TURN_END)]

        def bank(i):
            return ps[:, 4 + i % 4, :]

        def slab_done(eng, s):
            eng.wait_ge(unit_done, s * UNITS + UNITS)

        def run_steps(eng, step, middle=lambda: None):
            step(0, 0, True, False)
            step(1, 1, True, True)
            with eng.Fori(2, PH, 2) as s:
                step(s, 0, True, True)
                step(s + 1, 1, True, True)
            step(PH, 0, True, True)
            middle()
            step(PH + 1, 1, True, True)
            with eng.Fori(PH + 2, 2 * PH, 2) as s:
                step(s, 0, True, True)
                step(s + 1, 1, True, True)
            step(2 * PH, 0, False, True)
        def settle(eng):
            eng.sem_inc(waited, 1)

        @block.sync
        def _(sp):
            for t in range(NT):
                sp.dma_start(rows[:, t, :], x[t * P:(t + 1) * P, :]).then_inc(x_loaded[t], 16)
            sp.dma_start(meta_t, meta).then_inc(meta_loaded, 16)

            def load_gain(g, b):
                for i, r in enumerate((g, b)):
                    sp.dma_start(gain[:, i, :], r.partition_broadcast(P)).then_inc(gain_loaded, 16)

            load_gain(A["ln0_g"], A["ln0_b"])
            at = 0
            for r, n in (("ssd_conv_b", 32), ("ssd_norm_w", 16), ("cf_dw_b", 16), ("cf_ln_g", 16), ("cf_ln_b", 16)):
                sp.dma_start(prow[at:at + n, :], A[r][0].rearrange("(t p) -> t p", p=P)).then_inc(param_loaded, 16)
                at += n
            for k in range(KC):
                sp.dma_start(convrow[32 * k:32 * k + 32, :],
                             A["ssd_conv_w"][0, k].rearrange("(t p) -> t p", p=P)).then_inc(param_loaded, 16)
            sp.dma_start(cfrow, A["cf_dw_w"][0].rearrange("k (t p) -> (k t) p", p=P).rearrange(
                "(a r) p -> r a p", r=124)).then_inc(param_loaded, 16)
            sp.dma_start(head[:, 0:1], A["ssd_dt_bias"][0].rearrange("(h o) -> h o", o=1)).then_inc(param_loaded, 16)
            sp.dma_start(head[:, 1:2], A["ssd_a_log"][0].rearrange("(h o) -> h o", o=1)).then_inc(param_loaded, 16)
            d2 = A["ssd_d"][0].rearrange("(t u) -> u t", u=2)
            with nc.allow_non_contiguous_dma(reason="32 values"):
                for u in range(2):
                    sp.dma_start(dcol[HD * u:HD * u + HD, :],
                                 d2[u:u + 1, :].to_broadcast([HD, KT])).then_inc(param_loaded, 16)

            def unit_rows(w, q, at, n):
                return w[q * KU * P:(q + 1) * KU * P, ds(at, n)].rearrange("(k p) n -> p k n", p=P)

            def load(s, w, at):
                for q in range(UNITS):
                    if not (isinstance(s, int) and s == 0):
                        sp.wait_ge(lo_ready, s * UNITS + (q + 1 - UNITS))
                        settle(sp)
                    sp.dma_start(raw[q][:, :, :], unit_rows(w, q, at, SW)).then_inc(raw_loaded[q], 16)

            def load_bc(s, g):
                for q in range(UNITS):
                    sp.wait_ge(lo_ready, s * UNITS + (q + 1 - UNITS))
                    settle(sp)
                    sp.dma_start(raw[q][:, :, 0:P], unit_rows(w_in, q, g * P + OFF_XBC + D, P)).then_inc(
                        raw_loaded[q], 16)
                    sp.dma_start(raw[q][:, :, P:SW], unit_rows(w_in, q, g * P + OFF_XBC + D + GROUPS * P, P)).then_inc(
                        c_cols_loaded[q], 16)

            load(0, w_in, OFF_DT)
            with sp.Fori(0, GROUPS) as g:
                load(g * 5 + S_GROUP, w_in, g * SW + OFF_XBC)
                load_bc(g * 5 + (S_GROUP + 1), g)
                load(g * 5 + (S_GROUP + 2), w_in, g * SW + OFF_VAL)
                load(g * 5 + (S_GROUP + 3), w_in, g * SW)
                load(g * 5 + (S_GROUP + 4), w_in, g * SW + OFF_CGATE)
            with sp.Fori(0, NS) as i:
                load(i * 2 + S_SSD, w_in, i * SW + OFF_GSSD)
                load(i * 2 + (S_SSD + 1), ssd_out, i * SW)
            with sp.Fori(0, NS) as i:
                load(i * 2 + S_CF, w_in, i * SW + OFF_GCF)
                load(i * 2 + (S_CF + 1), cf_out, i * SW)
            with sp.Fori(0, NS) as i:
                load(i + S_WO, w_o, i * SW)
            sp.wait_ge(c_ready, 4)
            load_gain(A["ln1_g"][0], A["ln1_b"][0])
            slab_done(sp, S_WO - 1)
            sp.dma_start(keyrow, A["peer_keys"][0].rearrange("s h n k -> n (s h) k")).then_inc(keys_loaded, 16)
            with sp.Fori(0, NS) as i:
                load(i + S_WQ, wq, i * SW)
            sp.wait_ge(ln_done, LN_OUT)
            load_gain(A["ln2_g"][0], A["ln2_b"][0])
            for t in range(NT):
                sp.wait_ge(ln_done, LN_OUT + t + 1)
                sp.dma_start(out[0, t * P:(t + 1) * P, :], rows[:, t, :]).then_inc(stored, 16)
            sp.wait_ge(stored, 16 * NT)

        @block.gpsimd
        def _(pool):
            pool.memset(ident[:, :], 0.0).then_inc(const_step, 1)
            pool.memset(causal[:, :], 1.0).then_inc(const_step, 1)
            pool.memset(ones[:, :], 1.0).then_inc(const_ready, 1)
            pool.memset(avg[:, :], 1.0 / D).then_inc(const_ready, 1)
            pool.memset(zero[:, :], 0.0).then_inc(const_ready, 1)
            pool.memset(eps[:, :], EPS).then_inc(const_ready, 1)
            pool.iota(iota16[:, :], [[1, TOPK]], base=0, channel_multiplier=0,
                      allow_small_or_imprecise_dtypes=True).then_inc(const_ready, 1)
            pool.wait_ge(const_step, 2)
            pool.affine_select(out=ident[:, :], in_=ident[:, :], compare_op=ALU.not_equal, fill=1.0, base=0,
                               pattern=[[-1, P]], channel_multiplier=1).then_inc(const_ready, 1)
            pool.affine_select(out=causal[:, :], in_=causal[:, :], compare_op=ALU.is_ge, fill=0.0, base=0,
                               pattern=[[1, P]], channel_multiplier=-1).then_inc(const_ready, 1)

            def low_parts(s, mine=range(UNITS)):
                for q in mine:
                    pool.wait_ge(hi_ready, s * UNITS + (q + 1))
                    pool.tensor_tensor(wlo[q][:, :, :], raw[q][:, :, :], f32(whi[q][:, :, :]), ALU.subtract).then_inc(
                        lo_ready, 1)

            with pool.Fori(0, S_END) as s:
                low_parts(s)

            def gather(dst, table, index, landed):
                pool.indirect_dma_start(dst, None, table, bass.IndirectOffsetOnAxis(ap=index, axis=0)).then_inc(landed, 16)

            def step(s, par, u, v_):
                pool.wait_ge(ix_staged, s + 1)
                for k in range(TOPK):
                    b = k % UB
                    if u:
                        if not (isinstance(s, int) and s * TOPK + k < UB):
                            pool.wait_ge(u_used, s * TOPK + (k - UB + 1))
                            settle(pool)
                        gather(ubuf[b], peer_u, ixu[:, par, k:k + 1], u_loaded[b])
                    if v_:
                        if not (isinstance(s, int) and (s - 1) * TOPK + k < UB):
                            pool.wait_ge(v_used, s * TOPK + (k - UB + 1 - TOPK))
                            settle(pool)
                        gather(vbuf[b], peer_v, ixv[:, 1 - par, k:k + 1], v_loaded[b])

            run_steps(pool, step)

        @block.tensor
        def _(pe):
            def turn(i, sources, waits=()):
                for s, n in waits:
                    pe.wait_ge(s, n)
                if i >= 4:
                    pe.wait_ge(turned_hi, i - 3)
                    if i - 4 in WITH_LO:
                        pe.wait_ge(turned_lo, WITH_LO.index(i - 4) + 1)
                at = 0
                for src in sources:
                    n = src.shape[0]
                    last = pe.transpose(ps[0:src.shape[1], 4 + i % 4, at:at + n], src, ident[0:n, 0:n])
                    at += n
                last.then_inc(turned, 1)

            def product(s, bank0, act, tiles=2):
                for q in range(UNITS):
                    pe.wait_ge(lo_ready, s * UNITS + (q + 1))
                    for u in range(tiles):
                        for kk in range(KU):
                            k = q * KU + kk
                            hi, lo = act(k)
                            o = ps[:, bank0 + u, 0:hi.shape[-1]]
                            w_hi = whi[q][:, kk, u * P:(u + 1) * P]
                            w_lo = wlo[q][:, kk, u * P:(u + 1) * P]
                            pe.matmul(o, w_hi, hi, start=(k == 0), stop=False)
                            pe.matmul(o, w_hi, lo, start=False, stop=False)
                            last = pe.matmul(o, w_lo, hi, start=False, stop=(k == KT - 1))
                    last.then_inc(unit_done, 1)

            def split(tensor, a, b):
                return lambda k: (tensor[:, 0, k, a:b], tensor[:, 1, k, a:b])

            h_all, h_seq = split(h_split, 0, L), split(h_split, META, L)

            turn(0, [prow], [(const_ready, 7), (param_loaded, 16 * 14)])
            turn(1, [convrow])
            turn(2, [cfrow[:, a, :] for a in range(4)])
            for t in range(NT):
                for q in range(4):
                    turn(TURN_X + 4 * t + q, [rows[:, t, (4 * q + r) * P:(4 * q + r + 1) * P] for r in range(4)],
                         [(ln_done, LN_X + t + 1)])
            turn(TURN_META, [meta_t[:, k * P:(k + 1) * P] for k in range(KT)], [(ln_done, LN_META + 1)])
            pe.wait_ge(turned_hi, TURN_META + 1)
            pe.wait_ge(turned_lo, 4 * NT + 1)

            product(0, 0, h_all, tiles=1)
            pe.wait_ge(tabs_ready, 1)
            dtv, ncs, wst = hsm[4], hsm[5], hsm[6]
            for n, (tab, c) in enumerate(((dtv, 1), (dtv, 2), (ncs, 1), (ncs, 2), (wst, 1), (wst, 0))):
                a, b = CHUNKS[c]
                pe.transpose(T1[0:b - a, n * HEADS:(n + 1) * HEADS], tab[:, a:b], ident[0:HEADS, 0:HEADS])
            pe.matmul(T1[:, 6 * HEADS:7 * HEADS], hsm[7][:, 0:P], ident[0:HEADS, 0:HEADS],
                      start=True, stop=True).then_inc(tabs_done, 1)
            pe.wait_ge(tabs_copied, 2)

            with pe.Fori(0, GROUPS) as g:
                pe.wait_ge(proj_copied, g * 5 + 3)
                product(g * 5 + S_GROUP, 0, h_all)
                pe.wait_ge(proj_copied, g * 5 + 5)
                product(g * 5 + (S_GROUP + 1), 2, h_all)
                pe.wait_ge(r_ready, g + 1)
                pe.matmul(T0, ones[0:HEADS, :], rmask[:, 0, :, :].rearrange("p a b -> p (a b)"),
                          start=True, stop=True)
                pe.matmul(T1, ones[0:HEADS, :], rmask[:, 1, :, :].rearrange("p a b -> p (a b)"),
                          start=True, stop=True).then_inc(csb_done, 1)
                pe.wait_ge(proj_copied, g * 5 + 6)
                product(g * 5 + (S_GROUP + 2), 0, h_all)
                pe.wait_ge(xg_ready, g * 4 + 4)
                for c in range(2):
                    for u in range(2):
                        a, b = CHUNKS[1 + c]
                        pe.transpose(T2[:, (2 * c + u) * P:(2 * c + u + 1) * P], xg[:, u, a:b], ident[:, :])
                pe.transpose(T3[:, 0:P], xg[:, 2, META:META + P], ident[:, :])
                pe.transpose(T3[0:META, P:2 * P], xg[:, 2, 0:META], ident[:, :])
                for u in range(2):
                    last = pe.transpose(T3[0:META, (2 + u) * P:(3 + u) * P], xg[:, u, 0:META], ident[:, :])
                last.then_inc(xpose_done, 1)
                pe.wait_ge(seg_ready, g + 1)
                pe.wait_ge(ecs_ready, g + 1)
                for c in range(2):
                    a, b = CHUNKS[1 + c]
                    last = pe.matmul(T0[:, c * P:(c + 1) * P], xg[:, 2, a:b], xg[:, 3, a:b], start=True, stop=True)
                last.then_inc(score_done, 1)
                pe.wait_ge(proj_copied, g * 5 + 7)
                product(g * 5 + (S_GROUP + 3), 2, h_seq)
                pe.wait_ge(xtm_ready, g + 1)
                pe.wait_ge(btm_ready, g * 2 + 2)
                pe.matmul(T3[:, 0:HPG * HD], btm[0:META, 1, :], xw[0:META, 1, :], start=True, stop=True)
                pe.matmul(T3[:, HPG * HD:2 * HPG * HD], btm[:, 0, :], xw[:, 0, :],
                          start=True, stop=True).then_inc(state_done, 1)
                pe.wait_ge(mt_ready, g + 1)
                pe.wait_ge(s_ready, g + 1)
                for u in range(2):
                    for c in range(2):
                        for r in range(2):
                            hh = 2 * u + r
                            o = ps[HD * r:HD * r + HD, 5, (2 * u + c) * P:(2 * u + c + 1) * P]
                            pe.matmul(o, xdt[:, c, hh * HD:(hh + 1) * HD], seg[:, c, hh, :], start=True, stop=False)
                            last = pe.matmul(o, state[:, c, hh * HD:(hh + 1) * HD], ecs[:, c, hh, :],
                                             start=False, stop=True)
                last.then_inc(y_done, 1)
                pe.wait_ge(proj_copied, g * 5 + 9)
                product(g * 5 + (S_GROUP + 4), 2, h_all)
                pe.wait_ge(sq_ready, g + 1)
                for u in range(2):
                    last = pe.matmul(T2[:, 0:SEQ], ones[:, :], v2[:, u, :], start=(u == 0), stop=(u == 1))
                last.then_inc(nsum_done, 1)

            def mix_pair(i, base, s0, act):
                pe.wait_ge(sg_ready, i + (base + 1))
                product(i * 2 + s0, 0, h_seq)
                pe.wait_ge(mix_ready, i + (base + 1))
                product(i * 2 + (s0 + 1), 2, act)

            y_act, c_act = split(ym_split, 0, SEQ), split(c_split, 0, SEQ)
            pe.wait_ge(proj_copied, 5 * GROUPS + 5)
            pe.wait_ge(ynorm_ready, GROUPS)
            with pe.Fori(0, 2) as i:
                mix_pair(i, 0, S_SSD, y_act)
            pe.wait_ge(cf_ready, GROUPS + 1)
            for k in range(KT):
                last = pe.matmul(T0[:, 0:SEQ], avg[:, :], cT[:, k, :], start=(k == 0), stop=(k == KT - 1))
            last.then_inc(mean_done, 1)
            mix_pair(2, 0, S_SSD, y_act)
            pe.wait_ge(csq_ready, 1)
            for k in range(KT):
                last = pe.matmul(T1[:, 0:SEQ], avg[:, :], csq[:, k, :], start=(k == 0), stop=(k == KT - 1))
            last.then_inc(cvar_done, 1)
            with pe.Fori(3, NS) as i:
                mix_pair(i, 0, S_SSD, y_act)
            pe.wait_ge(c_ready, 4)
            with pe.Fori(0, NS) as i:
                mix_pair(i, NS, S_CF, c_act)

            m_act = split(ym_split, 0, SEQ)
            pe.nop().then_inc(res_turned, 2)
            pe.wait_ge(mix_ready, 2 * NS + 1)
            pe.wait_ge(m_ready, NS)
            with pe.Fori(0, NS // 2) as i:
                for j in range(2):
                    pe.wait_ge(res_ready, i * 2 + (j + 1))
                    product(i * 2 + (S_WO + j), 2 * j, m_act)
                for j in range(2):
                    pe.wait_ge(res_ready, i * 2 + (j + 3))
                    pe.wait_ge(res_copied, i * 2 + (j + 1))
                    for t in range(NT):
                        for u in range(2):
                            last = pe.transpose(ps[:, 4 + j, t * SW + u * P:t * SW + (u + 1) * P],
                                                res[j][:, u, t * P:(t + 1) * P], ident[:, :])
                    last.then_inc(res_turned, 1)
            pe.wait_ge(res_copied, NS + 2)
            for q in range(4):
                turn(TURN_KEYS + q, [keyrow[:, 4 * q + r, :] for r in range(4)], [(keys_loaded, 16)])
            for t in range(NT):
                for q in range(4):
                    turn(TURN_H1 + 4 * t + q, [rows[:, t, (4 * q + r) * P:(4 * q + r + 1) * P] for r in range(4)],
                         [(ln_done, LN_H1 + t + 1)])
            pe.wait_ge(turned_hi, TURN_END)
            pe.wait_ge(turned_lo, len(WITH_LO))

            def scores(i, j):
                pe.wait_ge(q_copied, i * 4 + (j + 3))
                pe.wait_ge(sc_copied, i * 4 + (j + 1))
                for t in range(NT):
                    for s in range(2):
                        last = pe.matmul(ps[:, 4 + j % 2, (2 * t + s) * NK:(2 * t + s + 1) * NK],
                                         qts[j % 2][:, s, t * P:(t + 1) * P],
                                         keysT[:, ds(i * 4 + (s * PH + j), 1), :].rearrange("p a b -> p (a b)"),
                                         start=True, stop=True)
                last.then_inc(sc_done, 1)

            h1_act = split(h_split, 0, SEQ)
            pe.nop().then_inc(sc_done, 2)
            with pe.Fori(0, 2) as i:
                for j in range(4):
                    pe.wait_ge(q_copied, i * 4 + (j + 1))
                    product(i * 4 + (S_WQ + j), 2 * (j % 2), h1_act)
                    if j:
                        scores(i, j - 1)
                scores(i, 3)

            def clear(t):
                for b in range(4):
                    pe.matmul(ps[:, 4 * t + b, :], zero[:, :], ones[:, 0:1].to_broadcast([P, 512]),
                              start=True, stop=False, skip_group_check=True)

            pe.wait_ge(sc_copied, 2 + PH)
            clear(0)
            clear(1)

            def step(s, par, u, v_):
                if not v_:
                    return
                t = tile_of_v[0]
                for k in range(TOPK):
                    b = k % UB
                    pe.wait_ge(v_loaded[b], (s - 1) * (TOPK // UB * 16) + (k // UB + 1) * 16)
                    pe.wait_ge(diag_ready, (s - 1) * TOPK + (k + 1))
                    for c in range(4):
                        last = pe.matmul(ps[:, 4 * t + c, :], diag[b], vbuf[b][:, c * 512:(c + 1) * 512],
                                         start=False, stop=False, skip_group_check=True)
                    last.then_inc(v_used, 1)

            tile_of_v = [0]
            run_steps(pe, step, lambda: tile_of_v.__setitem__(0, 1))

        @block.scalar
        def _(act):
            act.nop().then_inc(proj_copied, 5)
            act.nop().then_inc(sg_ready, 1)
            act.nop().then_inc(res_copied, 2)
            act.nop().then_inc(q_copied, 2)
            act.nop().then_inc(sc_copied, 2)

            def high_parts(s, units=range(UNITS), bc=None):
                for q in units:
                    act.wait_ge(raw_loaded[q], s * 16 + 16)
                    if bc is not None:
                        act.wait_ge(c_cols_loaded[q], bc * 16 + 16)
                    if not (isinstance(s, int) and s == 0):
                        act.wait_ge(unit_done, s * UNITS + (q + 1 - UNITS))
                    act.activation(whi[q][:, :, :], raw[q][:, :, :], ACT.Copy).then_inc(hi_ready, 1)

            def ln_sd(n, p=P):
                act.wait_ge(var_ready, n + 1)
                act.activation(sd[0:p, 0:1], mv[0:p, 1:2], ACT.Sqrt, bias=eps[0:p, :]).then_inc(sd_done, 1)

            def turned_copy(i, dst, src):
                act.wait_ge(turned, i + 1)
                act.activation(dst, src, ACT.Copy).then_inc(turned_hi, 1)

            act.wait_ge(const_ready, 7)
            ln_sd(LN_X)
            turned_copy(0, pcol[:, :], bank(0)[:, 0:96])
            turned_copy(1, convw[:, :, :].rearrange("p a b -> p (a b)"), bank(1)[:, 0:128])
            turned_copy(2, cfw[:, :], bank(2)[:, 0:496])
            ln_sd(LN_X + 1)
            for t in range(NT):
                if t == 1:
                    ln_sd(LN_META, META)
                    high_parts(0)
                for q in range(4):
                    i = TURN_X + 4 * t + q
                    turned_copy(i, h_split[:, 0, 4 * q:4 * q + 4, META + t * P:META + (t + 1) * P],
                                bank(i).rearrange("p (a b) -> p a b", a=4))
            turned_copy(TURN_META, h_split[:, 0, :, 0:META],
                        bank(TURN_META)[:, 0:KT * META].rearrange("p (a b) -> p a b", a=KT))

            act.wait_ge(param_loaded, 16 * 14)
            act.activation(head[:, 1:2], head[:, 1:2], ACT.Exp).then_inc(alog_ready, 1)
            high_parts(S_GROUP)
            act.wait_ge(x1_ready, 1)
            act.activation(hsm[2], hsm[1], ACT.Exp, scale=-1.0).then_inc(ex_ready, 1)
            act.wait_ge(rel_ready, 1)
            act.activation(hsm[6], hsm[8], ACT.Exp, scale=-1.0).then_inc(w_ready, 1)
            a, b = CHUNKS[1]
            act.activation(head[:, 2:3], cs[:, b - 1:b], ACT.Exp).then_inc(ecl_ready, 1)
            act.wait_ge(tabs_done, 1)
            act.activation(tm[:, 0:5, :], T1[:, 0:5 * HEADS].rearrange("p (a b) -> p a b", a=5), ACT.Copy)
            act.activation(tm[0:META, 5, :], T1[0:META, 5 * HEADS:6 * HEADS], ACT.Copy).then_inc(tabs_copied, 1)
            act.activation(edec[:, :], T1[:, 6 * HEADS:7 * HEADS], ACT.Copy).then_inc(tabs_copied, 1)

            with act.Fori(0, GROUPS) as g:
                s = g * 5 + S_GROUP
                high_parts(s + 1, bc=g)
                slab_done(act, s)
                act.wait_ge(conv_ready, g * 4 + 4)
                act.activation(xin[:, 0:2, :], ps[:, 0:2, 0:L], ACT.Copy).then_inc(proj_copied, 1)
                high_parts(s + 2)
                slab_done(act, s + 1)
                act.activation(xin[:, 2:4, :], ps[:, 2:4, 0:L], ACT.Copy).then_inc(proj_copied, 1)
                high_parts(s + 3, (0, 1))
                for i, tile in enumerate((g * 2, g * 2 + 1, g + 16, g + 24)):
                    act.wait_ge(conv_ready, g * 4 + (i + 5))
                    act.activation(xg[:, i, :], acc[:, i, :], ACT.Silu, bias=pcol[:, ds(tile, 1)]).then_inc(xg_ready, 1)
                high_parts(s + 3, (2,))
                act.wait_ge(seg_ready, g + 1)
                act.activation(ecs[:, :, :, :].rearrange("p c h i -> p c (h i)"), ps[:, 4:6, :], ACT.Exp).then_inc(
                    ecs_ready, 1)
                act.activation(seg[:, :, :, :], seg[:, :, :, :], ACT.Exp).then_inc(exp_ready, 1)
                high_parts(s + 3, (3,))
                slab_done(act, s + 2)
                act.wait_ge(cf_ready, g + 1)
                act.activation(vraw[:, :, :], ps[:, 0:2, 0:L], ACT.Copy).then_inc(proj_copied, 1)
                high_parts(s + 4, (0, 1))
                act.wait_ge(xtm_ready, g + 1)
                act.activation(btm[:, 0, :], T3[:, 0:P], ACT.Copy).then_inc(btm_ready, 1)
                act.activation(btm[0:META, 1, :], T3[0:META, P:2 * P], ACT.Copy).then_inc(btm_ready, 1)
                high_parts(s + 4, (2, 3))
                slab_done(act, s + 3)
                act.activation(zs[:, :, :], ps[:, 2:4, 0:SEQ], ACT.Silu).then_inc(proj_copied, 1)
                high_parts(s + 5, (0, 1))
                act.wait_ge(v_ready, g + 1)
                act.activation(v2[:, :, :], v[:, :, :], ACT.Square).then_inc(sq_ready, 1)
                high_parts(s + 5, (2, 3))
                slab_done(act, s + 4)
                act.activation(gsig[:, :, :], ps[:, 2:4, 0:L], ACT.Sigmoid).then_inc(proj_copied, 1)
                act.wait_ge(nsum_done, g + 1)
                act.activation(rinv[:, 0, :], T2[:, 0:SEQ], ACT.Sqrt, bias=eps[:, :], scale=1.0 / SW).then_inc(nsd_ready, 1)

            def sig_pair(i, base, s0, middle=lambda: None):
                s = i * 2 + s0
                high_parts(s + 1)
                slab_done(act, s)
                act.wait_ge(mix_ready, i + (base + 1))
                act.activation(v[:, :, :], ps[:, 0:2, 0:SEQ], ACT.Sigmoid).then_inc(sg_ready, 1)
                high_parts(s + 2, (0, 1))
                middle()
                high_parts(s + 2, (2, 3))

            with act.Fori(0, 2) as i:
                sig_pair(i, 0, S_SSD)

            def square():
                act.wait_ge(cen_ready, 1)
                act.activation(csq, cT, ACT.Square).then_inc(csq_ready, 1)

            sig_pair(2, 0, S_SSD, square)

            def cf_sd():
                act.wait_ge(cvar_done, 1)
                act.activation(rinv[:, 0, :], T1[:, 0:SEQ], ACT.Sqrt, bias=eps[:, :]).then_inc(csd_ready, 1)

            sig_pair(3, 0, S_SSD, cf_sd)
            with act.Fori(4, NS) as i:
                def silu():
                    act.wait_ge(cn_ready, 1)
                    for r in range(4):
                        k = i * 4 + (r - 16)
                        c = cT[:, ds(k, 1), :]
                        act.activation(c, c, ACT.Silu, bias=pcol[:, ds(k + 80, 1)],
                                       scale=pcol[:, ds(k + 64, 1)]).then_inc(silu_ready, 1)
                sig_pair(i, 0, S_SSD, silu)
            with act.Fori(0, NS) as i:
                sig_pair(i, NS, S_CF)

            with act.Fori(0, NS // 2) as i:
                high_parts(i * 2 + (S_WO + 1))
                high_parts(i * 2 + (S_WO + 2), (0, 1))
                for j in range(2):
                    act.wait_ge(res_turned, i * 2 + (j + 3))
                    act.activation(rows[:, :, ds(i * 2 * SW + j * SW, SW)],
                                   ps[:, 4 + j, :].rearrange("p (t n) -> p t n", t=NT), ACT.Copy).then_inc(res_copied, 1)
                    high_parts(i * 2 + (S_WO + 2), (2 + j,))

            for q in range(4):
                i = TURN_KEYS + q
                turned_copy(i, keysT[:, 4 * q:4 * q + 4, :], bank(i).rearrange("p (a b) -> p a b", a=4))
            for t in range(NT):
                ln_sd(LN_H1 + t)
            for t in range(NT):
                for q in range(4):
                    i = TURN_H1 + 4 * t + q
                    turned_copy(i, h_split[:, 0, 4 * q:4 * q + 4, t * P:(t + 1) * P],
                                bank(i).rearrange("p (a b) -> p a b", a=4))

            def sc_copy(i, j):
                act.wait_ge(sc_done, i * 4 + (j + 3))
                act.wait_ge(topk_done, i * 4 + (j + 1))
                act.activation(scs[j % 2], ps[:, 4 + j % 2, :].rearrange("p (a b) -> p a b", a=4), ACT.Copy).then_inc(
                    sc_copied, 1)

            def heads4(i, last=False):
                for j in range(4):
                    if not (last and j == 3):
                        high_parts(i * 4 + (S_WQ + j + 1))
                    slab_done(act, i * 4 + (S_WQ + j))
                    act.wait_ge(sc_done, i * 4 + (j + 1))
                    act.activation(qts[j % 2][:, :, :], ps[:, 2 * (j % 2):2 * (j % 2) + 2, 0:SEQ], ACT.Copy).then_inc(
                        q_copied, 1)
                    if j:
                        sc_copy(i, j - 1)
                sc_copy(i, 3)

            heads4(0)
            heads4(1, last=True)
            act.wait_ge(gexp_in, 1)
            act.activation(gates[:, :, :], gates[:, :, :], ACT.Exp).then_inc(gexp_done, 1)

            def step(s, par, u, v_):
                if not v_:
                    return
                act.wait_ge(u_used, s * TOPK)
                act.activation(gel[:, 1 - par, :], dots[:, 1 - par, :], ACT.Gelu).then_inc(gelu_ready, 1)
                act.wait_ge(wgt_ready, s)
                for k in range(TOPK):
                    if not (isinstance(s, int) and (s - 1) * TOPK + k < 4):
                        act.wait_ge(v_used, s * TOPK + (k - 3 - TOPK))
                    act.activation(diag[k % 4], ident[:, :], ACT.Copy, scale=wgt[:, 1 - par, k:k + 1]).then_inc(
                        diag_ready, 1)

            def tail(t):
                ln_sd(LN_OUT + t)

            run_steps(act, step, lambda: tail(0))
            tail(1)

        @block.vector
        def _(dve):
            dve.nop().then_inc(conv_ready, 4)
            dve.nop().then_inc(cf_ready, 1)
            dve.nop().then_inc(mix_ready, 1)
            dve.nop().then_inc(res_ready, 2)
            dve.nop().then_inc(topk_done, 2)
            count = [0]

            def done(ins):
                ins.then_inc(vec_step, 1)
                count[0] += 1

            def then():
                dve.wait_ge(vec_step, count[0])

            def layer_norm(n, rows_, p=P):
                for q in range(4):
                    last = dve.bn_stats(stats[0:p, q, :], rows_[:, q * 512:(q + 1) * 512])
                done(last)
                then()
                dve.bn_aggr(mv[0:p, :], stats[0:p, :, :].rearrange("p a b -> p (a b)")).then_inc(var_ready, 1)
                dve.wait_ge(var_ready, n + 1)
                dve.wait_ge(sd_done, n + 1)
                done(dve.reciprocal(sd[0:p, 1:2], sd[0:p, 0:1]))
                then()
                done(dve.tensor_scalar(rows_, rows_, mv[0:p, 0:1], sd[0:p, 1:2], ALU.subtract, ALU.mult))
                then()
                done(dve.tensor_tensor(rows_, rows_, gain[0:p, 0, :], ALU.mult))
                then()
                dve.tensor_tensor(rows_, rows_, gain[0:p, 1, :], ALU.add).then_inc(ln_done, 1)

            def turned_low(i, q, a, b):
                dve.wait_ge(turned_hi, i + 1)
                dve.tensor_tensor(h_split[:, 1, 4 * q:4 * q + 4, a:b], bank(i).rearrange("p (a b) -> p a b", a=4),
                                  f32(h_split[:, 0, 4 * q:4 * q + 4, a:b]), ALU.subtract).then_inc(turned_lo, 1)

            dve.wait_ge(gain_loaded, 32)
            for t in range(NT):
                dve.wait_ge(x_loaded[t], 16)
                layer_norm(LN_X + t, rows[:, t, :])
            for t in range(NT):
                if t == 1:
                    dve.wait_ge(meta_loaded, 16)
                    layer_norm(LN_META, meta_t, META)
                for q in range(4):
                    turned_low(TURN_X + 4 * t + q, q, META + t * P, META + (t + 1) * P)
            dve.wait_ge(turned_hi, TURN_META + 1)
            dve.tensor_tensor(h_split[:, 1, :, 0:META], bank(TURN_META)[:, 0:KT * META].rearrange(
                "p (a b) -> p a b", a=KT), f32(h_split[:, 0, :, 0:META]), ALU.subtract).then_inc(turned_lo, 1)

            xb, xa, u_, s_, dtv, ncs, wst, ecl, rel, q_, p_ = hsm[0:11]
            dve.wait_ge(param_loaded, 16 * 14)
            dve.wait_ge(const_ready, 7)
            slab_done(dve, 0)
            done(dve.tensor_scalar(xb, ps[0:HEADS, 0, 0:L], head[:, 0:1], None, ALU.add))
            then()
            dve.scalar_tensor_tensor(xa, xb, -1.0, xb, ALU.mult, ALU.max).then_inc(x1_ready, 1)
            dve.wait_ge(ex_ready, 1)
            done(dve.tensor_scalar(s_, u_, 2.0, None, ALU.add))
            then()
            done(dve.reciprocal(q_, s_))
            then()
            done(dve.tensor_tensor(s_, u_, q_, ALU.mult))
            then()
            done(dve.tensor_tensor(q_, s_, s_, ALU.mult))
            then()
            done(dve.tensor_scalar(p_, q_, 1.0 / 15, None, ALU.mult))
            then()
            for n in (13, 11, 9, 7, 5, 3):
                done(dve.scalar_tensor_tensor(p_, p_, 1.0 / n, q_, ALU.add, ALU.mult))
                then()
            done(dve.scalar_tensor_tensor(p_, p_, 1.0, s_, ALU.add, ALU.mult))
            done(dve.tensor_scalar(xb, xb, 0.0, None, ALU.max))
            then()
            done(dve.scalar_tensor_tensor(dtv, p_, 2.0, xb, ALU.mult, ALU.add))
            then()
            dve.wait_ge(alog_ready, 1)
            done(dve.tensor_scalar(q_, dtv, head[:, 1:2], -1.0, ALU.mult, ALU.mult))
            then()
            for a, b in CHUNKS:
                done(dve.tensor_tensor_scan(cs[:, a:b], ones[0:HEADS, 0:b - a], q_[:, a:b], 0.0, ALU.mult, ALU.add))
            then()
            done(dve.tensor_scalar(ncs, cs[:, :], -1.0, None, ALU.mult))
            for a, b in CHUNKS[0:1]:
                done(dve.tensor_scalar(rel[:, a:b], cs[:, a:b], cs[:, b - 1:b], None, ALU.subtract))
            a, b = CHUNKS[2]
            done(dve.tensor_scalar(rel[:, a:b], cs[:, a:b], cs[:, b - 1:b], None, ALU.subtract))
            a, b = CHUNKS[1]
            dve.tensor_scalar(rel[:, a:b], cs[:, a:b], cs[:, b - 1:b], None, ALU.subtract).then_inc(rel_ready, 1)
            dve.wait_ge(w_ready, 1)
            done(dve.tensor_tensor(wst, wst, dtv, ALU.mult))
            dve.wait_ge(ecl_ready, 1)
            dve.tensor_scalar(ecl[:, 0:P], ones[0:HEADS, :], head[:, 2:3], None, ALU.mult).then_inc(tabs_ready, 1)

            PER = 4 * (KC - 1) + 1 + 2 + 2 + 1 + 2 + 1 + 2 * (KF - 1) + 1
            start = count[0]
            with dve.Fori(0, GROUPS) as g:
                count[0] = start
                turn_ = g * PER

                def hold(back=0):
                    dve.wait_ge(vec_step, turn_ + (count[0] - back))

                for c in range(2):
                    a, b = CHUNKS[1 + c]
                    last = dve.tensor_tensor(rmask[:, c, :, :],
                                             ident[0:HEADS, ds(g * HPG, HPG)].unsqueeze(2).to_broadcast([HEADS, HPG, P]),
                                             cs[:, a:b].unsqueeze(1).to_broadcast([HEADS, HPG, P]), ALU.mult)
                last.then_inc(r_ready, 1)
                tiles = (g * 2, g * 2 + 1, g + 16, g + 24)
                for half in range(2):
                    for k in range(KC - 1, -1, -1):
                        for i in (2 * half, 2 * half + 1):
                            w = convw[:, k, ds(tiles[i], 1)]
                            m = KC - 1 - k
                            if k == KC - 1:
                                if i % 2 == 0:
                                    dve.wait_ge(proj_copied, g * 5 + (6 + half))
                                done(dve.tensor_scalar(acc[:, i, :], xin[:, i, :], w, None, ALU.mult))
                            else:
                                hold(1 if k else 1 - i % 2)
                                ins = dve.scalar_tensor_tensor(acc[:, i, m:L], xin[:, i, 0:L - m], w, acc[:, i, m:L],
                                                               ALU.mult, ALU.add)
                                if k:
                                    done(ins)
                                else:
                                    ins.then_inc(conv_ready, 1)
                dve.wait_ge(csb_done, g + 1)
                for c in range(2):
                    for hh in range(HPG):
                        last = dve.tensor_scalar(seg[:, c, hh, :], ps[:, 4 + c, hh * P:(hh + 1) * P],
                                                 tm[:, 2 + c, ds(g * HPG + hh, 1)], 0.0, ALU.add, ALU.min)
                last.then_inc(seg_ready, 1)
                dve.wait_ge(xpose_done, g + 1)

                def per_head(table, p=P):
                    return tm[0:p, table, ds(g * HPG, HPG)].unsqueeze(2).to_broadcast([p, HPG, HD])

                def heads(ap):
                    return ap.rearrange("p (h d) -> p h d", d=HD)

                for c in range(2):
                    dve.tensor_tensor(heads(xdt[:, c, :]), heads(T2[:, c * 2 * P:(c + 1) * 2 * P]), per_head(c), ALU.mult)
                dve.tensor_tensor(heads(xw[:, 0, :]), heads(T2[:, 0:2 * P]), per_head(4), ALU.mult)
                dve.tensor_tensor(heads(xw[0:META, 1, :]), heads(T3[0:META, 2 * P:4 * P]), per_head(5, META),
                                  ALU.mult).then_inc(xtm_ready, 1)
                dve.wait_ge(score_done, g + 1)
                done(dve.tensor_tensor(scm[:, :, :], T0[:, 0:2 * P].rearrange("p (c i) -> p c i", c=2),
                                       causal[:, :].unsqueeze(1).to_broadcast([P, 2, P]), ALU.mult))
                hold()
                dve.wait_ge(exp_ready, g + 1)
                for c in range(2):
                    dve.tensor_tensor(seg[:, c, :, :], seg[:, c, :, :],
                                      scm[:, c, :].unsqueeze(1).to_broadcast([P, HPG, P]), ALU.mult)
                dve.wait_ge(ecs_ready, g + 1)
                for c in range(2):
                    a, b = CHUNKS[1 + c]
                    last = dve.tensor_tensor(ecs[:, c, :, :], ecs[:, c, :, :],
                                             xg[:, 3, a:b].unsqueeze(1).to_broadcast([P, HPG, P]), ALU.mult)
                last.then_inc(mt_ready, 1)
                dve.wait_ge(state_done, g + 1)
                done(dve.tensor_copy(state[:, 0, :], T3[:, 0:HPG * HD]))
                hold()
                done(dve.tensor_tensor(heads(state[:, 1, :]), heads(state[:, 0, :]),
                                       edec[:, ds(g * HPG, HPG)].unsqueeze(2).to_broadcast([P, HPG, HD]), ALU.mult))
                hold()
                dve.tensor_tensor(state[:, 1, :], state[:, 1, :], T3[:, HPG * HD:2 * HPG * HD], ALU.add).then_inc(
                    s_ready, 1)
                dve.wait_ge(y_done, g + 1)
                for u in range(2):
                    done(dve.scalar_tensor_tensor(v[:, u, :], xg[:, u, META:L], dcol[:, ds(g * 2 + u, 1)],
                                                  T1[:, u * SEQ:(u + 1) * SEQ], ALU.mult, ALU.add))
                hold()
                dve.wait_ge(proj_copied, g * 5 + 9)
                dve.tensor_tensor(v[:, :, :], v[:, :, :], zs[:, :, :], ALU.mult).then_inc(v_ready, 1)
                dve.wait_ge(nsd_ready, g + 1)
                done(dve.reciprocal(rinv[:, 1, :], rinv[:, 0, :]))
                hold()
                for u in range(2):
                    last = dve.scalar_tensor_tensor(v[:, u, :], v[:, u, :], pcol[:, ds(g * 2 + (32 + u), 1)],
                                                    rinv[:, 1, :], ALU.mult, ALU.mult)
                done(last)
                hold()
                done(dve.tensor_copy(ym_split[:, 0, ds(g * 2, 2), :], v[:, :, :]))
                hold()
                dve.tensor_tensor(ym_split[:, 1, ds(g * 2, 2), :], v[:, :, :], f32(ym_split[:, 0, ds(g * 2, 2), :]),
                                  ALU.subtract).then_inc(ynorm_ready, 1)
                dve.wait_ge(proj_copied, g * 5 + 10)
                done(dve.tensor_tensor(gsig[:, :, :], gsig[:, :, :], vraw[:, :, :], ALU.mult))
                hold()
                for k in range(KF - 1, -1, -1):
                    back = KF - 1 - k
                    t0 = max(META, back)
                    for u in range(2):
                        w = cfw[:, ds(g * 2 + (k * KT + u), 1)]
                        if back == 0:
                            ct = cT[:, ds(g * 2 + u, 1), :].rearrange("p a b -> p (a b)")
                            ins = dve.tensor_scalar(ct, gsig[:, u, META:L], w, pcol[:, ds(g * 2 + (48 + u), 1)],
                                                    ALU.mult, ALU.add)
                        else:
                            hold(1)
                            o = cT[:, ds(g * 2 + u, 1), t0 - META:SEQ].rearrange("p a b -> p (a b)")
                            ins = dve.scalar_tensor_tensor(o, gsig[:, u, t0 - back:L - back], w, o, ALU.mult, ALU.add)
                        if k or u == 0:
                            done(ins)
                        else:
                            ins.then_inc(cf_ready, 1)
                body_steps = count[0] - start
            assert PER == body_steps, (PER, body_steps)
            count[0] = start + GROUPS * PER

            branch = ps[:, 2:4, 0:SEQ]

            def mix_first(i):
                dve.wait_ge(sg_ready, i + 2)
                slab_done(dve, i * 2 + (S_SSD + 1))
                dve.tensor_tensor(mix1[:, ds(i * 2, 2), :], v[:, :, :], branch, ALU.mult).then_inc(mix_ready, 1)

            with dve.Fori(0, 2) as i:
                mix_first(i)
            dve.wait_ge(mean_done, 1)
            dve.tensor_tensor(cT, cT, T0[:, 0:SEQ].unsqueeze(1).to_broadcast([P, KT, SEQ]),
                              ALU.subtract).then_inc(cen_ready, 1)
            mix_first(2)
            dve.wait_ge(csd_ready, 1)
            dve.wait_ge(csq_ready, 1)
            done(dve.reciprocal(rinv[:, 1, :], rinv[:, 0, :]))
            then()
            dve.tensor_tensor(cT, cT, rinv[:, 1, :].unsqueeze(1).to_broadcast([P, KT, SEQ]),
                              ALU.mult).then_inc(cn_ready, 1)
            mix_first(3)
            start = count[0]
            with dve.Fori(4, NS) as i:
                mix_first(i)
                dve.wait_ge(silu_ready, i * 4 - 12)
                tiles = ds(i * 4 - 16, 4)
                done(dve.tensor_copy(c_split[:, 0, tiles, :], cT[:, tiles, :]))
                dve.wait_ge(vec_step, i + (start - 3))
                dve.tensor_tensor(c_split[:, 1, tiles, :], cT[:, tiles, :], f32(c_split[:, 0, tiles, :]),
                                  ALU.subtract).then_inc(c_ready, 1)
            count[0] = start + 4
            start = count[0]
            with dve.Fori(0, NS) as i:
                dve.wait_ge(sg_ready, i + (NS + 2))
                slab_done(dve, i * 2 + (S_CF + 1))
                dve.tensor_tensor(v2[:, :, :], v[:, :, :], branch, ALU.mult).then_inc(mix_ready, 1)
                dve.wait_ge(mix_ready, i + (NS + 2))
                done(dve.tensor_tensor(v2[:, :, :], v2[:, :, :], mix1[:, ds(i * 2, 2), :], ALU.add))
                dve.wait_ge(vec_step, i * 2 + (start + 1))
                done(dve.tensor_copy(ym_split[:, 0, ds(i * 2, 2), :], v2[:, :, :]))
                dve.wait_ge(vec_step, i * 2 + (start + 2))
                dve.tensor_tensor(ym_split[:, 1, ds(i * 2, 2), :], v2[:, :, :], f32(ym_split[:, 0, ds(i * 2, 2), :]),
                                  ALU.subtract).then_inc(m_ready, 1)
                dve.wait_ge(m_ready, i + 1)
            count[0] = start + 2 * NS

            start = count[0]
            with dve.Fori(0, NS // 2) as i:
                for j in range(2):
                    slab_done(dve, i * 2 + (S_WO + j))
                    dve.wait_ge(res_turned, i * 2 + (j + 1))
                    r = res[j]
                    done(dve.scalar_tensor_tensor(r[:, :, :], f32(h_split[:, 0, ds(i * 4 + 2 * j, 2), META:L]), ALPHA,
                                                  ps[:, 2 * j:2 * j + 2, 0:SEQ], ALU.mult, ALU.add))
                    dve.wait_ge(vec_step, i * 2 + (start + j + 1))
                    dve.scalar_tensor_tensor(r[:, :, :], f32(h_split[:, 1, ds(i * 4 + 2 * j, 2), META:L]), ALPHA,
                                             r[:, :, :], ALU.mult, ALU.add).then_inc(res_ready, 1)
            count[0] = start + NS
            dve.wait_ge(res_copied, NS + 2)
            dve.wait_ge(gain_loaded, 64)
            for t in range(NT):
                layer_norm(LN_H1 + t, rows[:, t, :])
            for t in range(NT):
                for q in range(4):
                    turned_low(TURN_H1 + 4 * t + q, q, t * P, (t + 1) * P)

            start4 = count[0]
            with dve.Fori(0, 2) as i:
                count[0] = start4

                def hold():
                    dve.wait_ge(vec_step, i * T4 + count[0])
                    settle(dve)

                for j in range(4):
                    sc = scs[j % 2]
                    dve.wait_ge(sc_copied, i * 4 + (j + 3))
                    settle(dve)
                    for q in range(4):
                        last = dve.max(topv[:, q, 0:8], sc[:, q, :])
                    done(last)
                    hold()
                    for q in range(4):
                        dve.max_index(topi[:, q, 0:8], topv[:, q, 0:8], sc[:, q, :])
                        last = dve.match_replace(left[:, q, :], topv[:, q, 0:8], sc[:, q, :], LOW)
                    done(last)
                    hold()
                    for q in range(4):
                        last = dve.max(topv[:, q, 8:16], left[:, q, :])
                    done(last)
                    hold()
                    for q in range(4):
                        last = dve.max_index(topi[:, q, 8:16], topv[:, q, 8:16], left[:, q, :])
                    done(last)
                    for t in range(NT):
                        last = dve.tensor_tensor(cand[:, t, :].rearrange("p (a b) -> p a b", a=TOPK),
                                                 topv[:, 2 * t, :].unsqueeze(2).to_broadcast([P, TOPK, TOPK]),
                                                 topv[:, 2 * t + 1, :].unsqueeze(1).to_broadcast([P, TOPK, TOPK]),
                                                 ALU.add)
                    done(last)
                    hold()
                    dve.tensor_copy(topif, topi)
                    for t in range(NT):
                        last = dve.max(bestv[:, t, 0:8], cand[:, t, :])
                    done(last)
                    hold()
                    for t in range(NT):
                        dve.max_index(bestj[:, t, 0:8], bestv[:, t, 0:8], cand[:, t, :])
                        last = dve.match_replace(cand2[:, t, :], bestv[:, t, 0:8], cand[:, t, :], LOW)
                    done(last)
                    hold()
                    for t in range(NT):
                        last = dve.max(bestv[:, t, 8:16], cand2[:, t, :])
                    done(last)
                    hold()
                    for t in range(NT):
                        last = dve.max_index(bestj[:, t, 8:16], bestv[:, t, 8:16], cand2[:, t, :])
                        dve.tensor_copy(best[:, ds(i * 4 + (t * PH + j), 1), :].rearrange("p a b -> p (a b)"),
                                        bestv[:, t, :])
                    done(last)
                    hold()
                    dve.tensor_scalar(part[:, 0, :, :], bestj, 4, None, ALU.logical_shift_right)
                    done(dve.tensor_scalar(part[:, 1, :, :], bestj, 15, None, ALU.bitwise_and))
                    hold()
                    done(dve.tensor_copy(partf, part))
                    hold()
                    for s in range(2):
                        keyno = topif.rearrange("p (t s) i -> p s t i", s=2)[:, s, :, :]
                        done(dve.tensor_tensor(hot, partf[:, s, :, :].unsqueeze(3).to_broadcast([P, NT, TOPK, TOPK]),
                                               iota16[:, :].unsqueeze(1).unsqueeze(1).to_broadcast([P, NT, TOPK, TOPK]),
                                               ALU.is_equal))
                        hold()
                        for t in range(NT):
                            last = dve.tensor_tensor(hot[:, t, :, :], hot[:, t, :, :],
                                                     keyno[:, t, :].unsqueeze(1).to_broadcast([P, TOPK, TOPK]), ALU.mult)
                        done(last)
                        hold()
                        done(dve.tensor_reduce(pick[:, s, :, :], hot, AX.X, ALU.add))
                        hold()
                    for t in range(NT):
                        last = dve.scalar_tensor_tensor(
                            idx[:, ds(i * 4 + (t * PH + j), 1), :].rearrange("p a b -> p (a b)"),
                            pick[:, 0, t, :], float(NK), pick[:, 1, t, :], ALU.mult, ALU.add)
                    last.then_inc(topk_done, 1)
                body4 = count[0] - start4
            assert T4 == body4, body4
            count[0] = start4 + 2 * T4
            dve.memset(idx[:, NT * PH:, :], 0)
            dve.wait_ge(topk_done, 2 + PH)
            dve.tensor_copy(ixv[:, 0, :], idx[:, 0, :])
            dve.tensor_copy(ixu[:, 0, :], idx[:, 0, :]).then_inc(ix_staged, 1)
            dve.tensor_tensor(gates[:, :, :], best[:, :, :], best[:, :, 0:1].to_broadcast([P, NT * PH, TOPK]),
                              ALU.subtract).then_inc(gexp_in, 1)
            dve.wait_ge(gexp_done, 1)
            done(dve.tensor_reduce(gsum[:, :, 0], gates[:, :, :], AX.X, ALU.add))
            then()
            done(dve.reciprocal(gsum[:, :, :], gsum[:, :, :]))
            then()
            done(dve.tensor_tensor(gates[:, :, :], gates[:, :, :], gsum[:, :, 0:1].to_broadcast([P, NT * PH, TOPK]),
                                   ALU.mult))
            then()

            tile_of_u = [0]

            def weights(s, par):
                dve.wait_ge(gelu_ready, s)
                if not (isinstance(s, int) and s < 3):
                    dve.wait_ge(diag_ready, s * TOPK - 2 * TOPK)
                g_ = gates[:, ds(s - 1, 1), :].rearrange("p a b -> p (a b)")
                dve.tensor_tensor(wgt[:, 1 - par, :], gel[:, 1 - par, :], g_, ALU.mult).then_inc(wgt_ready, 1)

            def step(s, par, u, v_):
                if isinstance(s, int) and s == PH:
                    tile_of_u[0] = 1
                for k in range(TOPK):
                    if k == 1 and v_:
                        weights(s, par)
                    if k == 8 and not (isinstance(s, int) and s == 2 * PH):
                        if not (isinstance(s, int) and s < 2):
                            dve.wait_ge(v_used, s * TOPK - TOPK)
                        if not (isinstance(s, int) and s == 2 * PH - 1):
                            dve.tensor_copy(ixu[:, 1 - par, :], idx[:, ds(s + 1, 1), :].rearrange("p a b -> p (a b)"))
                        dve.tensor_copy(ixv[:, par, :], idx[:, ds(s, 1), :].rearrange("p a b -> p (a b)")).then_inc(
                            ix_staged, 1)
                    if u:
                        b = k % UB
                        dve.wait_ge(u_loaded[b], s * (TOPK // UB * 16) + (k // UB + 1) * 16)
                        dve.tensor_tensor_reduce(ubuf[b], ubuf[b], rows[:, tile_of_u[0], :], 1.0, 0.0,
                                                 ALU.mult, ALU.add, dots[:, par, k:k + 1]).then_inc(u_used, 1)

            def finish(t):
                dve.wait_ge(v_used, (t + 1) * PH * TOPK)
                dve.wait_ge(gain_loaded, 96)
                done(dve.scalar_tensor_tensor(rows[:, t, :], rows[:, t, :], ALPHA,
                                              ps[:, 4 * t:4 * t + 4, :].rearrange("p a b -> p (a b)"),
                                              ALU.mult, ALU.add))
                then()
                layer_norm(LN_OUT + t, rows[:, t, :])

            run_steps(dve, step, lambda: finish(0))
            finish(1)


T4 = 4 * 17


_INS = ["x", "meta", "ln0_g", "ln0_b", "w_in", "ssd_conv_w", "ssd_conv_b", "ssd_dt_bias", "ssd_a_log", "ssd_d",
        "ssd_norm_w", "ssd_out", "cf_dw_w", "cf_dw_b", "cf_ln_g", "cf_ln_b", "cf_out", "w_o", "ln1_g", "ln1_b",
        "peer_wq", "peer_keys", "peer_u", "peer_v", "ln2_g", "ln2_b"]


def kernel(**inputs):
    import numpy as _np
    import concourse.bacc as _bacc
    from concourse import mybir as _mybir
    from concourse.bass_utils import run_bass_kernel_spmd as _run

    nc = _bacc.Bacc("TRN2", target_bir_lowering=False, num_devices=1)
    arrays, A = {}, {}
    for name in _INS:
        a = _np.ascontiguousarray(inputs[name])
        arrays[f"in_{name}"] = a
        A[name] = nc.dram_tensor(f"in_{name}", a.shape, _mybir.dt.from_np(a.dtype), kind="ExternalInput").ap()
    out = nc.dram_tensor("out", (1, SEQ, D), _mybir.dt.float32, kind="ExternalOutput").ap()
    build(nc, A, out)
    return _run(nc, [arrays], core_ids=[0]).results[0]["out"]
```

```python
from contextlib import ExitStack

import concourse.bass as bass
from concourse import mybir
from concourse.alu_op_type import AluOpType as ALU

ACT = mybir.ActivationFunctionType
AX = mybir.AxisListType
F32 = mybir.dt.float32
U32 = mybir.dt.uint32
F32R = mybir.dt.float32r

P = 128
D = 2048
SEQ, META = 256, 16
L = META + SEQ
KT = D // P
SW = 256
NS = D // SW
GROUPS, HEADS, HPG, HD = 8, 32, 4, 64
KC, KF = 4, 31
XBC = D + 2 * GROUPS * P
OFF_XBC = D
OFF_DT = OFF_XBC + XBC
OFF_VAL = OFF_DT + HEADS
OFF_CGATE = OFF_VAL + D
OFF_GSSD = OFF_CGATE + D
OFF_GCF = OFF_GSSD + D
CHUNKS = [(0, META), (META, META + P), (META + P, L)]
PH, NK, TOPK = 8, 128, 16
NT = SEQ // P
EPS = 1e-5
ALPHA = 2.0 ** 0.25
LOW = -3.0e38
UNITS = 4
KU = KT // UNITS
S_GROUP = 1
S_SSD = S_GROUP + 5 * GROUPS
S_CF = S_SSD + 2 * NS
S_WO = S_CF + 2 * NS
S_WQ = S_WO + NS
S_END = S_WQ + NS
TOPK_STEPS = 17
UB = 4
LN_X, LN_META, LN_H1, LN_OUT = (0, 2), 1, 3, 5


def build(nc, A, out):
    ds = bass.ds
    x, meta = A["x"][0], A["meta"]
    w_in, ssd_out, cf_out, w_o, wq = (A[n][0] for n in ("w_in", "ssd_out", "cf_out", "w_o", "peer_wq"))
    peer_u, peer_v = A["peer_u"][0], A["peer_v"][0]

    with ExitStack() as ctx:
        def sb(name, shape, dt=F32):
            return ctx.enter_context(nc.sbuf_tensor(name, shape, dt))

        def arena(name, split):
            at = (nc.sbuf_base + 31) // 32 * 32
            flat = sb(name, [P, 2 * KT * SEQ])
            return flat, nc.alloc_sbuf_tensor_at(split, [P, 2, KT, SEQ], F32R, offset=at)

        def sem(name):
            return ctx.enter_context(nc.semaphore(name))

        mem_a, c_split = arena("mem_a", "c_split")
        mem_b, ym_split = arena("mem_b", "ym_split")
        h_split = sb("h_split", [P, 2, KT, L], F32R)
        rows = sb("rows", [P, NT, D])
        gain = sb("gain", [P, 2, D])
        raw_all = sb("raw_all", [P, UNITS, KU, SW])
        raw = [raw_all[:, i, :, :] for i in range(UNITS)]
        gain2 = raw_all[:, :, :, :].rearrange("p q k n -> p (q k n)").rearrange("p (a b) -> p a b", a=2)
        spare = sb("spare", [P, D])
        whi = [sb(f"whi{i}", [P, KU, SW], F32R) for i in range(UNITS)]
        wlo = [sb(f"wlo{i}", [P, KU, SW], F32R) for i in range(UNITS)]
        v = sb("v", [P, 2, SEQ])
        v2 = sb("v2", [P, 2, SEQ])
        rinv = sb("rinv", [P, 2, SEQ])
        ident = sb("ident", [P, P])
        ones = sb("ones", [P, P])
        avg = sb("avg", [P, P])
        alpha = sb("alpha", [P, P])
        causal = sb("causal", [P, P])
        iota16 = sb("iota16", [P, TOPK])
        eps = sb("eps", [P, 1])
        pcol = sb("pcol", [P, 96])
        convw = sb("convw", [P, KC, 32])
        cfw = sb("cfw", [P, 4 * 124])
        dcol = sb("dcol", [P, KT])
        head = sb("head", [HEADS, 4])
        cs = sb("cs", [HEADS, L])
        tm = sb("tm", [P, 6, HEADS])
        edec = sb("edec", [P, HEADS])
        stats = sb("stats", [P, 4, 6])
        hstats = [sb(f"hstats{t}", [P, 4, 6]) for t in range(NT)]
        mv = sb("mv", [P, 2])
        sd = sb("sd", [P, 2])
        hmv = [sb(f"hmv{t}", [P, 2]) for t in range(NT)]
        hsd = [sb(f"hsd{t}", [P, 2]) for t in range(NT)]
        unused = sb("unused", [P, 1])
        route = sb("route", [P, 720])

        def f32(ap):
            return ap.bitcast(F32)

        scr = mem_a[:, 0:12 * L].rearrange("p (a b) -> p a b", b=L)
        xin, acc, xg = scr[:, 0:4, :], scr[:, 4:8, :], scr[:, 8:12, :]
        hsm = [scr[0:HEADS, i, :] for i in range(12)]

        vraw = mem_a[:, 3264:3808].rearrange("p (a b) -> p a b", a=2)
        gsig = mem_a[:, 3808:4352].rearrange("p (a b) -> p a b", a=2)
        zs = mem_a[:, 4352:4864].rearrange("p (a b) -> p a b", a=2)
        btm = mem_a[:, 4864:5120].rearrange("p (a b) -> p a b", a=2)
        scm = mem_a[:, 5120:5376].rearrange("p (a b) -> p a b", a=2)
        state = mem_a[:, 5376:5888].rearrange("p (a b) -> p a b", a=2)
        meta_t = mem_a[0:META, 5888:5888 + D]
        prow = mem_b[0:96, 0:128]
        convrow = mem_b[:, 128:256]
        cfrow = mem_b[0:124, 256:768].rearrange("p (a b) -> p a b", a=4)
        rflat = rows[:, :, :].rearrange("p a b -> p (a b)")
        seg = rflat[:, 0:1024].rearrange("p (c h i) -> p c h i", c=2, h=HPG)
        ecs = rflat[:, 1024:2048].rearrange("p (c h i) -> p c h i", c=2, h=HPG)
        rmask = rflat[0:HEADS, 2048:3072].rearrange("p (c h i) -> p c h i", c=2, h=HPG)
        xdt = rflat[:, 3072:3584].rearrange("p (c n) -> p c n", c=2)
        xw = rflat[:, 3584:4096].rearrange("p (c n) -> p c n", c=2)
        mix1 = rflat.rearrange("p (a b) -> p a b", a=KT)
        gflat = gain[:, :, :].rearrange("p a b -> p (a b)")
        cT = gflat.rearrange("p (a b) -> p a b", a=KT)
        csq = mem_a[:, 0:KT * SEQ].rearrange("p (a b) -> p a b", a=KT)
        res = [v, v2]
        qts = [v, v2]
        left = mem_a[:, 0:512].rearrange("p (a b) -> p a b", a=4)
        cand = mem_a[:, 512:1024].rearrange("p (t a) -> p t a", t=2)
        cand2 = mem_a[:, 1024:1536].rearrange("p (t a) -> p t a", t=2)
        hot = mem_a[:, 1536:2048].rearrange("p (t k i) -> p t k i", t=2, k=TOPK)
        topv = mem_a[:, 2048:2112].rearrange("p (a b) -> p a b", a=4)
        topif = mem_a[:, 2112:2176].rearrange("p (a b) -> p a b", a=4)
        topi = mem_a[:, 2176:2240].rearrange("p (a b) -> p a b", a=4).bitcast(U32)
        bestv = mem_a[:, 2240:2272].rearrange("p (a b) -> p a b", a=2)
        bestj = mem_a[:, 2272:2304].rearrange("p (a b) -> p a b", a=2).bitcast(U32)
        part = mem_a[:, 2304:2368].rearrange("p (s a b) -> p s a b", s=2, a=2).bitcast(U32)
        partf = mem_a[:, 2368:2432].rearrange("p (s a b) -> p s a b", s=2, a=2)
        pick = mem_a[:, 2432:2496].rearrange("p (s a b) -> p s a b", s=2, a=2)
        scs = [mem_a[:, 2560 + 512 * i:3072 + 512 * i].rearrange("p (a b) -> p a b", a=4) for i in range(2)]
        keysT = mem_a[:, 3584:5632].rearrange("p (a b) -> p a b", a=2 * PH)
        keyrow = mem_a[:, 5632:7680].rearrange("p (a b) -> p a b", a=2 * PH)
        gates = route[:, 0:256].rearrange("p (a b) -> p a b", b=TOPK)
        idx = route[:, 256:544].rearrange("p (a b) -> p a b", b=TOPK).bitcast(U32)
        dots, gel, wgt, ixu, ixv = (route[:, 544 + 32 * i:576 + 32 * i].rearrange("p (a b) -> p a b", a=2)
                                    for i in range(5))
        ixu, ixv = ixu.bitcast(U32), ixv.bitcast(U32)
        gsum, grec = route[:, 704:706], route[:, 706:708]
        ubuf = [gflat[:, 0:D], gflat[:, D:2 * D], mem_a[:, 5632:5632 + D], spare[:, :]]
        vbuf = [mem_b[:, D * i:D * (i + 1)] for i in range(UB)]
        diag = [rinv[:, i // 2, i % 2 * P:(i % 2 + 1) * P] for i in range(4)]

        ps = ctx.enter_context(nc.psum_tensor("ps", [P, 8, 512], F32))
        T0, T1, T2, T3 = (ps[:, 4 + i, :] for i in range(4))

        x_loaded = [sem(f"x_loaded{i}") for i in range(NT)]
        meta_loaded, gain_loaded, param_loaded, keys_loaded = (sem(n) for n in (
            "meta_loaded", "gain_loaded", "param_loaded", "keys_loaded"))
        raw_loaded = [sem(f"raw_loaded{i}") for i in range(UNITS)]
        c_cols_loaded = [sem(f"c_cols_loaded{i}") for i in range(UNITS)]
        hi_ready, lo_ready, unit_done = sem("hi_ready"), sem("lo_ready"), sem("unit_done")
        u_loaded = [sem(f"u_loaded{i}") for i in range(UB)]
        v_loaded = [sem(f"v_loaded{i}") for i in range(UB)]
        const_step, const_ready = sem("const_step"), sem("const_ready")
        vec_step, gated = sem("vec_step"), sem("gated")
        var_ready, sd_done, ln_done = sem("var_ready"), sem("sd_done"), sem("ln_done")
        turned, turned_hi, turned_lo = sem("turned"), sem("turned_hi"), sem("turned_lo")
        rel_ready, w_ready, tabs_ready = sem("rel_ready"), sem("w_ready"), sem("tabs_ready")
        x1_ready, ex_ready, alog_ready, ecl_ready = (sem(n) for n in ("x1_ready", "ex_ready", "alog_ready", "ecl_ready"))
        tabs_done, tabs_copied, proj_copied = sem("tabs_done"), sem("tabs_copied"), sem("proj_copied")
        r_ready, csb_done, seg_ready, ecs_ready, exp_ready = (sem(n) for n in (
            "r_ready", "csb_done", "seg_ready", "ecs_ready", "exp_ready"))
        conv_ready, xg_ready, xpose_done, score_done = (sem(n) for n in (
            "conv_ready", "xg_ready", "xpose_done", "score_done"))
        xtm_ready, btm_ready, mt_ready, state_done, s_ready = (sem(n) for n in (
            "xtm_ready", "btm_ready", "mt_ready", "state_done", "s_ready"))
        y_done, v_ready, sq_ready, nsum_done, nsd_ready, ynorm_ready = (sem(n) for n in (
            "y_done", "v_ready", "sq_ready", "nsum_done", "nsd_ready", "ynorm_ready"))
        glu_ready = sem("glu_ready")
        sg_ready, mix_ready = sem("sg_ready"), sem("mix_ready")
        cf_ready, mean_done, cen_ready, csq_ready, cvar_done, csd_ready, cn_ready, silu_ready, c_ready = (sem(n) for n in (
            "cf_ready", "mean_done", "cen_ready", "csq_ready", "cvar_done", "csd_ready", "cn_ready", "silu_ready",
            "c_ready"))
        m_ready = sem("m_ready")
        res_ready, res_turned, res_copied = sem("res_ready"), sem("res_turned"), sem("res_copied")
        q_copied, sc_done, sc_copied, topk_done = (sem(n) for n in ("q_copied", "sc_done", "sc_copied", "topk_done"))
        gexp_in, topk_step, weight_step = sem("gexp_in"), sem("topk_step"), sem("weight_step")
        ix_staged, u_used, v_used, gelu_ready, wgt_ready, diag_ready = (sem(n) for n in (
            "ix_staged", "u_used", "v_used", "gelu_ready", "wgt_ready", "diag_ready"))
        stored, waited = sem("stored"), sem("waited")

        block = ctx.enter_context(nc.Block())

        TURN_X = 3
        TURN_META = TURN_X + 4
        TURN_KEYS = TURN_X + 4 * NT + 1
        TURN_H1 = TURN_KEYS + 4
        TURN_END = TURN_H1 + 4 * NT
        WITH_LO = [*range(TURN_X, TURN_KEYS), *range(TURN_H1, TURN_END)]

        def turn_x(t, q):
            return TURN_X + 5 * t + q

        def turn_h1(t, q):
            return TURN_H1 + 2 * q + t

        def bank(i):
            return ps[:, 4 + i % 4, :]

        def slab_done(eng, s):
            eng.wait_ge(unit_done, s * UNITS + UNITS)

        def run_steps(eng, step):
            step(0, 0, 0, None, True, True)
            step(1, 1, 0, 0, True, True)
            with eng.Fori(1, PH // 2 - 1) as i:
                step(i * 2, 0, 0, 0, True, True)
                step(i * 2 + 1, 1, 0, 0, True, True)
            step(PH - 2, 0, 0, 0, False, True)
            step(PH - 1, 1, 0, 0, False, False)
            step(PH, 0, 1, 0, False, False)
            step(PH + 1, 1, 1, 1, False, False)
            with eng.Fori(PH // 2 + 1, PH) as i:
                step(i * 2, 0, 1, 1, False, False)
                step(i * 2 + 1, 1, 1, 1, False, False)
            step(2 * PH, 0, None, 1, False, False)

        def settle(eng):
            eng.sem_inc(waited, 1)

        @block.sync
        def _(sp):
            def load_x(t):
                sp.dma_start(rows[:, t, :], x[t * P:(t + 1) * P, :]).then_inc(x_loaded[t], 16)

            def load_gain(g, b, gain_=gain):
                for i, r in enumerate((g, b)):
                    sp.dma_start(gain_[:, i, :], r.partition_broadcast(P)).then_inc(gain_loaded, 16)

            load_x(0)
            sp.dma_start(meta_t, meta).then_inc(meta_loaded, 16)
            load_gain(A["ln0_g"], A["ln0_b"])
            load_x(1)
            at = 0
            for r, n in (("ssd_conv_b", 32), ("ssd_norm_w", 16), ("cf_dw_b", 16), ("cf_ln_g", 16), ("cf_ln_b", 16)):
                sp.dma_start(prow[at:at + n, :], A[r][0].rearrange("(t p) -> t p", p=P)).then_inc(param_loaded, 16)
                at += n
            for k in range(KC):
                sp.dma_start(convrow[32 * k:32 * k + 32, :],
                             A["ssd_conv_w"][0, k].rearrange("(t p) -> t p", p=P)).then_inc(param_loaded, 16)
            sp.dma_start(cfrow, A["cf_dw_w"][0].rearrange("k (t p) -> (k t) p", p=P).rearrange(
                "(a r) p -> r a p", r=124)).then_inc(param_loaded, 16)
            sp.dma_start(head[:, 0:1], A["ssd_dt_bias"][0].rearrange("(h o) -> h o", o=1)).then_inc(param_loaded, 16)
            sp.dma_start(head[:, 1:2], A["ssd_a_log"][0].rearrange("(h o) -> h o", o=1)).then_inc(param_loaded, 16)
            d2 = A["ssd_d"][0].rearrange("(t u) -> u t", u=2)
            with nc.allow_non_contiguous_dma(reason="32 values"):
                for u in range(2):
                    sp.dma_start(dcol[HD * u:HD * u + HD, :],
                                 d2[u:u + 1, :].to_broadcast([HD, KT])).then_inc(param_loaded, 16)

            def unit_rows(w, q, at, n):
                return w[q * KU * P:(q + 1) * KU * P, ds(at, n)].rearrange("(k p) n -> p k n", p=P)

            def load(s, w, at):
                for q in range(UNITS):
                    if not (isinstance(s, int) and s == 0):
                        sp.wait_ge(lo_ready, s * UNITS + (q + 1 - UNITS))
                        settle(sp)
                    sp.dma_start(raw[q][:, :, :], unit_rows(w, q, at, SW)).then_inc(raw_loaded[q], 16)

            def load_bc(s, g):
                for q in range(UNITS):
                    sp.wait_ge(lo_ready, s * UNITS + (q + 1 - UNITS))
                    settle(sp)
                    sp.dma_start(raw[q][:, :, 0:P], unit_rows(w_in, q, g * P + OFF_XBC + D, P)).then_inc(
                        raw_loaded[q], 16)
                    sp.dma_start(raw[q][:, :, P:SW], unit_rows(w_in, q, g * P + OFF_XBC + D + GROUPS * P, P)).then_inc(
                        c_cols_loaded[q], 16)

            load(0, w_in, OFF_DT)
            with sp.Fori(0, GROUPS) as g:
                load(g * 5 + S_GROUP, w_in, g * SW + OFF_XBC)
                load_bc(g * 5 + (S_GROUP + 1), g)
                load(g * 5 + (S_GROUP + 2), w_in, g * SW + OFF_VAL)
                load(g * 5 + (S_GROUP + 3), w_in, g * SW)
                load(g * 5 + (S_GROUP + 4), w_in, g * SW + OFF_CGATE)
            with sp.Fori(0, NS) as i:
                load(i * 2 + S_SSD, w_in, i * SW + OFF_GSSD)
                load(i * 2 + (S_SSD + 1), ssd_out, i * SW)
            with sp.Fori(0, NS) as i:
                load(i * 2 + S_CF, w_in, i * SW + OFF_GCF)
                load(i * 2 + (S_CF + 1), cf_out, i * SW)
            for i in range(2):
                load(i + S_WO, w_o, i * SW)
            slab_done(sp, S_WO - 1)
            sp.dma_start(keyrow, A["peer_keys"][0].rearrange("s h n k -> n (s h) k")).then_inc(keys_loaded, 16)
            load(2 + S_WO, w_o, 2 * SW)
            sp.wait_ge(c_ready, 4)
            load_gain(A["ln1_g"][0], A["ln1_b"][0])
            with sp.Fori(3, NS) as i:
                load(i + S_WO, w_o, i * SW)
            with sp.Fori(0, NS) as i:
                load(i + S_WQ, wq, i * SW)
            sp.wait_ge(lo_ready, S_END * UNITS)
            load_gain(A["ln2_g"][0], A["ln2_b"][0], gain2)
            for t in range(NT):
                for half in range(2):
                    sp.wait_ge(ln_done, 4 * (LN_OUT + t) + 2 * half + 2)
                    c = slice(half * D // 2, (half + 1) * D // 2)
                    sp.dma_start(out[0, t * P:(t + 1) * P, c], rows[:, t, c]).then_inc(stored, 16)
            sp.wait_ge(stored, 2 * 16 * NT)

        @block.gpsimd
        def _(pool):
            pool.memset(ident[:, :], 0.0).then_inc(const_step, 1)
            pool.memset(causal[:, :], 1.0).then_inc(const_step, 1)
            pool.memset(alpha[:, :], 0.0).then_inc(const_step, 1)
            pool.memset(ones[:, :], 1.0).then_inc(const_ready, 1)
            pool.memset(avg[:, :], 1.0 / D).then_inc(const_ready, 1)
            pool.memset(eps[:, :], EPS).then_inc(const_ready, 1)
            pool.iota(iota16[:, :], [[1, TOPK]], base=0, channel_multiplier=0,
                      allow_small_or_imprecise_dtypes=True).then_inc(const_ready, 1)
            pool.wait_ge(const_step, 3)
            pool.affine_select(out=alpha[:, :], in_=alpha[:, :], compare_op=ALU.not_equal, fill=ALPHA, base=0,
                               pattern=[[-1, P]], channel_multiplier=1).then_inc(const_ready, 1)
            pool.affine_select(out=ident[:, :], in_=ident[:, :], compare_op=ALU.not_equal, fill=1.0, base=0,
                               pattern=[[-1, P]], channel_multiplier=1).then_inc(const_ready, 1)
            pool.affine_select(out=causal[:, :], in_=causal[:, :], compare_op=ALU.is_ge, fill=0.0, base=0,
                               pattern=[[1, P]], channel_multiplier=-1).then_inc(const_ready, 1)

            def low_parts(s, mine=range(UNITS)):
                for q in mine:
                    pool.wait_ge(hi_ready, s * UNITS + (q + 1))
                    pool.tensor_tensor(wlo[q][:, :, :], raw[q][:, :, :], f32(whi[q][:, :, :]), ALU.subtract).then_inc(
                        lo_ready, 1)

            with pool.Fori(0, S_WQ + 2) as s:
                low_parts(s)

            def gather(dst, table, index, landed):
                pool.indirect_dma_start(dst, None, table, bass.IndirectOffsetOnAxis(ap=index, axis=0)).then_inc(landed, 16)

            def step(s, par, tile_u, tile_v, scores, finds):
                pool.wait_ge(ix_staged, s + 1)
                for k in range(TOPK):
                    b = k % UB
                    if scores and 4 <= k < 4 + UNITS:
                        low_parts(s + (S_WQ + 2), (k - 4,))
                    if tile_u is not None:
                        if not (isinstance(s, int) and s * TOPK + k < UB):
                            pool.wait_ge(u_used, s * TOPK + (k - UB + 1))
                            settle(pool)
                        gather(ubuf[b], peer_u, ixu[:, par, k:k + 1], u_loaded[b])
                    if tile_v is not None:
                        if not (isinstance(s, int) and (s - 1) * TOPK + k < UB):
                            pool.wait_ge(v_used, s * TOPK + (k - UB + 1 - TOPK))
                            settle(pool)
                        gather(vbuf[b], peer_v, ixv[:, 1 - par, k:k + 1], v_loaded[b])

            run_steps(pool, step)

        @block.tensor
        def _(pe):
            def turn(i, sources, waits=()):
                for s, n in waits:
                    pe.wait_ge(s, n)
                if i >= 4:
                    pe.wait_ge(turned_hi, i - 3)
                    if i - 4 in WITH_LO:
                        pe.wait_ge(turned_lo, WITH_LO.index(i - 4) + 1)
                at = 0
                for src in sources:
                    n = src.shape[0]
                    last = pe.transpose(ps[0:src.shape[1], 4 + i % 4, at:at + n], src, ident[0:n, 0:n])
                    at += n
                last.then_inc(turned, 1)

            def unit(s, q, bank0, act, tiles=2):
                pe.wait_ge(lo_ready, s * UNITS + (q + 1))
                for u in range(tiles):
                    for kk in range(KU):
                        k = q * KU + kk
                        hi, lo = act(k)
                        o = ps[:, bank0 + u, 0:hi.shape[-1]]
                        w_hi = whi[q][:, kk, u * P:(u + 1) * P]
                        w_lo = wlo[q][:, kk, u * P:(u + 1) * P]
                        pe.matmul(o, w_hi, hi, start=(k == 0), stop=False)
                        pe.matmul(o, w_hi, lo, start=False, stop=False)
                        last = pe.matmul(o, w_lo, hi, start=False, stop=(k == KT - 1))
                last.then_inc(unit_done, 1)

            def product(s, bank0, act, tiles=2):
                for q in range(UNITS):
                    unit(s, q, bank0, act, tiles)

            def split(tensor, a, b):
                return lambda k: (tensor[:, 0, k, a:b], tensor[:, 1, k, a:b])

            h_all, h_seq = split(h_split, 0, L), split(h_split, META, L)

            turn(0, [prow], [(const_ready, 7), (param_loaded, 16 * 14)])
            turn(1, [convrow])
            turn(2, [cfrow[:, a, :] for a in range(4)])
            for t in range(NT):
                for q in range(4):
                    turn(turn_x(t, q), [rows[:, t, (4 * q + r) * P:(4 * q + r + 1) * P] for r in range(4)],
                         [(ln_done, 4 * LN_X[t] + q + 1)])
                if t == 0:
                    turn(TURN_META, [meta_t[:, k * P:(k + 1) * P] for k in range(KT)], [(ln_done, 4 * (LN_META + 1))])
            pe.wait_ge(turned_hi, TURN_KEYS)
            pe.wait_ge(turned_lo, 4 * NT + 1)

            product(0, 0, h_all, tiles=1)
            pe.wait_ge(x1_ready, 1)
            product(S_GROUP, 0, h_all)
            pe.wait_ge(tabs_ready, 1)
            dtv, ncs, wst = hsm[4], hsm[5], hsm[6]
            for n, (tab, c) in enumerate(((dtv, 1), (dtv, 2), (ncs, 1), (ncs, 2), (wst, 1), (wst, 0))):
                a, b = CHUNKS[c]
                pe.transpose(T1[0:b - a, n * HEADS:(n + 1) * HEADS], tab[:, a:b], ident[0:HEADS, 0:HEADS])
            pe.matmul(T1[:, 6 * HEADS:7 * HEADS], hsm[7][:, 0:P], ident[0:HEADS, 0:HEADS],
                      start=True, stop=True).then_inc(tabs_done, 1)

            def group(g, first=False):
                if not first:
                    pe.wait_ge(proj_copied, g * 5 + 3)
                    product(g * 5 + S_GROUP, 0, h_all)
                pe.wait_ge(proj_copied, g * 5 + 5)
                product(g * 5 + (S_GROUP + 1), 2, h_all)
                pe.wait_ge(r_ready, g + 1)
                if first:
                    pe.wait_ge(tabs_copied, 2)
                pe.matmul(T0, ones[0:HEADS, :], rmask[:, 0, :, :].rearrange("p a b -> p (a b)"),
                          start=True, stop=True)
                pe.matmul(T1, ones[0:HEADS, :], rmask[:, 1, :, :].rearrange("p a b -> p (a b)"),
                          start=True, stop=True).then_inc(csb_done, 1)
                pe.wait_ge(proj_copied, g * 5 + 6)
                product(g * 5 + (S_GROUP + 2), 0, h_all)
                pe.wait_ge(xg_ready, g * 4 + 4)
                for c in range(2):
                    for u in range(2):
                        a, b = CHUNKS[1 + c]
                        pe.transpose(T2[:, (2 * c + u) * P:(2 * c + u + 1) * P], xg[:, u, a:b], ident[:, :])
                pe.transpose(T3[:, 0:P], xg[:, 2, META:META + P], ident[:, :])
                pe.transpose(T3[0:META, P:2 * P], xg[:, 2, 0:META], ident[:, :])
                for u in range(2):
                    last = pe.transpose(T3[0:META, (2 + u) * P:(3 + u) * P], xg[:, u, 0:META], ident[:, :])
                last.then_inc(xpose_done, 1)
                pe.wait_ge(proj_copied, g * 5 + 7)
                for q in range(2):
                    unit(g * 5 + (S_GROUP + 3), q, 2, h_seq)
                pe.wait_ge(seg_ready, g + 1)
                pe.wait_ge(ecs_ready, g + 1)
                for c in range(2):
                    a, b = CHUNKS[1 + c]
                    last = pe.matmul(T0[:, c * P:(c + 1) * P], xg[:, 2, a:b], xg[:, 3, a:b], start=True, stop=True)
                last.then_inc(score_done, 1)
                pe.wait_ge(xtm_ready, g + 1)
                pe.wait_ge(btm_ready, g * 2 + 2)
                pe.matmul(T3[:, 0:HPG * HD], btm[0:META, 1, :], xw[0:META, 1, :], start=True, stop=True)
                pe.matmul(T3[:, HPG * HD:2 * HPG * HD], btm[:, 0, :], xw[:, 0, :],
                          start=True, stop=True).then_inc(state_done, 1)
                for q in range(2, UNITS):
                    unit(g * 5 + (S_GROUP + 3), q, 2, h_seq)
                pe.wait_ge(mt_ready, g + 1)
                pe.wait_ge(s_ready, g + 1)
                for u in range(2):
                    for c in range(2):
                        for r in range(2):
                            hh = 2 * u + r
                            o = ps[HD * r:HD * r + HD, 5, (2 * u + c) * P:(2 * u + c + 1) * P]
                            pe.matmul(o, xdt[:, c, hh * HD:(hh + 1) * HD], seg[:, c, hh, :], start=True, stop=False)
                            last = pe.matmul(o, state[:, c, hh * HD:(hh + 1) * HD], ecs[:, c, hh, :],
                                             start=False, stop=True)
                last.then_inc(y_done, 1)
                pe.wait_ge(proj_copied, g * 5 + 9)
                product(g * 5 + (S_GROUP + 4), 2, h_all)
                pe.wait_ge(sq_ready, g + 1)
                for u in range(2):
                    last = pe.matmul(T2[:, 0:SEQ], ones[:, :], v2[:, u, :], start=(u == 0), stop=(u == 1))
                last.then_inc(nsum_done, 1)

            group(0, True)
            with pe.Fori(1, GROUPS) as g:
                group(g)

            def mix_pair(i, base, s0, act, branch=()):
                pe.wait_ge(sg_ready, i + (base + 1))
                product(i * 2 + s0, 0, h_seq)
                for ready, n in branch:
                    pe.wait_ge(ready, n)
                pe.wait_ge(mix_ready, i + (base + 1))
                product(i * 2 + (s0 + 1), 2, act)

            y_act, c_act = split(ym_split, 0, SEQ), split(c_split, 0, SEQ)
            pe.wait_ge(proj_copied, 5 * GROUPS + 5)
            mix_pair(0, 0, S_SSD, y_act, [(ynorm_ready, GROUPS)])
            mix_pair(1, 0, S_SSD, y_act)
            pe.wait_ge(cf_ready, GROUPS + 1)
            for k in range(KT):
                last = pe.matmul(T0[:, 0:SEQ], avg[:, :], cT[:, k, :], start=(k == 0), stop=(k == KT - 1))
            last.then_inc(mean_done, 1)
            mix_pair(2, 0, S_SSD, y_act)
            pe.wait_ge(csq_ready, 1)
            for k in range(KT):
                last = pe.matmul(T1[:, 0:SEQ], avg[:, :], csq[:, k, :], start=(k == 0), stop=(k == KT - 1))
            last.then_inc(cvar_done, 1)
            with pe.Fori(3, NS) as i:
                mix_pair(i, 0, S_SSD, y_act)
            mix_pair(0, NS, S_CF, c_act, [(c_ready, 4)])
            with pe.Fori(1, NS) as i:
                mix_pair(i, NS, S_CF, c_act)

            m_act = split(ym_split, 0, SEQ)
            pe.nop().then_inc(res_turned, 2)
            pe.wait_ge(sg_ready, 2 * NS + 1)

            def turn_res(n, j):
                pe.wait_ge(res_ready, n + 3)
                pe.wait_ge(res_copied, n + 1)
                for t in range(NT):
                    for u in range(2):
                        last = pe.transpose(ps[:, 4 + j, t * SW + u * P:t * SW + (u + 1) * P],
                                            res[j][:, u, t * P:(t + 1) * P], ident[:, :])
                last.then_inc(res_turned, 1)

            pe.wait_ge(m_ready, NS - 1)
            for q in range(UNITS):
                if q == UNITS - 1:
                    pe.wait_ge(m_ready, NS)
                unit(S_WO, q, 0, m_act)
            for q in range(4):
                turn(TURN_KEYS + q, [keyrow[:, 4 * q + r, :] for r in range(4)], [(keys_loaded, 16)])
            product(S_WO + 1, 2, m_act)
            pe.wait_ge(turned_hi, TURN_KEYS + 4)
            turn_res(0, 0)
            with pe.Fori(1, NS // 2) as i:
                for j in range(2):
                    pe.wait_ge(res_ready, i * 2 + (j + 1))
                    product(i * 2 + (S_WO + j), 2 * j, m_act)
                    turn_res(i * 2 + (j - 1), 1 - j)
            turn_res(NS - 1, 1)
            pe.wait_ge(res_copied, NS + 2)
            def head_scores(h, j):
                pe.wait_ge(q_copied, h + 2)
                pe.wait_ge(sc_copied, h + 1)
                for t in range(NT):
                    for s in range(2):
                        last = pe.matmul(ps[:, 2 + j, (2 * t + s) * NK:(2 * t + s + 1) * NK],
                                         qts[j][:, s, t * P:(t + 1) * P],
                                         keysT[:, ds(h + s * PH, 1), :].rearrange("p a b -> p (a b)"),
                                         start=True, stop=True)
                last.then_inc(sc_done, 1)

            h1_act = split(h_split, 0, SEQ)
            pe.nop().then_inc(sc_done, 2)

            def turn_quarter(q):
                for t in range(NT):
                    turn(turn_h1(t, q), [rows[:, t, (4 * q + r) * P:(4 * q + r + 1) * P] for r in range(4)],
                         [(ln_done, 4 * LN_H1 + 2 * q + t + 1)])

            turn_quarter(0)
            pe.wait_ge(q_copied, 1)
            for q in range(UNITS):
                if q + 1 < UNITS:
                    turn_quarter(q + 1)
                pe.wait_ge(turned_hi, turn_h1(NT - 1, q) + 1)
                pe.wait_ge(turned_lo, WITH_LO.index(turn_h1(NT - 1, q)) + 1)
                unit(S_WQ, q, 0, h1_act)
            head_scores(0, 0)
            pe.wait_ge(q_copied, 2)
            product(S_WQ + 1, 0, h1_act)
            head_scores(1, 1)

            def v_bank(t, c):
                return ps[:, 4 * (1 - t) + c, :]

            def residual(t):
                for c in range(4):
                    pe.matmul(v_bank(t, c), alpha[:, :], rows[:, t, c * 512:(c + 1) * 512],
                              start=True, stop=False, skip_group_check=True)

            residual(0)

            def step(s, par, tile_u, tile_v, scores, finds):
                if isinstance(s, int) and s == PH + 1:
                    pe.wait_ge(sc_copied, 2 + PH)
                    residual(1)
                for k in range(TOPK):
                    if tile_v is not None:
                        b = k % UB
                        pe.wait_ge(v_loaded[b], (s - 1) * (TOPK // UB * 16) + (k // UB + 1) * 16)
                        pe.wait_ge(diag_ready, (s - 1) * TOPK + (k + 1))
                        for c in range(4):
                            last = pe.matmul(v_bank(tile_v, c), diag[b], vbuf[b][:, c * 512:(c + 1) * 512],
                                             start=False, stop=False, skip_group_check=True)
                        last.then_inc(v_used, 1)
                    if scores and 3 <= k < 3 + UNITS:
                        if k == 3:
                            pe.wait_ge(q_copied, s + 3)
                        unit(s + (S_WQ + 2), k - 3, 0, h1_act)
                    if scores and k == 3 + UNITS:
                        head_scores(s + 2, par)

            run_steps(pe, step)

        @block.scalar
        def _(act):
            act.nop().then_inc(proj_copied, 5)
            act.nop().then_inc(sg_ready, 1)
            act.nop().then_inc(res_copied, 2)
            act.nop().then_inc(q_copied, 1)
            act.nop().then_inc(sc_copied, 2)

            def high_parts(s, units=range(UNITS), bc=None):
                for q in units:
                    act.wait_ge(raw_loaded[q], s * 16 + 16)
                    if bc is not None:
                        act.wait_ge(c_cols_loaded[q], bc * 16 + 16)
                    if not (isinstance(s, int) and s == 0):
                        act.wait_ge(unit_done, s * UNITS + (q + 1 - UNITS))
                    act.activation(whi[q][:, :, :], raw[q][:, :, :], ACT.Copy).then_inc(hi_ready, 1)

            def sqrt_table():
                act.activation(unused[:, :], eps[:, :], ACT.Sqrt)

            def ln_sd(n, p=P, mv=mv, sd=sd):
                act.wait_ge(var_ready, n + 1)
                act.activation(sd[0:p, 0:1], mv[0:p, 1:2], ACT.Sqrt, bias=eps[0:p, :]).then_inc(sd_done, 1)

            def turned_copy(i, dst, src):
                act.wait_ge(turned, i + 1)
                act.activation(dst, src, ACT.Copy).then_inc(turned_hi, 1)

            act.wait_ge(const_ready, 7)
            ln_sd(LN_X[0])
            turned_copy(0, pcol[:, :], bank(0)[:, 0:96])
            turned_copy(1, convw[:, :, :].rearrange("p a b -> p (a b)"), bank(1)[:, 0:128])
            turned_copy(2, cfw[:, :], bank(2)[:, 0:496])
            for t in range(NT):
                for q in range(4):
                    i = turn_x(t, q)
                    turned_copy(i, h_split[:, 0, 4 * q:4 * q + 4, META + t * P:META + (t + 1) * P],
                                bank(i).rearrange("p (a b) -> p a b", a=4))
                if t == 0:
                    ln_sd(LN_META, META)
                    ln_sd(LN_X[1], mv=hmv[1], sd=hsd[1])
                    high_parts(0)
                    turned_copy(TURN_META, h_split[:, 0, :, 0:META],
                                bank(TURN_META)[:, 0:KT * META].rearrange("p (a b) -> p a b", a=KT))

            act.wait_ge(param_loaded, 16 * 14)
            act.activation(head[:, 1:2], head[:, 1:2], ACT.Exp).then_inc(alog_ready, 1)
            high_parts(S_GROUP)
            act.wait_ge(x1_ready, 1)
            act.activation(hsm[2], hsm[1], ACT.Exp, scale=-1.0).then_inc(ex_ready, 1)
            high_parts(S_GROUP + 1, (0, 1, 2), bc=0)
            act.wait_ge(rel_ready, 1)
            act.activation(hsm[6], hsm[8], ACT.Exp, scale=-1.0).then_inc(w_ready, 1)
            a, b = CHUNKS[1]
            act.activation(head[:, 2:3], cs[:, b - 1:b], ACT.Exp).then_inc(ecl_ready, 1)
            act.wait_ge(tabs_done, 1)
            act.activation(tm[:, 0:5, :], T1[:, 0:5 * HEADS].rearrange("p (a b) -> p a b", a=5), ACT.Copy)
            act.activation(tm[0:META, 5, :], T1[0:META, 5 * HEADS:6 * HEADS], ACT.Copy).then_inc(tabs_copied, 1)
            act.activation(edec[:, :], T1[:, 6 * HEADS:7 * HEADS], ACT.Copy).then_inc(tabs_copied, 1)

            def group(g, first=False):
                s = g * 5 + S_GROUP
                high_parts(s + 1, (3,) if first else range(UNITS), bc=g)
                slab_done(act, s)
                act.wait_ge(conv_ready, g * 4 + 4)
                act.activation(xin[:, 0:2, :], ps[:, 0:2, 0:L], ACT.Copy).then_inc(proj_copied, 1)
                high_parts(s + 2)
                slab_done(act, s + 1)
                act.activation(xin[:, 2:4, :], ps[:, 2:4, 0:L], ACT.Copy).then_inc(proj_copied, 1)
                high_parts(s + 3, (0, 1))
                for i, tile in enumerate((g * 2, g * 2 + 1, g + 16, g + 24)):
                    act.wait_ge(conv_ready, g * 4 + (i + 5))
                    act.activation(xg[:, i, :], acc[:, i, :], ACT.Silu, bias=pcol[:, ds(tile, 1)]).then_inc(xg_ready, 1)
                high_parts(s + 3, (2,))
                act.wait_ge(seg_ready, g + 1)
                act.activation(ecs[:, :, :, :].rearrange("p c h i -> p c (h i)"), ps[:, 4:6, :], ACT.Exp).then_inc(
                    ecs_ready, 1)
                act.activation(seg[:, :, :, :], seg[:, :, :, :], ACT.Exp).then_inc(exp_ready, 1)
                high_parts(s + 3, (3,))
                slab_done(act, s + 2)
                act.wait_ge(glu_ready, g + 1)
                act.activation(vraw[:, :, :], ps[:, 0:2, 0:L], ACT.Copy).then_inc(proj_copied, 1)
                act.wait_ge(xtm_ready, g + 1)
                act.activation(btm[:, 0, :], T3[:, 0:P], ACT.Copy).then_inc(btm_ready, 1)
                act.activation(btm[0:META, 1, :], T3[0:META, P:2 * P], ACT.Copy).then_inc(btm_ready, 1)
                high_parts(s + 4)
                slab_done(act, s + 3)
                act.activation(zs[:, :, :], ps[:, 2:4, 0:SEQ], ACT.Silu).then_inc(proj_copied, 1)
                high_parts(s + 5, (0, 1))
                act.wait_ge(v_ready, g + 1)
                act.activation(v2[:, :, :], v[:, :, :], ACT.Square).then_inc(sq_ready, 1)
                high_parts(s + 5, (2, 3))
                slab_done(act, s + 4)
                act.wait_ge(cf_ready, g + 1)
                act.activation(gsig[:, :, :], ps[:, 2:4, 0:L], ACT.Sigmoid).then_inc(proj_copied, 1)
                act.wait_ge(nsum_done, g + 1)
                act.activation(rinv[:, 0, :], T2[:, 0:SEQ], ACT.Sqrt, bias=eps[:, :], scale=1.0 / SW).then_inc(nsd_ready, 1)

            group(0, True)
            with act.Fori(1, GROUPS) as g:
                group(g)

            def sig_pair(i, base, s0, middle=lambda: None):
                s = i * 2 + s0
                high_parts(s + 1)
                slab_done(act, s)
                act.wait_ge(mix_ready, i + (base + 1))
                act.activation(v[:, :, :], ps[:, 0:2, 0:SEQ], ACT.Sigmoid).then_inc(sg_ready, 1)
                high_parts(s + 2, (0, 1))
                middle()
                high_parts(s + 2, (2, 3))

            act.wait_ge(ynorm_ready, GROUPS)
            with act.Fori(0, 2) as i:
                sig_pair(i, 0, S_SSD)

            def square():
                act.wait_ge(cen_ready, 1)
                act.activation(csq, cT, ACT.Square).then_inc(csq_ready, 1)

            sig_pair(2, 0, S_SSD, square)

            def cf_sd():
                act.wait_ge(cvar_done, 1)
                act.activation(rinv[:, 0, :], T1[:, 0:SEQ], ACT.Sqrt, bias=eps[:, :]).then_inc(csd_ready, 1)

            sig_pair(3, 0, S_SSD, cf_sd)
            with act.Fori(4, NS) as i:
                def silu():
                    act.wait_ge(cn_ready, 1)
                    for r in range(4):
                        k = i * 4 + (r - 16)
                        c = cT[:, ds(k, 1), :]
                        act.activation(c, c, ACT.Silu, bias=pcol[:, ds(k + 80, 1)],
                                       scale=pcol[:, ds(k + 64, 1)]).then_inc(silu_ready, 1)
                sig_pair(i, 0, S_SSD, silu)
            with act.Fori(0, NS) as i:
                sig_pair(i, NS, S_CF)

            def res_copy(n, j):
                act.wait_ge(res_turned, n + 3)
                act.activation(rows[:, :, ds(n * SW, SW)],
                               ps[:, 4 + j, :].rearrange("p (t n) -> p t n", t=NT), ACT.Copy).then_inc(res_copied, 1)

            high_parts(S_WO + 1)
            for q in range(4):
                i = TURN_KEYS + q
                turned_copy(i, keysT[:, 4 * q:4 * q + 4, :], bank(i).rearrange("p (a b) -> p a b", a=4))
            high_parts(S_WO + 2)
            res_copy(0, 0)
            with act.Fori(1, NS // 2) as i:
                for j in range(2):
                    high_parts(i * 2 + (S_WO + 1 + j))
                    res_copy(i * 2 + (j - 1), 1 - j)
            sqrt_table()
            res_copy(NS - 1, 1)

            for t in range(NT):
                ln_sd(LN_H1 + t, mv=hmv[t], sd=hsd[t])
            for q in range(4):
                for t in range(NT):
                    i = turn_h1(t, q)
                    turned_copy(i, h_split[:, 0, 4 * q:4 * q + 4, t * P:(t + 1) * P],
                                bank(i).rearrange("p (a b) -> p a b", a=4))

            def sc_copy(h, j):
                act.wait_ge(sc_done, h + 3)
                act.wait_ge(topk_done, h + 1)
                act.activation(scs[j], ps[:, 2 + j, :].rearrange("p (a b) -> p a b", a=4), ACT.Copy).then_inc(
                    sc_copied, 1)

            def q_copy(h, j):
                slab_done(act, h + S_WQ)
                act.wait_ge(sc_done, h + 1)
                act.activation(qts[j][:, :, :], ps[:, 0:2, 0:SEQ], ACT.Copy).then_inc(q_copied, 1)

            high_parts(S_WQ + 1, (0, 1, 2))
            q_copy(0, 0)
            high_parts(S_WQ + 1, (3,))
            sc_copy(0, 0)
            q_copy(1, 1)
            sc_copy(1, 1)

            def step(s, par, tile_u, tile_v, scores, finds):
                if scores:
                    high_parts(s + (S_WQ + 2))
                if tile_v is None:
                    q_copy(s + 2, par)
                    sc_copy(s + 2, par)
                    return
                if tile_v == 0:
                    act.wait_ge(gexp_in, s)
                    for t in range(NT):
                        e = gates[:, ds(s + (t * PH - 1), 1), :].rearrange("p a b -> p (a b)")
                        act.activation(e, e, ACT.Exp)
                act.wait_ge(u_used, s * TOPK)
                act.activation(gel[:, 1 - par, :], dots[:, 1 - par, :], ACT.Gelu).then_inc(gelu_ready, 1)
                act.wait_ge(wgt_ready, s)
                for k in range(TOPK):
                    if not (isinstance(s, int) and (s - 1) * TOPK + k < 4):
                        act.wait_ge(v_used, s * TOPK + (k - 3 - TOPK))
                    act.activation(diag[k % 4], ident[:, :], ACT.Copy, scale=wgt[:, 1 - par, k:k + 1]).then_inc(
                        diag_ready, 1)
                    if scores and k == 7:
                        q_copy(s + 2, par)
                    if scores and k == 11:
                        sc_copy(s + 2, par)
                    if isinstance(s, int) and s == PH + 1 and k == 7:
                        ln_sd(LN_OUT)

            run_steps(act, step)
            sqrt_table()
            ln_sd(LN_OUT + 1)

        @block.vector
        def _(dve):
            dve.nop().then_inc(conv_ready, 4)
            dve.nop().then_inc(cf_ready, 1)
            dve.nop().then_inc(glu_ready, 1)
            dve.nop().then_inc(mix_ready, 1)
            dve.nop().then_inc(res_ready, 2)
            dve.nop().then_inc(topk_done, 2)
            count = [0]

            def done(ins):
                ins.then_inc(vec_step, 1)
                count[0] += 1

            def then():
                dve.wait_ge(vec_step, count[0])

            def quarter(ap, q):
                return ap[:, q, :] if len(ap.shape) == 3 else ap[:, q * 512:(q + 1) * 512]

            def ln_stats(src, p=P, stats=stats, quarters=range(4)):
                for q in quarters:
                    last = dve.bn_stats(stats[0:p, q, :], quarter(src, q))
                done(last)

            def aggregate(mv=mv, stats=stats, p=P):
                then()
                dve.bn_aggr(mv[0:p, :], stats[0:p, :, :].rearrange("p a b -> p (a b)")).then_inc(var_ready, 1)

            def layer_norm(n, rows_, gain=gain, src=None, gain_load=None):
                aggregate()
                if gain_load:
                    dve.wait_ge(gain_loaded, gain_load)
                normalise(n, rows_, gain=gain, src=src)

            def normalise(n, rows_, p=P, gain=gain, src=None, mv=mv, sd=sd):
                dve.wait_ge(var_ready, n + 1)
                dve.wait_ge(sd_done, n + 1)
                done(dve.reciprocal(sd[0:p, 1:2], sd[0:p, 0:1]))
                then()
                for half in range(2):
                    parts = (2 * half, 2 * half + 1)
                    for q in parts:
                        c = slice(q * 512, (q + 1) * 512)
                        done(dve.scalar_tensor_tensor(rows_[:, c], quarter(rows_ if src is None else src, q),
                                                      mv[0:p, 0:1], gain[0:p, 0, c], ALU.subtract, ALU.mult))
                    for i, q in enumerate(parts):
                        c = slice(q * 512, (q + 1) * 512)
                        dve.wait_ge(vec_step, count[0] - 1 + i)
                        dve.scalar_tensor_tensor(rows_[:, c], rows_[:, c], sd[0:p, 1:2], gain[0:p, 1, c],
                                                 ALU.mult, ALU.add).then_inc(ln_done, 1)

            def turned_low(i, q, a, b):
                dve.wait_ge(turned_hi, i + 1)
                dve.tensor_tensor(h_split[:, 1, 4 * q:4 * q + 4, a:b], bank(i).rearrange("p (a b) -> p a b", a=4),
                                  f32(h_split[:, 0, 4 * q:4 * q + 4, a:b]), ALU.subtract).then_inc(turned_lo, 1)

            dve.wait_ge(x_loaded[0], 16)
            ln_stats(rows[:, 0, :])
            dve.wait_ge(meta_loaded, 16)
            ln_stats(meta_t, META, stats=hstats[0])
            layer_norm(LN_X[0], rows[:, 0, :], gain_load=32)
            dve.wait_ge(x_loaded[1], 16)
            ln_stats(rows[:, 1, :], stats=hstats[1])
            aggregate(mv, hstats[0], META)
            aggregate(hmv[1], hstats[1])
            for q in range(2):
                turned_low(turn_x(0, q), q, META, META + P)
            normalise(LN_META, meta_t, META)
            for q in range(2, 4):
                turned_low(turn_x(0, q), q, META, META + P)
            normalise(LN_X[1], rows[:, 1, :], mv=hmv[1], sd=hsd[1])
            dve.wait_ge(turned_hi, TURN_META + 1)
            dve.tensor_tensor(h_split[:, 1, :, 0:META], bank(TURN_META)[:, 0:KT * META].rearrange(
                "p (a b) -> p a b", a=KT), f32(h_split[:, 0, :, 0:META]), ALU.subtract).then_inc(turned_lo, 1)
            for q in range(4):
                turned_low(turn_x(1, q), q, META + P, L)

            xb, xa, u_, s_, dtv, ncs, wst, ecl, rel, q_, p_ = hsm[0:11]
            dve.wait_ge(param_loaded, 16 * 14)
            dve.wait_ge(const_ready, 7)
            slab_done(dve, 0)
            done(dve.tensor_scalar(xb, ps[0:HEADS, 0, 0:L], head[:, 0:1], None, ALU.add))
            then()
            dve.scalar_tensor_tensor(xa, xb, -1.0, xb, ALU.mult, ALU.max).then_inc(x1_ready, 1)
            dve.wait_ge(ex_ready, 1)
            done(dve.tensor_scalar(s_, u_, 2.0, None, ALU.add))
            then()
            done(dve.reciprocal(q_, s_))
            then()
            done(dve.tensor_tensor(s_, u_, q_, ALU.mult))
            then()
            done(dve.tensor_tensor(q_, s_, s_, ALU.mult))
            then()
            done(dve.tensor_scalar(p_, q_, 1.0 / 15, None, ALU.mult))
            then()
            for n in (13, 11, 9, 7, 5, 3):
                done(dve.scalar_tensor_tensor(p_, p_, 1.0 / n, q_, ALU.add, ALU.mult))
                then()
            done(dve.scalar_tensor_tensor(p_, p_, 1.0, s_, ALU.add, ALU.mult))
            done(dve.tensor_scalar(xb, xb, 0.0, None, ALU.max))
            then()
            done(dve.scalar_tensor_tensor(dtv, p_, 2.0, xb, ALU.mult, ALU.add))
            then()
            dve.wait_ge(alog_ready, 1)
            done(dve.tensor_scalar(q_, dtv, head[:, 1:2], -1.0, ALU.mult, ALU.mult))
            then()
            for a, b in CHUNKS:
                done(dve.tensor_tensor_scan(cs[:, a:b], ones[0:HEADS, 0:b - a], q_[:, a:b], 0.0, ALU.mult, ALU.add))
            then()
            done(dve.tensor_scalar(ncs, cs[:, :], -1.0, None, ALU.mult))
            for a, b in CHUNKS[0:1]:
                done(dve.tensor_scalar(rel[:, a:b], cs[:, a:b], cs[:, b - 1:b], None, ALU.subtract))
            a, b = CHUNKS[2]
            done(dve.tensor_scalar(rel[:, a:b], cs[:, a:b], cs[:, b - 1:b], None, ALU.subtract))
            a, b = CHUNKS[1]
            dve.tensor_scalar(rel[:, a:b], cs[:, a:b], cs[:, b - 1:b], None, ALU.subtract).then_inc(rel_ready, 1)
            dve.wait_ge(w_ready, 1)
            done(dve.tensor_tensor(wst, wst, dtv, ALU.mult))
            dve.wait_ge(ecl_ready, 1)
            dve.tensor_scalar(ecl[:, 0:P], ones[0:HEADS, :], head[:, 2:3], None, ALU.mult).then_inc(tabs_ready, 1)

            PER = 4 * (KC - 1) + 1 + 2 + 2 + 3 + 2 * (KF - 1) + 1
            start = count[0]
            turn_ = [0]

            def hold(back=0):
                dve.wait_ge(vec_step, turn_[0] + (count[0] - back))

            def norm_glu(g):
                dve.wait_ge(nsd_ready, g + 1)
                done(dve.reciprocal(rinv[:, 1, :], rinv[:, 0, :]))
                hold()
                for u in range(2):
                    last = dve.scalar_tensor_tensor(v[:, u, :], v[:, u, :], pcol[:, ds(g * 2 + (32 + u), 1)],
                                                    rinv[:, 1, :], ALU.mult, ALU.mult)
                done(last)
                hold()
                done(dve.tensor_copy(ym_split[:, 0, ds(g * 2, 2), :], v[:, :, :]))
                hold()
                dve.tensor_tensor(ym_split[:, 1, ds(g * 2, 2), :], v[:, :, :], f32(ym_split[:, 0, ds(g * 2, 2), :]),
                                  ALU.subtract).then_inc(ynorm_ready, 1)
                dve.wait_ge(proj_copied, g * 5 + 10)
                dve.tensor_tensor(gsig[:, :, :], gsig[:, :, :], vraw[:, :, :], ALU.mult).then_inc(glu_ready, 1)

            def taps(g, first, end):
                for back in range(first, end):
                    k = KF - 1 - back
                    t0 = max(META, back)
                    for u in range(2):
                        w = cfw[:, ds(g * 2 + (k * KT + u), 1)]
                        if back == 0:
                            if u == 0:
                                dve.wait_ge(glu_ready, g + 2)
                            ct = cT[:, ds(g * 2 + u, 1), :].rearrange("p a b -> p (a b)")
                            ins = dve.tensor_scalar(ct, gsig[:, u, META:L], w, pcol[:, ds(g * 2 + (48 + u), 1)],
                                                    ALU.mult, ALU.add)
                        else:
                            hold(1)
                            o = cT[:, ds(g * 2 + u, 1), t0 - META:SEQ].rearrange("p a b -> p (a b)")
                            ins = dve.scalar_tensor_tensor(o, gsig[:, u, t0 - back:L - back], w, o, ALU.mult, ALU.add)
                        if k or u == 0:
                            done(ins)
                        else:
                            ins.then_inc(cf_ready, 1)

            def short_conv(g, half):
                tiles = (g * 2, g * 2 + 1, g + 16, g + 24)
                for k in range(KC - 1, -1, -1):
                    for i in (2 * half, 2 * half + 1):
                        w = convw[:, k, ds(tiles[i], 1)]
                        m = KC - 1 - k
                        if k == KC - 1:
                            if i % 2 == 0:
                                dve.wait_ge(proj_copied, g * 5 + (6 + half))
                            done(dve.tensor_scalar(acc[:, i, :], xin[:, i, :], w, None, ALU.mult))
                        else:
                            hold(1 if k else 1 - i % 2)
                            ins = dve.scalar_tensor_tensor(acc[:, i, m:L], xin[:, i, 0:L - m], w, acc[:, i, m:L],
                                                           ALU.mult, ALU.add)
                            if k:
                                done(ins)
                            else:
                                ins.then_inc(conv_ready, 1)

            def group(g, first=False):
                def last_taps(a, b):
                    if not first:
                        taps(g - 1, a, b)

                if not first:
                    norm_glu(g - 1)
                for c in range(2):
                    a, b = CHUNKS[1 + c]
                    last = dve.tensor_tensor(rmask[:, c, :, :],
                                             ident[0:HEADS, ds(g * HPG, HPG)].unsqueeze(2).to_broadcast([HEADS, HPG, P]),
                                             cs[:, a:b].unsqueeze(1).to_broadcast([HEADS, HPG, P]), ALU.mult)
                last.then_inc(r_ready, 1)
                last_taps(0, 5)
                short_conv(g, 0)
                last_taps(5, 13)
                short_conv(g, 1)
                dve.wait_ge(csb_done, g + 1)
                for c in range(2):
                    for hh in range(HPG):
                        last = dve.tensor_scalar(seg[:, c, hh, :], ps[:, 4 + c, hh * P:(hh + 1) * P],
                                                 tm[:, 2 + c, ds(g * HPG + hh, 1)], 0.0, ALU.add, ALU.min)
                last.then_inc(seg_ready, 1)
                last_taps(13, 19)
                dve.wait_ge(xpose_done, g + 1)

                def per_head(table, p=P):
                    return tm[0:p, table, ds(g * HPG, HPG)].unsqueeze(2).to_broadcast([p, HPG, HD])

                def heads(ap):
                    return ap.rearrange("p (h d) -> p h d", d=HD)

                for c in range(2):
                    dve.tensor_tensor(heads(xdt[:, c, :]), heads(T2[:, c * 2 * P:(c + 1) * 2 * P]), per_head(c), ALU.mult)
                dve.tensor_tensor(heads(xw[:, 0, :]), heads(T2[:, 0:2 * P]), per_head(4), ALU.mult)
                dve.tensor_tensor(heads(xw[0:META, 1, :]), heads(T3[0:META, 2 * P:4 * P]), per_head(5, META),
                                  ALU.mult).then_inc(xtm_ready, 1)
                last_taps(19, 24)
                dve.wait_ge(score_done, g + 1)
                done(dve.tensor_tensor(scm[:, :, :], T0[:, 0:2 * P].rearrange("p (c i) -> p c i", c=2),
                                       causal[:, :].unsqueeze(1).to_broadcast([P, 2, P]), ALU.mult))
                hold()
                dve.wait_ge(exp_ready, g + 1)
                for c in range(2):
                    dve.tensor_tensor(seg[:, c, :, :], seg[:, c, :, :],
                                      scm[:, c, :].unsqueeze(1).to_broadcast([P, HPG, P]), ALU.mult)
                dve.wait_ge(ecs_ready, g + 1)
                for c in range(2):
                    a, b = CHUNKS[1 + c]
                    last = dve.tensor_tensor(ecs[:, c, :, :], ecs[:, c, :, :],
                                             xg[:, 3, a:b].unsqueeze(1).to_broadcast([P, HPG, P]), ALU.mult)
                last.then_inc(mt_ready, 1)
                dve.wait_ge(state_done, g + 1)
                done(dve.tensor_copy(state[:, 0, :], T3[:, 0:HPG * HD]))
                hold()
                done(dve.tensor_tensor(heads(state[:, 1, :]), heads(state[:, 0, :]),
                                       edec[:, ds(g * HPG, HPG)].unsqueeze(2).to_broadcast([P, HPG, HD]), ALU.mult))
                hold()
                dve.tensor_tensor(state[:, 1, :], state[:, 1, :], T3[:, HPG * HD:2 * HPG * HD], ALU.add).then_inc(
                    s_ready, 1)
                dve.wait_ge(y_done, g + 1)
                for u in range(2):
                    done(dve.scalar_tensor_tensor(v[:, u, :], xg[:, u, META:L], dcol[:, ds(g * 2 + u, 1)],
                                                  T1[:, u * SEQ:(u + 1) * SEQ], ALU.mult, ALU.add))
                hold()
                dve.wait_ge(proj_copied, g * 5 + 9)
                dve.tensor_tensor(v[:, :, :], v[:, :, :], zs[:, :, :], ALU.mult).then_inc(v_ready, 1)
                last_taps(24, KF)

            group(0, True)
            start = count[0]
            with dve.Fori(1, GROUPS) as g:
                count[0] = start
                turn_[0] = g * PER - PER
                group(g)
                assert PER == count[0] - start, (PER, count[0] - start)
            count[0] = start + (GROUPS - 1) * PER
            turn_[0] = 0
            norm_glu(GROUPS - 1)
            taps(GROUPS - 1, 0, KF)

            branch = ps[:, 2:4, 0:SEQ]

            def mix_first(i):
                dve.wait_ge(sg_ready, i + 2)
                slab_done(dve, i * 2 + (S_SSD + 1))
                dve.tensor_tensor(mix1[:, ds(i * 2, 2), :], v[:, :, :], branch, ALU.mult).then_inc(mix_ready, 1)

            with dve.Fori(0, 2) as i:
                mix_first(i)
            dve.wait_ge(mean_done, 1)
            dve.tensor_tensor(cT, cT, T0[:, 0:SEQ].unsqueeze(1).to_broadcast([P, KT, SEQ]),
                              ALU.subtract).then_inc(cen_ready, 1)
            mix_first(2)
            dve.wait_ge(csd_ready, 1)
            dve.wait_ge(csq_ready, 1)
            done(dve.reciprocal(rinv[:, 1, :], rinv[:, 0, :]))
            then()
            dve.tensor_tensor(cT, cT, rinv[:, 1, :].unsqueeze(1).to_broadcast([P, KT, SEQ]),
                              ALU.mult).then_inc(cn_ready, 1)
            mix_first(3)
            start = count[0]
            with dve.Fori(4, NS) as i:
                mix_first(i)
                dve.wait_ge(silu_ready, i * 4 - 12)
                tiles = ds(i * 4 - 16, 4)
                done(dve.tensor_copy(c_split[:, 0, tiles, :], cT[:, tiles, :]))
                dve.wait_ge(vec_step, i + (start - 3))
                dve.tensor_tensor(c_split[:, 1, tiles, :], cT[:, tiles, :], f32(c_split[:, 0, tiles, :]),
                                  ALU.subtract).then_inc(c_ready, 1)
            count[0] = start + 4
            start = count[0]
            with dve.Fori(0, NS) as i:
                dve.wait_ge(sg_ready, i + (NS + 2))
                slab_done(dve, i * 2 + (S_CF + 1))
                dve.tensor_tensor(v2[:, :, :], v[:, :, :], branch, ALU.mult).then_inc(mix_ready, 1)
                dve.wait_ge(mix_ready, i + (NS + 2))
                done(dve.tensor_tensor(v2[:, :, :], v2[:, :, :], mix1[:, ds(i * 2, 2), :], ALU.add))
                dve.wait_ge(vec_step, i * 2 + (start + 1))
                done(dve.tensor_copy(ym_split[:, 0, ds(i * 2, 2), :], v2[:, :, :]))
                dve.wait_ge(vec_step, i * 2 + (start + 2))
                dve.tensor_tensor(ym_split[:, 1, ds(i * 2, 2), :], v2[:, :, :], f32(ym_split[:, 0, ds(i * 2, 2), :]),
                                  ALU.subtract).then_inc(m_ready, 1)
                dve.wait_ge(m_ready, i + 1)
            count[0] = start + 2 * NS

            def chunk_stats(n):
                dve.wait_ge(res_copied, 2 * n + 4)
                for t in range(NT):
                    ln_stats(rows[:, t, :], stats=hstats[t], quarters=[n])

            for n in range(NS):
                slab_done(dve, n + S_WO)
                dve.wait_ge(res_turned, n + 1)
                r, bank0 = res[n % 2], 2 * (n % 2)
                tiles = slice(2 * n, 2 * n + 2)
                done(dve.scalar_tensor_tensor(r[:, :, :], f32(h_split[:, 0, tiles, META:L]), ALPHA,
                                              ps[:, bank0:bank0 + 2, 0:SEQ], ALU.mult, ALU.add))
                then()
                dve.scalar_tensor_tensor(r[:, :, :], f32(h_split[:, 1, tiles, META:L]), ALPHA,
                                         r[:, :, :], ALU.mult, ALU.add).then_inc(res_ready, 1)
                if n % 2 and n > 1:
                    chunk_stats(n // 2 - 1)
            chunk_stats(NS // 2 - 1)
            dve.wait_ge(gain_loaded, 64)
            then()
            for t in range(NT):
                dve.bn_aggr(hmv[t][:, :], hstats[t][:, :, :].rearrange("p a b -> p (a b)")).then_inc(var_ready, 1)
            for t in range(NT):
                dve.wait_ge(var_ready, LN_H1 + t + 1)
                dve.wait_ge(sd_done, LN_H1 + t + 1)
                done(dve.reciprocal(hsd[t][:, 1:2], hsd[t][:, 0:1]))
            then()

            def low_quarter(q):
                for t in range(NT):
                    turned_low(turn_h1(t, q), q, t * P, (t + 1) * P)

            for q in range(4):
                c = slice(q * 512, (q + 1) * 512)
                for t in range(NT):
                    done(dve.scalar_tensor_tensor(rows[:, t, c], rows[:, t, c], hmv[t][:, 0:1], gain[:, 0, c],
                                                  ALU.subtract, ALU.mult))
                for t in range(NT):
                    dve.wait_ge(vec_step, count[0] - 1 + t)
                    dve.scalar_tensor_tensor(rows[:, t, c], rows[:, t, c], hsd[t][:, 1:2], gain[:, 1, c],
                                             ALU.mult, ALU.add).then_inc(ln_done, 1)
                if q:
                    low_quarter(q - 1)
            low_quarter(3)

            def find_experts(h, j, tiles=range(NT)):
                tt = slice(tiles[0], tiles[-1] + 1)
                qq = range(2 * tiles[0], 2 * tiles[-1] + 2)
                n = len(tiles)
                if n == NT:
                    base = h * TOPK_STEPS + 2 * (TOPK_STEPS + 1)
                else:
                    base = h * (2 * TOPK_STEPS + 1) + tiles[0] * (TOPK_STEPS + 1)
                local = [0]

                def done(ins):
                    ins.then_inc(topk_step, 1)
                    local[0] += 1

                def hold():
                    dve.wait_ge(topk_step, base + local[0])
                    settle(dve)

                sc = scs[j]
                dve.wait_ge(sc_copied, h + 3)
                settle(dve)
                for q in qq:
                    last = dve.max(topv[:, q, 0:8], sc[:, q, :])
                done(last)
                hold()
                for q in qq:
                    dve.max_index(topi[:, q, 0:8], topv[:, q, 0:8], sc[:, q, :])
                    last = dve.match_replace(left[:, q, :], topv[:, q, 0:8], sc[:, q, :], LOW)
                done(last)
                hold()
                for q in qq:
                    last = dve.max(topv[:, q, 8:16], left[:, q, :])
                done(last)
                hold()
                for q in qq:
                    last = dve.max_index(topi[:, q, 8:16], topv[:, q, 8:16], left[:, q, :])
                done(last)
                for t in tiles:
                    last = dve.tensor_tensor(cand[:, t, :].rearrange("p (a b) -> p a b", a=TOPK),
                                             topv[:, 2 * t, :].unsqueeze(2).to_broadcast([P, TOPK, TOPK]),
                                             topv[:, 2 * t + 1, :].unsqueeze(1).to_broadcast([P, TOPK, TOPK]),
                                             ALU.add)
                done(last)
                hold()
                dve.tensor_copy(topif[:, 2 * tt.start:2 * tt.stop, :], topi[:, 2 * tt.start:2 * tt.stop, :])
                for t in tiles:
                    last = dve.max(bestv[:, t, 0:8], cand[:, t, :])
                done(last)
                hold()
                for t in tiles:
                    dve.max_index(bestj[:, t, 0:8], bestv[:, t, 0:8], cand[:, t, :])
                    last = dve.match_replace(cand2[:, t, :], bestv[:, t, 0:8], cand[:, t, :], LOW)
                done(last)
                hold()
                for t in tiles:
                    last = dve.max(bestv[:, t, 8:16], cand2[:, t, :])
                done(last)
                hold()
                for t in tiles:
                    last = dve.max_index(bestj[:, t, 8:16], bestv[:, t, 8:16], cand2[:, t, :])
                done(last)
                hold()
                for t in tiles:
                    last = dve.tensor_scalar(gates[:, ds(h + t * PH, 1), :].rearrange("p a b -> p (a b)"),
                                             bestv[:, t, :], bestv[:, t, 0:1], None, ALU.subtract)
                if tiles[-1] == NT - 1:
                    last.then_inc(gexp_in, 1)
                dve.tensor_scalar(part[:, 0, tt, :], bestj[:, tt, :], 4, None, ALU.logical_shift_right)
                done(dve.tensor_scalar(part[:, 1, tt, :], bestj[:, tt, :], 15, None, ALU.bitwise_and))
                hold()
                done(dve.tensor_copy(partf[:, :, tt, :], part[:, :, tt, :]))
                hold()
                for s in range(2):
                    keyno = topif.rearrange("p (t s) i -> p s t i", s=2)[:, s, :, :]
                    done(dve.tensor_tensor(hot[:, tt, :, :], partf[:, s, tt, :].unsqueeze(3).to_broadcast([P, n, TOPK, TOPK]),
                                           iota16[:, :].unsqueeze(1).unsqueeze(1).to_broadcast([P, n, TOPK, TOPK]),
                                           ALU.is_equal))
                    hold()
                    for t in tiles:
                        last = dve.tensor_tensor(hot[:, t, :, :], hot[:, t, :, :],
                                                 keyno[:, t, :].unsqueeze(1).to_broadcast([P, TOPK, TOPK]), ALU.mult)
                    done(last)
                    hold()
                    done(dve.tensor_reduce(pick[:, s, tt, :], hot[:, tt, :, :], AX.X, ALU.add))
                    hold()
                for t in tiles:
                    last = dve.scalar_tensor_tensor(
                        idx[:, ds(h + t * PH, 1), :].rearrange("p a b -> p (a b)"),
                        pick[:, 0, t, :], float(NK), pick[:, 1, t, :], ALU.mult, ALU.add)
                if tiles[-1] == NT - 1:
                    last.then_inc(topk_done, 1)
                    assert local[0] == TOPK_STEPS, local[0]
                else:
                    done(last)
                    dve.wait_ge(topk_step, base + local[0])

            dve.memset(idx[:, NT * PH:, :], 0)
            find_experts(0, 0, [0])
            dve.tensor_copy(ixu[:, 0, :], idx[:, 0, :]).then_inc(ix_staged, 1)
            find_experts(0, 0, [1])

            def weights(s, par):
                dve.wait_ge(gelu_ready, s)
                e = gates[:, ds(s - 1, 1), :].rearrange("p a b -> p (a b)")
                dve.tensor_reduce(gsum[:, par:par + 1], e, AX.X, ALU.add).then_inc(weight_step, 1)
                dve.wait_ge(weight_step, s * 2 - 1)
                dve.reciprocal(grec[:, par:par + 1], gsum[:, par:par + 1]).then_inc(weight_step, 1)
                dve.wait_ge(weight_step, s * 2)
                if not (isinstance(s, int) and s < 3):
                    dve.wait_ge(diag_ready, s * TOPK - 2 * TOPK)
                dve.scalar_tensor_tensor(wgt[:, 1 - par, :], gel[:, 1 - par, :], grec[:, par:par + 1], e,
                                         ALU.mult, ALU.mult).then_inc(wgt_ready, 1)

            def finish(t):
                dve.wait_ge(v_used, (t + 1) * PH * TOPK)
                sums = ps[:, 4 * (1 - t):4 * (1 - t) + 4, :]
                ln_stats(sums)
                layer_norm(LN_OUT + t, rows[:, t, :], gain=gain2, src=sums, gain_load=96)

            def step(s, par, tile_u, tile_v, scores, finds):
                for k in range(TOPK):
                    if k == 1 and tile_v is not None:
                        weights(s, par)
                    if k == 4 and tile_v is None:
                        find_experts(1, 1, [0])
                    if k == 2 and isinstance(s, int) and s == 1:
                        find_experts(1, 1, [1])
                    if k == 6 and finds and tile_v is not None:
                        find_experts(s + 1, 1 - par)
                    if k == 5 and isinstance(s, int) and s == PH + 1:
                        finish(0)
                    if k == 9 and tile_u is not None:
                        if finds and tile_v is not None:
                            dve.wait_ge(topk_done, s + 4)
                        if not (isinstance(s, int) and s < 2):
                            dve.wait_ge(v_used, s * TOPK - TOPK)
                        settle(dve)
                        dve.tensor_copy(ixu[:, 1 - par, :], idx[:, ds(s + 1, 1), :].rearrange("p a b -> p (a b)"))
                        dve.tensor_copy(ixv[:, par, :], idx[:, ds(s, 1), :].rearrange("p a b -> p (a b)")).then_inc(
                            ix_staged, 1)
                    if tile_u is not None:
                        b = k % UB
                        dve.wait_ge(u_loaded[b], s * (TOPK // UB * 16) + (k // UB + 1) * 16)
                        dve.tensor_tensor_reduce(ubuf[b], ubuf[b], rows[:, tile_u, :], 1.0, 0.0,
                                                 ALU.mult, ALU.add, dots[:, par, k:k + 1]).then_inc(u_used, 1)

            run_steps(dve, step)
            finish(1)


_INS = ["x", "meta", "ln0_g", "ln0_b", "w_in", "ssd_conv_w", "ssd_conv_b", "ssd_dt_bias", "ssd_a_log", "ssd_d",
        "ssd_norm_w", "ssd_out", "cf_dw_w", "cf_dw_b", "cf_ln_g", "cf_ln_b", "cf_out", "w_o", "ln1_g", "ln1_b",
        "peer_wq", "peer_keys", "peer_u", "peer_v", "ln2_g", "ln2_b"]


def kernel(**inputs):
    import numpy as _np
    import concourse.bacc as _bacc
    from concourse import mybir as _mybir
    from concourse.bass_utils import run_bass_kernel_spmd as _run

    nc = _bacc.Bacc("TRN2", target_bir_lowering=False, num_devices=1)
    arrays, A = {}, {}
    for name in _INS:
        a = _np.ascontiguousarray(inputs[name])
        arrays[f"in_{name}"] = a
        A[name] = nc.dram_tensor(f"in_{name}", a.shape, _mybir.dt.from_np(a.dtype), kind="ExternalInput").ap()
    out = nc.dram_tensor("out", (1, SEQ, D), _mybir.dt.float32, kind="ExternalOutput").ap()
    build(nc, A, out)
    return _run(nc, [arrays], core_ids=[0]).results[0]["out"]
```
